# Optimizing a Trainium2 kernel written in Bass

```python
import jax, jax.numpy as jnp
from jax import lax
import numpy as np

D_MODEL = 1024
BATCH = 1
SEQ = 512
DEPTH = 2

N_MIXERS = 2
HEAD_DIM = 64
ROPE_THETA = 10000.0
NORM_EPS = 1e-6
Q_BLOCK = 128
NSA_Q_HEADS = D_MODEL // HEAD_DIM
NSA_KV_HEADS = 4
NSA_GROUP = NSA_Q_HEADS // NSA_KV_HEADS
CMP_BLOCK = 32
CMP_STRIDE = 16
CMP_HIDDEN = 4 * HEAD_DIM
SEL_BLOCK = 64
SEL_TOPK = 8
SEL_Q_CHUNK = 32
NSA_WINDOW = 512
NSA_IN = NSA_Q_HEADS * HEAD_DIM + 6 * NSA_KV_HEADS * HEAD_DIM + 3 * NSA_Q_HEADS
SWA_Q_HEADS = D_MODEL // HEAD_DIM
SWA_KV_HEADS = 2
SWA_GROUP = SWA_Q_HEADS // SWA_KV_HEADS
SWA_WINDOW = 128
SWA_IN = SWA_Q_HEADS * HEAD_DIM + 2 * SWA_KV_HEADS * HEAD_DIM
MLP_HIDDEN = 4 * D_MODEL


def rms_norm(x, g):
    xf = x.astype(jnp.float32)
    y = xf * lax.rsqrt(jnp.mean(xf * xf, axis=-1, keepdims=True) + NORM_EPS)
    return (y * g.astype(jnp.float32)).astype(x.dtype)

def modulate(h, shift, scale):
    return h * (1 + scale[:, None, :]) + shift[:, None, :]

def rope_tables(positions):
    inv = 1.0 / (ROPE_THETA ** (jnp.arange(0, HEAD_DIM, 2, dtype=jnp.float32) / HEAD_DIM))
    ang = positions.astype(jnp.float32)[..., None] * inv
    return jnp.cos(ang)[:, :, None, :], jnp.sin(ang)[:, :, None, :]

def apply_rope(x, cos, sin):
    x1, x2 = jnp.split(x.astype(jnp.float32), 2, axis=-1)
    return jnp.concatenate([x1 * cos - x2 * sin, x2 * cos + x1 * sin], axis=-1).astype(x.dtype)

def banded_attention(q, k, v, window, sinks):
    B, S, Hkv, G, dh = q.shape
    span = window + Q_BLOCK
    pad = ((0, 0), (window, 0), (0, 0), (0, 0))
    kp = jnp.pad(k, pad)
    vp = jnp.pad(v, pad)
    scale = dh ** -0.5

    def block(bi):
        s0 = bi * Q_BLOCK
        qb = lax.dynamic_slice_in_dim(q, s0, Q_BLOCK, axis=1)
        kb = lax.dynamic_slice_in_dim(kp, s0, span, axis=1)
        vb = lax.dynamic_slice_in_dim(vp, s0, span, axis=1)
        s = jnp.einsum('bqhgd,bkhd->bhgqk', qb, kb).astype(jnp.float32) * scale
        t = s0 + jnp.arange(Q_BLOCK)
        j = s0 - window + jnp.arange(span)
        dist = t[:, None] - j[None, :]
        mask = (dist >= 0) & (dist < window) & (j[None, :] >= 0)
        s = jnp.where(mask, s, -jnp.inf)
        if sinks is None:
            p = jax.nn.softmax(s, axis=-1)
        else:
            sk = sinks.astype(jnp.float32)[None, :, :, None, None]
            m = jnp.maximum(jnp.max(s, axis=-1, keepdims=True), sk)
            e = jnp.exp(s - m)
            p = e / (jnp.sum(e, axis=-1, keepdims=True) + jnp.exp(sk - m))
        return jnp.einsum('bhgqk,bkhd->bqhgd', p.astype(v.dtype), vb)

    out = lax.map(block, jnp.arange(S // Q_BLOCK))
    return jnp.moveaxis(out, 0, 1).reshape(B, S, Hkv, G, dh)

def compress_tokens(x, pe, w1, b1, w2, b2):
    B, S, Hkv, dh = x.shape
    n_cmp = (S - CMP_BLOCK) // CMP_STRIDE + 1
    idx = np.arange(n_cmp)[:, None] * CMP_STRIDE + np.arange(CMP_BLOCK)[None, :]
    xb = x[:, idx] + pe[None, None, :, None, :]
    xb = jnp.moveaxis(xb, 3, 2).reshape(B, n_cmp, Hkv, CMP_BLOCK * dh)
    return jax.nn.gelu(xb @ w1 + b1) @ w2 + b2

def compressed_attention(q, kc, vc):
    B, S, Hkv, G, dh = q.shape
    n_cmp = kc.shape[1]
    s = jnp.einsum('bshgd,bnhd->bhgsn', q, kc).astype(jnp.float32) * dh ** -0.5
    blk_end = jnp.arange(n_cmp) * CMP_STRIDE + CMP_BLOCK - 1
    mask = blk_end[None, :] <= jnp.arange(S)[:, None]
    s = jnp.where(mask, s, -jnp.inf)
    m = jnp.max(s, axis=-1, keepdims=True)
    m = jnp.where(jnp.isfinite(m), m, 0.0)
    e = jnp.where(mask, jnp.exp(s - m), 0.0)
    den = jnp.sum(e, axis=-1, keepdims=True)
    p = e / jnp.where(den > 0, den, 1.0)
    o = jnp.einsum('bhgsn,bnhd->bshgd', p.astype(vc.dtype), vc)
    return o, p

def select_blocks(p_cmp, S):
    n_cmp = p_cmp.shape[-1]
    n_sel = S // SEL_BLOCK
    cs = np.arange(n_cmp)[:, None] * CMP_STRIDE
    ss = np.arange(n_sel)[None, :] * SEL_BLOCK
    overlap = np.clip(np.minimum(cs + CMP_BLOCK, ss + SEL_BLOCK) - np.maximum(cs, ss), 0, None)
    M = jnp.asarray((overlap / CMP_STRIDE).astype(np.float32))
    imp = jnp.einsum('bhgsn,nj->bhsj', p_cmp, M)
    cur = jnp.arange(S) // SEL_BLOCK
    jj = jnp.arange(n_sel)
    causal = jj[None, :] <= cur[:, None]
    forced = (jj[None, :] == 0) | (jj[None, :] == cur[:, None]) | (jj[None, :] == cur[:, None] - 1)
    imp = jnp.where(forced, jnp.inf, jnp.where(causal, imp, -jnp.inf))
    _, idx = lax.top_k(imp, min(SEL_TOPK, n_sel))
    return idx

def selected_block_attention(q, k, v, sel_idx):
    B, S, Hkv, G, dh = q.shape
    n_sel = S // SEL_BLOCK
    kb = k.reshape(B, n_sel, SEL_BLOCK, Hkv, dh).transpose(0, 3, 1, 2, 4)
    vb = v.reshape(B, n_sel, SEL_BLOCK, Hkv, dh).transpose(0, 3, 1, 2, 4)
    bi = jnp.arange(B)[:, None, None, None]
    hi = jnp.arange(Hkv)[None, :, None, None]
    scale = dh ** -0.5

    def chunk(ci):
        s0 = ci * SEL_Q_CHUNK
        qc = lax.dynamic_slice_in_dim(q, s0, SEL_Q_CHUNK, axis=1)
        ic = lax.dynamic_slice_in_dim(sel_idx, s0, SEL_Q_CHUNK, axis=2)
        kg = kb[bi, hi, ic]
        vg = vb[bi, hi, ic]
        s = jnp.einsum('bqhgd,bhqnld->bhgqnl', qc, kg).astype(jnp.float32) * scale
        t = s0 + jnp.arange(SEL_Q_CHUNK)
        pos = ic[..., None] * SEL_BLOCK + jnp.arange(SEL_BLOCK)
        mask = (pos <= t[None, None, :, None, None])[:, :, None]
        s = jnp.where(mask, s, -jnp.inf)
        n = ic.shape[-1]
        p = jax.nn.softmax(s.reshape(B, Hkv, G, SEL_Q_CHUNK, n * SEL_BLOCK), axis=-1).reshape(s.shape)
        return jnp.einsum('bhgqnl,bhqnld->bqhgd', p.astype(v.dtype), vg)

    out = lax.map(chunk, jnp.arange(S // SEL_Q_CHUNK))
    return jnp.moveaxis(out, 0, 1).reshape(B, S, Hkv, G, dh)

def nsa_mixer(h, w_in, w_out, cmp_pe, phi_w1, phi_b1, phi_w2, phi_b2, cos, sin):
    B, S, _ = h.shape
    qd = NSA_Q_HEADS * HEAD_DIM
    kd = NSA_KV_HEADS * HEAD_DIM
    proj = h @ w_in
    splits = [qd + i * kd for i in range(7)]
    q, kc, vc, ks, vs, kw, vw, g = jnp.split(proj, splits, axis=-1)
    q = apply_rope(q.reshape(B, S, NSA_Q_HEADS, HEAD_DIM), cos, sin)
    q = q.reshape(B, S, NSA_KV_HEADS, NSA_GROUP, HEAD_DIM)
    kv_shape = (B, S, NSA_KV_HEADS, HEAD_DIM)
    kc = apply_rope(kc.reshape(kv_shape), cos, sin)
    ks = apply_rope(ks.reshape(kv_shape), cos, sin)
    kw = apply_rope(kw.reshape(kv_shape), cos, sin)
    vc, vs, vw = vc.reshape(kv_shape), vs.reshape(kv_shape), vw.reshape(kv_shape)
    kcc = compress_tokens(kc, cmp_pe[0], phi_w1[0], phi_b1[0], phi_w2[0], phi_b2[0])
    vcc = compress_tokens(vc, cmp_pe[1], phi_w1[1], phi_b1[1], phi_w2[1], phi_b2[1])
    o_cmp, p_cmp = compressed_attention(q, kcc, vcc)
    sel_idx = select_blocks(p_cmp, S)
    o_sel = selected_block_attention(q, ks, vs, sel_idx)
    o_win = banded_attention(q, kw, vw, NSA_WINDOW, None)
    g = jax.nn.sigmoid(g.astype(jnp.float32)).astype(h.dtype)
    g = g.reshape(B, S, NSA_KV_HEADS, NSA_GROUP, 3)
    o = g[..., 0:1] * o_cmp + g[..., 1:2] * o_sel + g[..., 2:3] * o_win
    return o.reshape(B, S, qd) @ w_out

def swa_sink_mixer(h, w_in, w_out, sinks, cos, sin):
    B, S, _ = h.shape
    qd = SWA_Q_HEADS * HEAD_DIM
    kd = SWA_KV_HEADS * HEAD_DIM
    q, k, v = jnp.split(h @ w_in, [qd, qd + kd], axis=-1)
    q = apply_rope(q.reshape(B, S, SWA_Q_HEADS, HEAD_DIM), cos, sin)
    q = q.reshape(B, S, SWA_KV_HEADS, SWA_GROUP, HEAD_DIM)
    k = apply_rope(k.reshape(B, S, SWA_KV_HEADS, HEAD_DIM), cos, sin)
    v = v.reshape(B, S, SWA_KV_HEADS, HEAD_DIM)
    o = banded_attention(q, k, v, SWA_WINDOW, sinks.reshape(SWA_KV_HEADS, SWA_GROUP))
    return o.reshape(B, S, qd) @ w_out

def squared_relu_mlp(h, w_up, w_down):
    a = jax.nn.relu(h @ w_up)
    return (a * a) @ w_down

def first_inputs(seed: int = 0) -> dict:
    key = jax.random.key(seed)
    ks = jax.random.split(key, 20)
    n_a = (DEPTH + N_MIXERS - 1) // N_MIXERS
    n_b = DEPTH // N_MIXERS
    nrm = jax.random.normal
    f32 = jnp.float32
    x = nrm(ks[0], (BATCH, SEQ, D_MODEL), f32)
    c = nrm(ks[1], (BATCH, D_MODEL), f32)
    offset = jax.random.randint(ks[2], (BATCH, 1), 0, 4096, dtype=jnp.int32)
    positions = (offset + jnp.arange(SEQ, dtype=jnp.int32)[None, :]).astype(jnp.int32)
    ada_w = nrm(ks[3], (DEPTH, D_MODEL, 6 * D_MODEL), f32) * (0.5 * D_MODEL ** -0.5)
    ada_b = nrm(ks[4], (DEPTH, 6 * D_MODEL), f32) * 0.01
    norm_g = 1.0 + 0.02 * nrm(ks[5], (DEPTH, 4, D_MODEL), f32)
    nsa_w_in = nrm(ks[6], (n_a, D_MODEL, NSA_IN), f32) * D_MODEL ** -0.5
    nsa_w_out = nrm(ks[7], (n_a, NSA_Q_HEADS * HEAD_DIM, D_MODEL), f32) * (NSA_Q_HEADS * HEAD_DIM) ** -0.5
    nsa_cmp_pe = 0.1 * nrm(ks[8], (n_a, 2, CMP_BLOCK, HEAD_DIM), f32)
    nsa_phi_w1 = nrm(ks[9], (n_a, 2, CMP_BLOCK * HEAD_DIM, CMP_HIDDEN), f32) * (CMP_BLOCK * HEAD_DIM) ** -0.5
    nsa_phi_b1 = 0.01 * nrm(ks[10], (n_a, 2, CMP_HIDDEN), f32)
    nsa_phi_w2 = nrm(ks[11], (n_a, 2, CMP_HIDDEN, HEAD_DIM), f32) * CMP_HIDDEN ** -0.5
    nsa_phi_b2 = 0.01 * nrm(ks[12], (n_a, 2, HEAD_DIM), f32)
    swa_w_in = nrm(ks[13], (n_b, D_MODEL, SWA_IN), f32) * D_MODEL ** -0.5
    swa_w_out = nrm(ks[14], (n_b, SWA_Q_HEADS * HEAD_DIM, D_MODEL), f32) * (SWA_Q_HEADS * HEAD_DIM) ** -0.5
    swa_sinks = nrm(ks[15], (n_b, SWA_Q_HEADS), f32)
    mlp_w_up = nrm(ks[16], (DEPTH, D_MODEL, MLP_HIDDEN), f32) * D_MODEL ** -0.5
    mlp_w_down = nrm(ks[17], (DEPTH, MLP_HIDDEN, D_MODEL), f32) * MLP_HIDDEN ** -0.5
    return {"x": x, "c": c, "positions": positions, "ada_w": ada_w, "ada_b": ada_b,
            "norm_g": norm_g, "nsa_w_in": nsa_w_in, "nsa_w_out": nsa_w_out,
            "nsa_cmp_pe": nsa_cmp_pe, "nsa_phi_w1": nsa_phi_w1, "nsa_phi_b1": nsa_phi_b1,
            "nsa_phi_w2": nsa_phi_w2, "nsa_phi_b2": nsa_phi_b2, "swa_w_in": swa_w_in,
            "swa_w_out": swa_w_out, "swa_sinks": swa_sinks, "mlp_w_up": mlp_w_up,
            "mlp_w_down": mlp_w_down}

def first_block(x, c, positions, ada_w, ada_b, norm_g, nsa_w_in, nsa_w_out, nsa_cmp_pe,
              nsa_phi_w1, nsa_phi_b1, nsa_phi_w2, nsa_phi_b2, swa_w_in, swa_w_out,
              swa_sinks, mlp_w_up, mlp_w_down):
    cos, sin = rope_tables(positions)
    cond = jax.nn.silu(c)
    for i in range(DEPTH):
        mod = cond @ ada_w[i] + ada_b[i]
        sh1, sc1, g1, sh2, sc2, g2 = jnp.split(mod, 6, axis=-1)
        h = modulate(rms_norm(x, norm_g[i, 0]), sh1, sc1)
        a = i // N_MIXERS
        if i % N_MIXERS == 0:
            y = nsa_mixer(h, nsa_w_in[a], nsa_w_out[a], nsa_cmp_pe[a], nsa_phi_w1[a],
                          nsa_phi_b1[a], nsa_phi_w2[a], nsa_phi_b2[a], cos, sin)
        else:
            y = swa_sink_mixer(h, swa_w_in[a], swa_w_out[a], swa_sinks[a], cos, sin)
        x = x + (1 + g1)[:, None, :] * rms_norm(y, norm_g[i, 1])
        h = modulate(rms_norm(x, norm_g[i, 2]), sh2, sc2)
        y = squared_relu_mlp(h, mlp_w_up[i], mlp_w_down[i])
        x = x + (1 + g2)[:, None, :] * rms_norm(y, norm_g[i, 3])
    return x


DEPTH_2 = 1

N_MEM = 256
MIX_WIDTH = D_MODEL
POOL_WIDTH = MIX_WIDTH // 2
POOL_GROUPS = 4
POOL_GROUP_DIM = POOL_WIDTH // POOL_GROUPS
POOL_WINDOWS = (2, 4, 8, 16)
GLA_VALUE_WIDTH = MIX_WIDTH - POOL_WIDTH
GLA_KEY_WIDTH = GLA_VALUE_WIDTH // 2
GLA_HEADS = 4
GLA_DK = GLA_KEY_WIDTH // GLA_HEADS
GLA_DV = GLA_VALUE_WIDTH // GLA_HEADS
GLA_GATE_RANK = 16
GLA_GATE_NORMALIZER = 16.0
GLA_CHUNK = 64
OFF_Q = POOL_WIDTH
OFF_K = OFF_Q + GLA_KEY_WIDTH
OFF_V = OFF_K + GLA_KEY_WIDTH
OFF_G = OFF_V + GLA_VALUE_WIDTH
OFF_R = OFF_G + GLA_GATE_RANK
IN_PROJ_WIDTH = OFF_R + GLA_VALUE_WIDTH
XATTN_HEADS = 4
XATTN_HEAD_DIM = D_MODEL // XATTN_HEADS
D_FF = 2816
CONV_WIDTH = 3
EPS = 1e-6


def rms_norm_2(x, w):
    x32 = x.astype(jnp.float32)
    y = x32 * lax.rsqrt(jnp.mean(x32 * x32, axis=-1, keepdims=True) + EPS)
    return (y * w.astype(jnp.float32)).astype(x.dtype)

def multiscale_pool(p, pool_w, pool_scale):
    b, s, _ = p.shape
    pg = p.reshape(b, s, POOL_GROUPS, POOL_GROUP_DIM)
    cs = jnp.cumsum(pg.astype(jnp.float32), axis=1)
    t = jnp.arange(s)
    pooled = []
    for g, w in enumerate(POOL_WINDOWS):
        c = cs[:, :, g]
        c_prev = jnp.pad(c, ((0, 0), (w, 0), (0, 0)))[:, :s]
        cnt = jnp.minimum(t + 1, w).astype(jnp.float32)[None, :, None]
        pooled.append((c - c_prev) / cnt)
    pooled = jnp.stack(pooled, axis=2).astype(p.dtype) - pg
    mixed = jnp.einsum('bsgc,gcd->bsgd', pooled, pool_w)
    return mixed.reshape(b, s, POOL_WIDTH) * pool_scale

def gla_chunked(q, k, v, log_g):
    b, h, s, dk = q.shape
    dv = v.shape[-1]
    nc = s // GLA_CHUNK
    f32 = jnp.float32
    q = q.astype(f32).reshape(b, h, nc, GLA_CHUNK, dk) * (dk ** -0.5)
    k = k.astype(f32).reshape(b, h, nc, GLA_CHUNK, dk)
    v = v.astype(f32).reshape(b, h, nc, GLA_CHUNK, dv)
    G = jnp.cumsum(log_g.astype(f32).reshape(b, h, nc, GLA_CHUNK, dk), axis=3)
    G_last = G[:, :, :, -1]
    q_dec = q * jnp.exp(G)
    k_dec = k * jnp.exp(-G)
    causal = jnp.tril(jnp.ones((GLA_CHUNK, GLA_CHUNK), dtype=bool))
    scores = jnp.where(causal, jnp.einsum('bhnid,bhnjd->bhnij', q_dec, k_dec), 0.0)
    o_intra = jnp.einsum('bhnij,bhnje->bhnie', scores, v)
    k_to_end = k * jnp.exp(G_last[:, :, :, None] - G)
    chunk_kv = jnp.einsum('bhnjd,bhnje->bhnde', k_to_end, v)
    decay = jnp.exp(G_last)

    def step(state, inp):
        dec, kv = inp
        return state * dec[..., None] + kv, state

    init = jnp.zeros((b, h, dk, dv), f32)
    _, prev_states = lax.scan(step, init, (jnp.moveaxis(decay, 2, 0), jnp.moveaxis(chunk_kv, 2, 0)))
    prev_states = jnp.moveaxis(prev_states, 0, 2)
    o_inter = jnp.einsum('bhnid,bhnde->bhnie', q_dec, prev_states)
    return (o_intra + o_inter).reshape(b, h, s, dv)

def hybrid_mixer(h, w_in, pool_w, pool_scale, gk_w2, gk_b, gla_norm_w, w_out):
    b, s, _ = h.shape
    proj = h @ w_in
    p = proj[..., :OFF_Q]
    q = proj[..., OFF_Q:OFF_K]
    k = proj[..., OFF_K:OFF_V]
    v = proj[..., OFF_V:OFF_G]
    g_low = proj[..., OFF_G:OFF_R]
    r = proj[..., OFF_R:]
    pool_out = multiscale_pool(p, pool_w, pool_scale)
    log_g = jax.nn.log_sigmoid((g_low @ gk_w2 + gk_b).astype(jnp.float32)) / GLA_GATE_NORMALIZER

    def heads(t, d):
        return t.reshape(b, s, GLA_HEADS, d).transpose(0, 2, 1, 3)

    o = gla_chunked(heads(q, GLA_DK), heads(k, GLA_DK), heads(v, GLA_DV), heads(log_g, GLA_DK))
    o = rms_norm_2(o, gla_norm_w).transpose(0, 2, 1, 3).reshape(b, s, GLA_VALUE_WIDTH).astype(h.dtype)
    gla_out = o * jax.nn.silu(r)
    return jnp.concatenate([pool_out, gla_out], axis=-1) @ w_out

def memory_cross_attention(h, mem_n, wq, wkv, wo):
    b, s, _ = h.shape
    m = mem_n.shape[1]
    q = (h @ wq).reshape(b, s, XATTN_HEADS, XATTN_HEAD_DIM)
    kv = mem_n @ wkv
    k = kv[..., :D_MODEL].reshape(b, m, XATTN_HEADS, XATTN_HEAD_DIM)
    v = kv[..., D_MODEL:].reshape(b, m, XATTN_HEADS, XATTN_HEAD_DIM)
    scores = jnp.einsum('bshd,bmhd->bhsm', q, k).astype(jnp.float32) * (XATTN_HEAD_DIM ** -0.5)
    probs = jax.nn.softmax(scores, axis=-1).astype(v.dtype)
    o = jnp.einsum('bhsm,bmhd->bshd', probs, v).reshape(b, s, D_MODEL)
    return o @ wo

def conv_ffn(h, w_up, conv_w, conv_b, w_down):
    s = h.shape[1]
    u = h @ w_up
    u_pad = jnp.pad(u, ((0, 0), (CONV_WIDTH - 1, 0), (0, 0)))
    u = conv_b + conv_w[0] * u_pad[:, 0:s] + conv_w[1] * u_pad[:, 1:1 + s] + conv_w[2] * u_pad[:, 2:2 + s]
    gate = u[..., :D_FF]
    val = u[..., D_FF:]
    return (jax.nn.silu(gate) * val) @ w_down

def second_inputs(seed: int = 0) -> dict:
    key = jax.random.key(seed)
    ks = jax.random.split(key, 24)
    f32 = jnp.float32
    L = DEPTH_2

    def nrm(k, shape, scale):
        return jax.random.normal(k, shape, f32) * scale

    def gain(k, shape):
        return 1.0 + 0.05 * jax.random.normal(k, shape, f32)

    return {
        'x': jax.random.normal(ks[0], (BATCH, SEQ, D_MODEL), f32),
        'mem': jax.random.normal(ks[1], (BATCH, N_MEM, D_MODEL), f32),
        'norm_mix_w': gain(ks[2], (L, D_MODEL)),
        'w_in': nrm(ks[3], (L, D_MODEL, IN_PROJ_WIDTH), D_MODEL ** -0.5),
        'pool_w': nrm(ks[4], (L, POOL_GROUPS, POOL_GROUP_DIM, POOL_GROUP_DIM), POOL_GROUP_DIM ** -0.5),
        'pool_scale': 0.5 + 0.05 * jax.random.normal(ks[5], (L, POOL_WIDTH), f32),
        'gk_w2': nrm(ks[6], (L, GLA_GATE_RANK, GLA_KEY_WIDTH), GLA_GATE_RANK ** -0.5),
        'gk_b': nrm(ks[7], (L, GLA_KEY_WIDTH), 0.1),
        'gla_norm_w': gain(ks[8], (L, GLA_DV)),
        'w_out': nrm(ks[9], (L, MIX_WIDTH, D_MODEL), MIX_WIDTH ** -0.5),
        'norm_xattn_w': gain(ks[10], (L, D_MODEL)),
        'norm_mem_w': gain(ks[11], (L, D_MODEL)),
        'xattn_wq': nrm(ks[12], (L, D_MODEL, D_MODEL), D_MODEL ** -0.5),
        'xattn_wkv': nrm(ks[13], (L, D_MODEL, 2 * D_MODEL), D_MODEL ** -0.5),
        'xattn_wo': nrm(ks[14], (L, D_MODEL, D_MODEL), D_MODEL ** -0.5),
        'norm_ffn_w': gain(ks[15], (L, D_MODEL)),
        'ffn_w_up': nrm(ks[16], (L, D_MODEL, 2 * D_FF), D_MODEL ** -0.5),
        'ffn_conv_w': nrm(ks[17], (L, CONV_WIDTH, 2 * D_FF), CONV_WIDTH ** -0.5),
        'ffn_conv_b': nrm(ks[18], (L, 2 * D_FF), 0.01),
        'ffn_w_down': nrm(ks[19], (L, D_FF, D_MODEL), D_FF ** -0.5),
        'norm_final_w': gain(ks[20], (D_MODEL,)),
    }

def second_block(x, mem, norm_mix_w, w_in, pool_w, pool_scale, gk_w2, gk_b, gla_norm_w, w_out,
              norm_xattn_w, norm_mem_w, xattn_wq, xattn_wkv, xattn_wo,
              norm_ffn_w, ffn_w_up, ffn_conv_w, ffn_conv_b, ffn_w_down, norm_final_w):
    for l in range(DEPTH_2):
        h = rms_norm_2(x, norm_mix_w[l])
        x = x + hybrid_mixer(h, w_in[l], pool_w[l], pool_scale[l], gk_w2[l], gk_b[l], gla_norm_w[l], w_out[l])
        h = rms_norm_2(x, norm_xattn_w[l])
        m = rms_norm_2(mem, norm_mem_w[l])
        x = x + memory_cross_attention(h, m, xattn_wq[l], xattn_wkv[l], xattn_wo[l])
        h = rms_norm_2(x, norm_ffn_w[l])
        x = x + conv_ffn(h, ffn_w_up[l], ffn_conv_w[l], ffn_conv_b[l], ffn_w_down[l])
    return rms_norm_2(x, norm_final_w)


def setup_inputs(seed=0):
    out = dict(first_inputs(seed))
    for name, value in second_inputs(seed + 1).items():
        if name != "x":
            out[name + "_2"] = value
    return out


def reference(
    x, c, positions, ada_w, ada_b, norm_g, nsa_w_in, nsa_w_out, nsa_cmp_pe, nsa_phi_w1,
    nsa_phi_b1, nsa_phi_w2, nsa_phi_b2, swa_w_in, swa_w_out, swa_sinks, mlp_w_up, mlp_w_down,
    mem_2, norm_mix_w_2, w_in_2, pool_w_2, pool_scale_2, gk_w2_2, gk_b_2, gla_norm_w_2, w_out_2,
    norm_xattn_w_2, norm_mem_w_2, xattn_wq_2, xattn_wkv_2, xattn_wo_2, norm_ffn_w_2, ffn_w_up_2,
    ffn_conv_w_2, ffn_conv_b_2, ffn_w_down_2, norm_final_w_2,
):
    x = first_block(
        x, c, positions, ada_w, ada_b, norm_g, nsa_w_in, nsa_w_out, nsa_cmp_pe, nsa_phi_w1,
        nsa_phi_b1, nsa_phi_w2, nsa_phi_b2, swa_w_in, swa_w_out, swa_sinks, mlp_w_up,
        mlp_w_down,
    )
    return second_block(
        x, mem_2, norm_mix_w_2, w_in_2, pool_w_2, pool_scale_2, gk_w2_2, gk_b_2, gla_norm_w_2,
        w_out_2, norm_xattn_w_2, norm_mem_w_2, xattn_wq_2, xattn_wkv_2, xattn_wo_2,
        norm_ffn_w_2, ffn_w_up_2, ffn_conv_w_2, ffn_conv_b_2, ffn_w_down_2, norm_final_w_2,
    )


_drawn_inputs = setup_inputs


def setup_inputs(seed=0):
    import zlib

    import numpy as np

    out = dict(_drawn_inputs(seed))
    spreads = {}
    factors = {'nsa_phi_b1': 8.0,
     'nsa_phi_b2': 4.213,
     'swa_sinks': 4.701,
     'norm_mix_w_2': 2.809,
     'pool_scale_2': 6.114,
     'gk_b_2': 5.683,
     'gla_norm_w_2': 7.009,
     'norm_xattn_w_2': 8.0,
     'norm_mem_w_2': 8.0,
     'norm_ffn_w_2': 3.079,
     'ffn_conv_b_2': 26.8}
    for name, (base, spread) in spreads.items():
        noise = np.random.default_rng([zlib.crc32(name.encode()), seed]).standard_normal(out[name].shape)
        drawn = base * np.exp(spread * noise) if base else spread * noise
        out[name] = __import__('jax').numpy.asarray(drawn.astype(out[name].dtype))
    for name, factor in factors.items():
        out[name] = (out[name] * factor).astype(out[name].dtype)
    return out
```

```python
from contextlib import ExitStack

import concourse.bass as bass
import numpy as np
from concourse import mybir

F32 = mybir.dt.float32
F32R = mybir.dt.float32r
I32 = mybir.dt.int32
ALU = mybir.AluOpType
ACT = mybir.ActivationFunctionType
X = mybir.AxisListType.X

P = 128
D = 1024
S = 512
DC = D // P
SC = S // P
HD = 64
HEADS = D // HD
GROUPS = 4
NCMP = (S - 32) // 16 + 1
MEM = 256
MC = MEM // P
KB = 1024
NEG = -1.0e30
RING = 4

UNITS_NSA_IN = 21
UNITS_PHI = 8
UNITS_OUT = 8
UNITS_MLP = 64
UNITS_SWA_IN = 11
UNITS_MIX_IN = 17
UNITS_KV = 16
UNITS_Q = 8
FF_CHUNKS = 22
FF_GROUPS = (8, 8, 6)
UNITS_FFN = 2 * FF_CHUNKS + 8 * len(FF_GROUPS)
STAGES = (("nsa_in", UNITS_NSA_IN), ("phi", UNITS_PHI), ("nsa_out", UNITS_OUT), ("mlp0", UNITS_MLP),
          ("swa_in", UNITS_SWA_IN), ("swa_out", UNITS_OUT), ("mlp1", UNITS_MLP),
          ("mix_in", UNITS_MIX_IN), ("mix_out", UNITS_OUT), ("xq", UNITS_Q), ("kv", UNITS_KV),
          ("xo", UNITS_OUT), ("ffn", UNITS_FFN))
FIRST = {}
_n = 0
for _name, _count in STAGES:
    FIRST[_name] = _n
    _n += _count
UNITS = _n

SMALL = (("ones", P), ("ident", P), ("diag", P), ("prev", P), ("cmp_add", SC * P), 
         ("inv", 1), ("cT", DC), ("ada_b", 96), ("norm_g", 64), ("pe", 32), ("b1", 4), ("b2k", 1), ("b2v", HD),
         ("w2", 4 * HD), ("sinks", HEADS), ("norm_mix", DC), ("norm_xattn", DC), ("norm_mem", DC),
         ("norm_ffn", DC), ("norm_final", DC), ("pool_scale", 4), ("gk_b", 2), ("gla_norm", 1),
         ("conv_w", 3 * 44), ("conv_b", 44), ("pool_w", 4 * P), ("gk_w2", 256), ("invcnt", 4 * 16),
         ("tri", HD))
COL = {}
_n = 0
for _name, _count in SMALL:
    COL[_name] = (_n, _n + _count)
    _n += _count
SMALL_COLS = _n


class Count:

    def __init__(self, sem, start=0):
        self.sem, self.base, self.turn, self.per, self.inner = sem, start, None, 0, 0

    def add(self, n=1):
        self.inner += n
        return self.now()

    def now(self, ahead=0):
        if self.turn is None:
            return self.base + self.inner + ahead
        return self.turn * self.per + (self.base + self.inner + ahead)

    def enter(self, turn, per):
        self.base += self.inner
        self.turn, self.per, self.inner = turn, per, 0

    def leave(self, turns):
        assert self.inner == self.per, f"{self.sem}: {self.inner} in a turn, not {self.per}"
        self.base += self.per * turns
        self.turn, self.inner = None, 0


def over_units(eng, a, b, one):
    while a < b and (a % RING or b - a < 2 * RING):
        one(a, a % RING)
        a += 1
    turns = max(0, (b - a) // RING)
    if turns > 0:
        with eng.Fori(0, turns) as it:
            for slot in range(RING):
                one(it * RING + (a + slot), slot)
    for u in range(a + turns * RING, b):
        one(u, u % RING)


def build(nc, src, out):
    ctx = ExitStack()
    sb0 = (nc.sbuf_base + 63) // 64 * 64

    def at(name, kib, shape, dt=F32):
        return nc.alloc_sbuf_tensor_at(name, shape, dt, offset=sb0 + int(kib * KB))

    def sem(name):
        return ctx.enter_context(nc.semaphore(name))

    def scratch(name, shape):
        return nc.dram_tensor(name, shape, F32, kind="Internal").ap()

    ps = ctx.enter_context(nc.psum_tensor("ps", [P, 8, S], F32))

    x = at("x", 0, [P, DC, S])
    ah = at("ah", 16, [P, DC, S], F32R)
    al = at("al", 32, [P, DC, S], F32R)
    y = at("y", 48, [P, DC, S])
    raw = at("raw", 64, [P, RING, DC, P])
    wh = at("wh", 80, [P, RING, DC, P], F32R)
    wl = at("wl", 96, [P, RING, DC, P], F32R)
    rs = at("rs", 112, [P, 2, S])
    tt = at("tt", 116, [P, 3, S])
    sq = at("sq", 122, [P, 2, S])
    ada_ring = at("ada_ring", 116, [P, 2, 1024])
    sm = at("sm", 126, [P, SMALL_COLS])
    k1 = 126 + (SMALL_COLS * 4 + KB - 1) // KB
    mod = at("mod", k1, [P, 96])
    cond = at("cond", k1 + 0.375, [P, DC])
    coef = at("coef", k1 + 0.4375, [P, 2, 6, DC])
    eps = at("eps", k1 + 0.875, [P, 1])
    neg_sinks = at("neg_sinks", k1 + 0.9375, [P, HEADS])
    ident_r = at("ident_r", k1 + 1, [P, P], F32R)
    diag_r = at("diag_r", k1 + 1.5, [P, P], F32R)
    prev_r = at("prev_r", k1 + 2, [P, P], F32R)
    w0 = k1 + 2.5
    assert w0 + 68 <= 207.75, w0

    def small(name):
        a, b = COL[name]
        return sm[:, a:b]

    hh = at("hh", w0, [P, 2, DC, S], F32R)
    hl = at("hl", w0 + 32, [P, 2, DC, S], F32R)
    ada0 = at("ada0", w0, [P, RING, 1024])
    acc = at("acc", w0 + 64, [P, 1024])

    pair = at("pair", w0, [P, 6, S])
    rot_h = at("rot_h", w0 + 12, [P, 2, 2, S], F32R)
    rot_l = at("rot_l", w0 + 20, [P, 2, 2, S], F32R)
    rot_f = at("rot_f", w0 + 28, [P, 2, S])
    vtmp = at("vtmp", w0 + 32, [P, 2, S])
    xb = at("xb", w0 + 36, [P, 16, 4 * NCMP])
    xb_h = at("xb_h", w0 + 44, [P, 16, 4 * NCMP], F32R)
    xb_l = at("xb_l", w0 + 52, [P, 16, 4 * NCMP], F32R)
    h1 = at("h1", w0 + 60, [P, 2, 2, 4 * NCMP])
    kc_f = at("kc_f", w0 + 62, [P, 4, 32])
    kc_h = at("kc_h", w0 + 62.5, [P, 4, 32], F32R)
    kc_l = at("kc_l", w0 + 63, [P, 4, 32], F32R)
    vc_f = at("vc_f", w0 + 63.5, [P, 4, HD])
    gates = at("gates", w0 + 64.5, [P, SC, P])
    x2 = at("x2", 48, [P, 2, 4, S])
    ang = at("ang", 48, [P, 6, S])
    pos_i = at("pos_i", 60, [P, S], I32)
    trig = at("trig", 112, [P, 2, S])
    qs = at("qs", w0, [P, 4, S], F32R)
    ks = at("ks", w0 + 8, [P, 2, 2, S], F32R)
    vs = at("vs", w0 + 16, [P, 2, SC, HD])
    pr = at("pr", w0 + 18, [P, 2, S])
    pt = at("pt", w0 + 22, [P, 2, S])
    og = at("og", w0 + 26, [P, SC, 4 * HD])
    kcs = at("kcs", w0 + 30, [P, 2, 32], F32R)
    vb = at("vb", w0 + 31, [P, 4 * HD])
    st = at("st", w0 + 32, [P, 8, 4])
    st4 = at("st4", w0 + 33, [P, 4, 4])
    gg = at("gg", w0 + 34, [P, SC, 12])
    gs = at("gs", w0 + 34.25, [P, 2, 4])

    qscr = scratch("qscr", [HEADS, P, S])
    kscr = scratch("kscr", [2, GROUPS, 2, P, S])
    vscr = scratch("vscr", [2, GROUPS, P, SC, HD])
    cscr = scratch("cscr", [2, GROUPS, HD, S])
    kcscr = scratch("kcscr", [GROUPS, 2, P, 32])
    vcscr = scratch("vcscr", [GROUPS, 32, HD])
    trscr = scratch("trscr", [P, 2, S])

    po = at("po", 48, [P, 4, S])
    go = at("go", 56, [P, 4, S])
    mq = at("mq", w0, [P, 2, S])
    mk = at("mk", w0 + 4, [P, 2, S])
    mv = at("mv", w0 + 8, [P, SC, S])
    mr = at("mr", w0 + 16, [P, 4, S])
    lo_g = at("lo_g", w0 + 24, [16, S])
    gl = at("gl", w0 + 26, [P, 2, S])
    gl2 = at("gl2", w0 + 30, [P, 2, S])
    qd = at("qd", w0 + 34, [P, 2, S])
    kd = at("kd", w0 + 38, [P, 2, S])
    ke = at("ke", w0 + 42, [P, 2, S])
    ken = at("ken", w0 + 46, [P, SC, 2 * P])
    stt = at("stt", w0 + 50, [P, 8, 2, P])
    sct = at("sct", w0 + 58, [P, 2, 4, 2, HD])
    dec = at("dec", w0 + 62, [P, 2, 8])
    pd = at("pd", w0 + 62.5, [P, S])

    me = at("me", w0, [P, DC, MEM])
    mh = at("mh", w0 + 8, [P, DC, MEM], F32R)
    ml = at("ml", w0 + 16, [P, DC, MEM], F32R)
    xk = at("xk", w0 + 24, [P, DC, MEM])
    xv = at("xv", w0 + 32, [P, MC, D])
    xq = at("xq", w0 + 40, [P, DC, S])
    xp = at("xp", w0 + 56, [P, 2, MEM])
    xt = at("xt", w0 + 58, [P, 2, MC, S])
    xs = at("xs", w0 + 66, [P, 16, 4])

    uc = at("uc", 48, [P, 2, 2, S])
    ah_f = at("ah_f", 16, [P, DC, S])

    raw_in = [sem(f"raw_in{i}") for i in range(RING)]
    hi_done = sem("hi_done")
    lo_done = sem("lo_done")
    unit_used = sem("unit_used")
    evac = sem("evac")
    v_step = sem("v_step")
    a_step = sem("a_step")
    small_in = sem("small_in")
    x_in = sem("x_in")
    ada_in = [sem(f"ada_in{i}") for i in range(RING)]
    cond_done = sem("cond_done")
    ada_used = sem("ada_used")
    ada_sum = sem("ada_sum")
    ada_read = sem("ada_read")
    setup_done = sem("setup_done")
    ang_done = sem("ang_done")
    trig_made = sem("trig_made")
    trig_kept = sem("trig_kept")
    trig_in = sem("trig_in")
    x_new = sem("x_new")
    sq_made = sem("sq_made")
    sq_used = sem("sq_used")
    std_made = sem("std_made")
    t_made = sem("t_made")
    high_made = sem("high_made")
    a_ready = sem("a_ready")
    rot_made = sem("rot_made")
    rot_kept = [sem(f"rot_kept{i}") for i in range(2)]
    kc_made = sem("kc_made")
    v_made = sem("v_made")
    v_kept = [sem(f"v_kept{i}") for i in range(2)]
    c_kept = sem("c_kept")
    x2_in = [sem(f"x2_in{i}") for i in range(2)]
    xb_made = sem("xb_made")
    z_made = sem("z_made")
    h1_made = sem("h1_made")
    comp_made = sem("comp_made")
    comp_ready = sem("comp_ready")
    comp_kept = sem("comp_kept")
    gate_raw = sem("gate_raw")
    gate_made = sem("gate_made")
    q_in = [sem(f"q_in{i}") for i in range(4)]
    k_in = [sem(f"k_in{i}") for i in range(2)]
    vv_in = [sem(f"vv_in{i}") for i in range(2)]
    kcs_in = sem("kcs_in")
    vb_in = sem("vb_in")
    vb_clear = sem("vb_clear")
    sc_made = sem("sc_made")
    nm_made = sem("nm_made")
    p_made = sem("p_made")
    pc_made = sem("pc_made")
    p_turned = sem("p_turned")
    pt_made = sem("pt_made")
    pv_made = sem("pv_made")
    o_added = sem("o_added")
    o_turned = sem("o_turned")
    o_split = sem("o_split")
    hid_made = sem("hid_made")

    gate_sum = sem("gate_sum")
    gate_exp = sem("gate_exp")
    cum_exp = sem("cum_exp")
    silu_made = sem("silu_made")
    pooled = sem("pooled")
    pool_mixed = sem("pool_mixed")
    decays = sem("decays")
    ke_turned = sem("ke_turned")
    ken_made = sem("ken_made")
    gla_scores = sem("gla_scores")
    chunk_kv = sem("chunk_kv")
    states = sem("states")
    gla_out = sem("gla_out")
    gla_o = sem("gla_o")
    gla_sq = sem("gla_sq")
    gla_ss = sem("gla_ss")
    gla_std = sem("gla_std")
    gla_used = sem("gla_used")
    mix_ready = sem("mix_ready")
    xs_made = sem("xs_made")
    xn_made = sem("xn_made")
    xp_made = sem("xp_made")
    xp_normed = sem("xp_normed")
    xp_turned = sem("xp_turned")
    xt_made = sem("xt_made")
    xo_made = sem("xo_made")
    xo_split = sem("xo_split")
    conv_silu = sem("conv_silu")
    out_ready = sem("out_ready")
    out_kept = sem("out_kept")

    TAU = 2 * float(np.pi)
    TAU1 = 6.28125
    TAU2 = float(np.float32(np.round((TAU - TAU1) * 2 ** 21) / 2 ** 21))
    TAU3 = TAU - TAU1 - TAU2
    ROUND = 1.5 * 2 ** 23
    PI_IN = float(np.nextafter(np.float32(np.pi), np.float32(0)))
    V_STEPS = {"nsa": 127, "swa": 51}
    ROT_DMAS, ROT_DMAS_SWA, V_DMAS = (16, 16), (16, 8), (4, 4)

    def kv_place(n, pair):
        return (2, 3, 6, 7)[2 * (n % 2) + n // 4], n // 2 % 2 * 256 + pair * P

    A_READY = {k: DC * i for i, k in enumerate(("nsa_in", "mlp0", "swa_in", "mlp1", "mix_in", "xq", "mem", "ffn"))}
    BANKS_MIX_OUT = FIRST["xq"] - 4 + 4
    FFN_BLOCKS = (("up", 0), ("up", 1), ("down", 0), ("up", 2), ("down", 1), ("down", 2))

    SCALE = HD ** -0.5

    def works(ncmp, branches):
        return [("cmp", 0, i) for i in range(ncmp)] + [(b, j, i) for b in branches for j in range(4) for i in range(SC)]

    NSA = dict(works=works(SC, (0, 1)), window=False, base=0, turns=0, sink=False)
    SWA = dict(works=works(0, (0,)), window=True, base=GROUPS * len(NSA["works"]), turns=GROUPS, sink=True)

    def keys_of(att, i):
        return (max(i - 1, 0) if att["window"] else 0), i + 1

    MLP_BLOCKS = (("up", 0), ("up", 1), ("down", 0), ("up", 2), ("down", 1), ("up", 3), ("down", 2), ("down", 3))

    block = ctx.enter_context(nc.Block())

    @block.sync
    def _(sp):
        sp.dma_start(sm[:], src["small"]).then_inc(small_in, 16)
        sp.dma_start(pos_i[:], src["pos"]).then_inc(small_in, 16)
        sp.dma_start(x[:], src["xT"]).then_inc(x_in, 16)

        def units(a, b):
            def one(u, slot):
                if not isinstance(u, int) or u >= RING:
                    sp.wait_ge(lo_done, u - (RING - 1))
                sp.dma_start(raw[:, slot].rearrange("p k m -> p (k m)"),
                             src["units"][bass.ds(u, 1)].rearrange("a p n -> p (a n)")).then_inc(raw_in[slot], 16)
            over_units(sp, a, b, one)

        def group_loads(att, g, first):
            n, ncmp = len(att["works"]), len(att["works"]) % 16

            def after(work):
                if not first:
                    sp.wait_ge(pv_made, g * n + (att["base"] + work - n))
                elif att["base"]:
                    sp.wait_ge(pv_made, att["base"])
            if ncmp:
                after(ncmp)
                sp.dma_start(kcs[:].bitcast(F32).rearrange("p h n -> p h n"),
                             kcscr[bass.ds(g, 1)].rearrange("a h p n -> p (a h) n")).then_inc(kcs_in, 16)
                for j in range(4):
                    sp.dma_start(vb[32 * j:32 * j + 32, HD * j:HD * j + HD],
                                 vcscr[bass.ds(g, 1)].rearrange("a n d -> n (a d)")).then_inc(vb_in, 16)
            for b in range((n - ncmp) // 16):
                after(ncmp + 16 * (b + 1))
                sp.dma_start(ks[:, b].bitcast(F32),
                             kscr[b, bass.ds(g, 1)].rearrange("a h p t -> p (a h) t")).then_inc(k_in[b], 16)
                sp.dma_start(vs[:, b], vscr[b, bass.ds(g, 1)].rearrange("a p i d -> p (a i) d")).then_inc(vv_in[b], 16)
            for j in range(4):
                after(n)
                sp.dma_start(qs[:, j].bitcast(F32),
                             qscr[bass.ds(g * 4 + j, 1)].rearrange("a p t -> p (a t)")).then_inc(q_in[j], 16)

        for n in range(48):
            if n >= RING:
                sp.wait_ge(ada_used, n - RING + 1)
            sp.dma_start(ada0[:, n % RING], src["ada"][n]).then_inc(ada_in[n % RING], 16)
        sp.wait_ge(trig_made, 2)
        sp.dma_start(trscr, ang[:, 4:6]).then_inc(trig_kept, 16)
        units(0, RING)
        sp.wait_ge(trig_kept, 16)
        sp.wait_ge(t_made, DC)
        sp.dma_start(trig[:], trscr).then_inc(trig_in, 16)
        units(RING, 8)
        sp.wait_ge(c_kept, 64)
        for kind in range(2):
            for half in range(2):
                sp.dma_start(x2[64 * half:64 * half + 64, kind, :, 0:S - half],
                             cscr[kind].rearrange("g d t -> d g t")[:, :, half:S]).then_inc(x2_in[kind], 16)
        units(8, FIRST["nsa_out"] + RING)
        sp.wait_ge(comp_kept, 16 * 5)
        for r in range(2):
            sp.wait_ge(rot_kept[r], 16 * ROT_DMAS[r])
            sp.wait_ge(v_kept[r], 16 * V_DMAS[r])
        sp.wait_ge(vb_clear, 1)
        group_loads(NSA, 0, True)
        with sp.Fori(1, GROUPS) as g:
            group_loads(NSA, g, False)
        units(FIRST["nsa_out"] + RING, FIRST["swa_in"] + RING)
        sp.wait_ge(t_made, 3 * DC)
        sp.dma_start(trig[:], trscr).then_inc(trig_in, 16)
        units(FIRST["swa_in"] + RING, FIRST["swa_out"] + RING)
        for r in range(2):
            sp.wait_ge(rot_kept[r], 16 * (ROT_DMAS[r] + ROT_DMAS_SWA[r]))
        sp.wait_ge(v_kept[0], 16 * (V_DMAS[0] + GROUPS))
        group_loads(SWA, 0, True)
        with sp.Fori(1, GROUPS) as g:
            group_loads(SWA, g, False)
        units(FIRST["swa_out"] + RING, FIRST["xq"] + RING)
        sp.wait_ge(evac, BANKS_MIX_OUT)
        sp.dma_start(me[:], src["memT"]).then_inc(x_in, 16)
        units(FIRST["xq"] + RING, UNITS)
        sp.wait_ge(out_ready, DC)
        sp.dma_start(out, ah_f[:]).then_inc(out_kept, 16)
        sp.wait_ge(out_kept, 16)

    @block.gpsimd
    def _(pool):
        def low(u, slot):
            pool.wait_ge(hi_done, u + 1)
            nc.gpsimd.tensor_tensor(wl[:, slot], raw[:, slot], wh[:, slot].bitcast(F32), ALU.subtract).then_inc(lo_done, 1)
        over_units(pool, 0, UNITS, low)

    @block.tensor
    def _(pe):
        done = [0]

        def bank_free(n):
            if not isinstance(n, int) or n >= RING:
                pe.wait_ge(evac, n - (RING - 1))

        def products(out_ap, slot, high, low, k0=0, ks=DC, first=True, last=True, ready=None):
            for k in range(ks):
                if ready is not None:
                    pe.wait_ge(ready[0], ready[1] + k + 1)
                nc.tensor.matmul(out_ap, wh[:, slot, k], high[:, k0 + k], start=first and k == 0, stop=False)
                nc.tensor.matmul(out_ap, wl[:, slot, k], high[:, k0 + k], start=False, stop=False)
                mm = nc.tensor.matmul(out_ap, wh[:, slot, k], low[:, k0 + k], start=False, stop=last and k == ks - 1)
            return mm

        def products_t(bank, slot, high, low, tokens, ready=None):
            if ready is not None:
                pe.wait_ge(ready[0], ready[1] + DC)
            for i in range(tokens // P):
                o = ps[:, bank, i * P:(i + 1) * P]
                t = slice(i * P, (i + 1) * P)
                for k in range(DC):
                    nc.tensor.matmul(o, high[:, k, t], wh[:, slot, k], start=k == 0, stop=False)
                    nc.tensor.matmul(o, high[:, k, t], wl[:, slot, k], start=False, stop=False)
                    mm = nc.tensor.matmul(o, low[:, k, t], wh[:, slot, k], start=False, stop=k == DC - 1)
            return mm

        def gemm(first, count, high, low, turned=False, tokens=S, ks=DC, ready=None, each=1):
            n0 = done[0] - first

            def one(u, slot):
                n = u + n0
                bank = (slot + n0) % RING
                bank_free(n)
                pe.wait_ge(lo_done, u + 1)
                if turned:
                    mm = products_t(bank, slot, high, low, tokens, ready)
                else:
                    mm = products(ps[:, bank, 0:tokens], slot, high, low, ks=ks, ready=ready)
                mm.then_inc(unit_used, 1)
            over_units(pe, first, first + count, one)
            done[0] += count

        squares = [0]

        def square_sum(c, tokens=S):
            q = squares[0]
            pe.wait_ge(sq_made, DC * q + c + 1)
            nc.tensor.matmul(ps[:, 4 + q % 2, 0:tokens], small("ones"), sq[:, c % 2, 0:tokens],
                             start=c == 0, stop=c == DC - 1).then_inc(sq_used, 1)
            if c == DC - 1:
                squares[0] += 1

        def square_sums(tokens=S):
            for c in range(DC):
                square_sum(c, tokens)

        def gemm_squared(first, high, low, ready=None, ks=DC):
            for c in range(DC):
                gemm(first + c, 1, high, low, ready=ready, ks=ks)
                if c:
                    square_sum(c - 1)
            square_sum(DC - 1)

        def ada(part):
            pe.wait_ge(ada_used, 8 * (part + 1))
            for m in range(8):
                mm = nc.tensor.matmul(ps[:, 6 + part % 2, m:m + 1], acc[:, m * P:(m + 1) * P], small("ones")[:, 0:1],
                                      start=True, stop=True)
            mm.then_inc(ada_sum, 1)

        def attention(att):
            works, base, n = att["works"], att["base"], len(att["works"])
            ncmp = n % 16
            pe.wait_ge(evac, done[0])

            def group(g):
                w0 = g * n + base

                def score(w):
                    kind, j, i = works[w]
                    t = slice(i * P, (i + 1) * P)
                    bank = w % 4
                    if w >= 4:
                        pe.wait_ge(p_made, w0 + (w - 3))
                    if kind == "cmp":
                        if w == 0:
                            pe.wait_ge(kcs_in, (g + 1) * 16)
                            for h in range(4):
                                pe.wait_ge(q_in[h], (g + (att["turns"] + 1)) * 16)
                        for h in range(4):
                            for part in range(2):
                                mm = nc.tensor.matmul(ps[:, bank, 32 * h:32 * h + 32], qs[:, h, t], kcs[:, part],
                                                      start=part == 0, stop=part == 1)
                    else:
                        if i == 0 and j == 0:
                            pe.wait_ge(k_in[kind], (g + (att["turns"] + 1)) * 16)
                        if i == 0 and w < 16 and not ncmp:
                            pe.wait_ge(q_in[j], (g + (att["turns"] + 1)) * 16)
                        a, b = keys_of(att, i)
                        width = (b - a) * P
                        for part in range(2):
                            nc.tensor.matmul(ps[:, bank, 0:width], qs[:, j, t], ks[:, kind, part, a * P:b * P],
                                             start=part == 0, stop=False)
                        if att["window"] and i > 0:
                            nc.tensor.matmul(ps[:, bank, 0:P], ident_r[:], prev_r[:], start=False, stop=False)
                        mm = nc.tensor.matmul(ps[:, bank, width - P:width], ident_r[:], diag_r[:], start=False, stop=True)
                    mm.then_inc(sc_made, 1)

                def turn(w):
                    kind, j, i = works[w]
                    if w >= 2:
                        pe.wait_ge(pt_made, w0 + (w - 1))
                    if kind == "cmp":
                        pe.wait_ge(pc_made, g * ncmp + (i + 1))
                        blocks = 1
                    else:
                        pe.wait_ge(p_made, w0 + (w + 1))
                        a, b = keys_of(att, i)
                        blocks = b - a
                    for m in range(blocks):
                        mm = nc.tensor.transpose(ps[:, 4 + w % 2, m * P:(m + 1) * P], pr[:, w % 2, m * P:(m + 1) * P],
                                                 small("ident"))
                    mm.then_inc(p_turned, 1)

                def value(w):
                    kind, j, i = works[w]
                    pe.wait_ge(pt_made, w0 + (w + 1))
                    if w >= 2:
                        pe.wait_ge(o_added, w0 + (w - 1))
                    if kind == "cmp":
                        if i == 0:
                            pe.wait_ge(vb_in, (g + 1) * 64)
                        mm = nc.tensor.matmul(ps[:, 6 + w % 2, 0:4 * HD], pt[:, w % 2, 0:P], vb[:], start=True, stop=True)
                    else:
                        if i == 0 and j == 0:
                            pe.wait_ge(vv_in[kind], (g + (att["turns"] + 1)) * 16)
                        a, b = keys_of(att, i)
                        for m in range(b - a):
                            mm = nc.tensor.matmul(ps[:, 6 + w % 2, 0:HD], pt[:, w % 2, m * P:(m + 1) * P],
                                                  vs[:, kind, a + m], start=m == 0, stop=m == b - a - 1)
                    mm.then_inc(pv_made, 1)

                score(0)
                score(1)
                for w in range(n):
                    if w + 2 < n:
                        score(w + 2)
                    turn(w)
                    if w:
                        value(w - 1)
                value(n - 1)
                pe.wait_ge(o_added, w0 + n)
                for f in range(2):
                    for i in range(SC):
                        mm = nc.tensor.transpose(ps[:, f, i * P:(i + 1) * P], og[:, i, f * P:(f + 1) * P], small("ident"))
                    mm.then_inc(o_turned, 1)
                pe.wait_ge(o_split, 2 * g + 2 * (att["turns"] + 1))
            with pe.Fori(0, GROUPS) as g:
                group(g)

        def mlp(name, hid0, layer):
            u = FIRST[name]
            for b, (what, grp) in enumerate(MLP_BLOCKS):
                if what == "up":
                    gemm(u, 8, ah, al, ready=(a_ready, A_READY[name]))
                else:
                    pe.wait_ge(hid_made, hid0 + 8 * (grp + 1))
                    if b == 7:
                        gemm_squared(u, hh[:, grp % 2], hl[:, grp % 2])
                    else:
                        gemm(u, 8, hh[:, grp % 2], hl[:, grp % 2])
                if layer == 0 and b < 6:
                    ada(6 + b)
                u += 8

        pe.wait_ge(setup_done, 1)
        for part in range(6):
            ada(part)
        square_sums()
        u = FIRST["nsa_in"]
        gemm(u, RING, ah, al, ready=(a_ready, 0))
        gemm(u + RING, 16 - RING, ah, al, ready=(a_ready, 0))
        gemm(u + 16, 5, ah, al, turned=True)
        for m in range(4):
            n = done[0]
            bank_free(n)
            for half in range(2):
                v = FIRST["phi"] + 2 * m + half
                pe.wait_ge(lo_done, v + 1)
                if half == 0:
                    pe.wait_ge(xb_made, m // 2 + 1)
                products(ps[:, n % RING, 0:4 * NCMP], v % RING, xb_h, xb_l, k0=8 * half,
                         first=half == 0, last=half == 1).then_inc(unit_used, 1)
            done[0] += 1
        w2 = small("w2").rearrange("p (k c d) -> p k c d", k=2, c=2)
        pe.wait_ge(h1_made, 4)
        for c in range(2):
            mm = nc.tensor.matmul(ps[0:HD, 4, 0:4 * NCMP], w2[:, 0, c], h1[:, 0, c], start=c == 0, stop=c == 1)
        for g in range(GROUPS):
            for c in range(2):
                mm = nc.tensor.matmul(ps[0:NCMP, 5, g * HD:(g + 1) * HD], h1[:, 1, c, g * NCMP:(g + 1) * NCMP],
                                      w2[:, 1, c], start=c == 0, stop=c == 1)
        mm.then_inc(comp_made, 1)
        pe.wait_ge(comp_ready, 1)
        attention(NSA)
        gemm_squared(FIRST["nsa_out"], ah, al)
        square_sums()
        mlp("mlp0", 0, 0)
        square_sums()
        gemm(FIRST["swa_in"], 10, ah, al, ready=(a_ready, A_READY["swa_in"]))
        gemm(FIRST["swa_in"] + 10, 1, ah, al, turned=True)
        attention(SWA)
        gemm_squared(FIRST["swa_out"], ah, al)
        square_sums()
        mlp("mlp1", 32, 1)
        square_sums()
        gemm(FIRST["mix_in"], 13, ah, al, ready=(a_ready, A_READY["mix_in"]))
        gemm(FIRST["mix_in"] + 13, 4, ah, al, turned=True)
        pe.wait_ge(evac, done[0] - 16)
        for c in range(2):
            mm = nc.tensor.matmul(ps[:, 6 + c], small("gk_w2")[0:16, c * P:(c + 1) * P], lo_g[:], start=True, stop=True)
        mm.then_inc(gate_sum, 1)
        for g in range(4):
            n = done[0]
            bank_free(n)
            pe.wait_ge(pooled, g + 1)
            nc.tensor.matmul(ps[:, n % RING], small("pool_w")[:, g * P:(g + 1) * P], pd[:],
                             start=True, stop=True).then_inc(pool_mixed, 1)
            done[0] += 1
        pe.wait_ge(evac, done[0])
        pe.wait_ge(decays, 1)
        for c in range(2):
            for i in range(SC):
                mm = nc.tensor.transpose(ps[:, 4 + c, i * P:(i + 1) * P], ke[:, c, i * P:(i + 1) * P], small("ident"))
        mm.then_inc(ke_turned, 1)
        for n in range(8):
            for h in range(4):
                r, a = slice(64 * (h % 2), 64 * (h % 2) + 64), 64 * (n % 2)
                col = (n // 2) * P + h // 2 * HD
                mm = nc.tensor.matmul(ps[a:a + 64, h % 2, col:col + 64], kd[r, h // 2, 64 * n:64 * n + 64],
                                      qd[r, h // 2, 64 * n:64 * n + 64], start=True, stop=True)
        mm.then_inc(gla_scores, 1)
        pe.wait_ge(ken_made, 1)
        for n in range(7):
            for h in range(4):
                t = slice(64 * (n % 2), 64 * (n % 2) + 64)
                d = 64 * (h % 2)
                b, col = kv_place(n, h // 2)
                mm = nc.tensor.matmul(ps[d:d + 64, b, col:col + P], ken[t, n // 2, h * HD:(h + 1) * HD],
                                      mv[t, n // 2, h * P:(h + 1) * P], start=True, stop=True)
        mm.then_inc(chunk_kv, 1)
        pe.wait_ge(states, 1)
        for h in range(4):
            r = slice(64 * (h % 2), 64 * (h % 2) + 64)
            for n in range(8):
                t, col = slice(64 * (n % 2), 64 * (n % 2) + 64), h % 2 * 256 + n // 2 * 64
                nc.tensor.matmul(ps[:, 2 * (n % 2) + h // 2, col:col + 64], mv[t, n // 2, h * P:(h + 1) * P],
                                 sct[t, h % 2, n // 2, h // 2], start=True, stop=True)
                mm = nc.tensor.matmul(ps[:, 4 + 2 * (h % 2) + h // 2, 64 * n:64 * n + 64], stt[r, n, h // 2],
                                      qd[r, h // 2, 64 * n:64 * n + 64], start=True, stop=True)
            mm.then_inc(gla_out, 1)
        pe.wait_ge(gla_o, 4)
        for h in range(4):
            pe.wait_ge(gla_sq, h + 1)
            nc.tensor.matmul(ps[:, 4 + h % 2], small("ones"), sq[:, h % 2], start=True, stop=True).then_inc(gla_ss, 1)
        gemm_squared(FIRST["mix_out"], ah, al, ready=(mix_ready, 0))
        gemm(FIRST["xq"], 8, ah, al, ready=(a_ready, A_READY["xq"]))
        square_sums(MEM)
        gemm(FIRST["kv"], 8, mh, ml, tokens=MEM, ready=(a_ready, A_READY["mem"]))
        gemm(FIRST["kv"] + 8, 8, mh, ml, turned=True, tokens=MEM)
        pe.wait_ge(evac, done[0])

        def xscore(w):
            h, i = w // SC, w % SC
            if w >= 4:
                pe.wait_ge(xp_made, w - 3)
            for c in range(2):
                mm = nc.tensor.matmul(ps[:, w % 4, 0:MEM], xq[:, 2 * h + c, i * P:(i + 1) * P], xk[:, 2 * h + c],
                                      start=c == 0, stop=c == 1)
            mm.then_inc(xs_made, 1)

        xscore(0)
        xscore(1)
        for w in range(16):
            h, i = w // SC, w % SC
            if w + 2 < 16:
                xscore(w + 2)
            pe.wait_ge(xp_normed, w + 1)
            if w >= 2:
                pe.wait_ge(xt_made, w - 1)
            for m in range(MC):
                mm = nc.tensor.transpose(ps[:, 4 + w % 2, m * P:(m + 1) * P], xp[:, w % 2, m * P:(m + 1) * P],
                                         small("ident"))
            mm.then_inc(xp_turned, 1)
            if i == SC - 1:
                pe.wait_ge(xt_made, w + 1)
                if h:
                    pe.wait_ge(xo_split, 2 * h)
                for e in range(2):
                    for m in range(MC):
                        mm = nc.tensor.matmul(ps[:, 6 + e], xv[:, m, (2 * h + e) * P:(2 * h + e + 1) * P],
                                              xt[:, h % 2, m], start=m == 0, stop=m == MC - 1)
                    mm.then_inc(xo_made, 1)
        gemm_squared(FIRST["xo"], ah, al, ready=(xo_split, 0))
        u = FIRST["ffn"]
        made = 0
        for what, grp in FFN_BLOCKS:
            n = FF_GROUPS[grp]
            if what == "up":
                gemm(u, 2 * n, ah, al, ready=(a_ready, A_READY["ffn"]))
                u += 2 * n
            else:
                pe.wait_ge(hid_made, 64 + sum(FF_GROUPS[:grp + 1]))
                if grp == 2:
                    gemm_squared(u, hh[:, grp % 2], hl[:, grp % 2], ks=n)
                else:
                    gemm(u, 8, hh[:, grp % 2], hl[:, grp % 2], ks=n)
                u += 8

    @block.vector
    def _(dve):
        v = nc.vector
        chain = Count(v_step)
        banks = [0]
        units = [0]
        normed = [0]
        stds = [0]
        added = [0]

        def mark(ins):
            ins.then_inc(v_step, 1)
            return chain.add()

        def link(ins):
            dve.wait_ge(v_step, mark(ins))

        def rms(slot, tokens=S):
            stds[0] += 1
            dve.wait_ge(std_made, stds[0])
            link(v.reciprocal(rs[:, slot, 0:tokens], rs[:, slot, 0:tokens]))

        def add_y(layer, which):
            rms(0)
            t0 = mark(v.tensor_tensor(tt[:, 0], y[:, 0], rs[:, 0], ALU.mult))
            x0 = DC * added[0]
            added[0] += 1
            for c in range(DC):
                if c + 1 < DC:
                    if c >= 2:
                        dve.wait_ge(x_new, x0 + c - 1)
                    t1 = mark(v.tensor_tensor(tt[:, (c + 1) % 3], y[:, c + 1], rs[:, 0], ALU.mult))
                dve.wait_ge(v_step, t0)
                v.scalar_tensor_tensor(out=x[:, c], in0=tt[:, c % 3], scalar=coef[:, layer, which, c:c + 1], in1=x[:, c],
                                       op0=ALU.mult, op1=ALU.add).then_inc(x_new, 1)
                t0 = t1

        def norm(src_t, high, low, tokens=S):
            rms(1, tokens)
            n0 = DC * normed[0]

            def scaled(c):
                v.tensor_tensor(tt[:, c % 3, 0:tokens], src_t[:, c], rs[:, 1, 0:tokens], ALU.mult).then_inc(t_made, 1)
            scaled(0)
            scaled(1)
            for c in range(DC):
                if c + 2 < DC:
                    if c:
                        dve.wait_ge(a_ready, n0 + c)
                    scaled(c + 2)
                dve.wait_ge(high_made, n0 + c + 1)
                v.tensor_tensor(low[:, c], tt[:, c % 3, 0:tokens], high[:, c].bitcast(F32), ALU.subtract).then_inc(a_ready, 1)
            normed[0] += 1

        def bank():
            b = banks[0] % RING
            banks[0] += 1
            units[0] += 1
            dve.wait_ge(unit_used, units[0])
            return ps[:, b]

        def banks_loop(count, one, steps=0):
            with dve.Fori(0, count // RING) as it:
                chain.enter(it, steps)
                for j in range(RING):
                    dve.wait_ge(unit_used, it * RING + (units[0] + j + 1))
                    one(it * RING + j, j, ps[:, (banks[0] + j) % RING])
                chain.leave(count // RING)
            banks[0] += count
            units[0] += count

        v.memset(eps[:], 1e-6)
        dve.wait_ge(small_in, 32)
        v.tensor_copy(ident_r[:], small("ident"))
        v.tensor_copy(diag_r[:], small("diag"))
        v.tensor_copy(prev_r[:], small("prev"))
        v.tensor_scalar(neg_sinks[:], small("sinks"), -1.0, None, ALU.mult)
        v.memset(acc[:], 0.0).then_inc(setup_done, 1)
        link(v.tensor_copy(ang[:, 0], pos_i[:]))
        link(v.tensor_scalar(ang[:, 1], ang[:, 0], small("inv"), None, ALU.mult))
        for half in range(2):
            link(v.tensor_scalar(ang[:, 2], ang[:, 1], 1 / TAU, 0.25 * half, ALU.mult, ALU.add))
            link(v.tensor_scalar(ang[:, 2], ang[:, 2], ROUND, None, ALU.add))
            link(v.tensor_scalar(ang[:, 2], ang[:, 2], -ROUND, None, ALU.add))
            link(v.scalar_tensor_tensor(out=ang[:, 3], in0=ang[:, 2], scalar=-TAU1, in1=ang[:, 1], op0=ALU.mult, op1=ALU.add))
            link(v.scalar_tensor_tensor(out=ang[:, 3], in0=ang[:, 2], scalar=-TAU2, in1=ang[:, 3], op0=ALU.mult, op1=ALU.add))
            link(v.scalar_tensor_tensor(out=ang[:, 3], in0=ang[:, 2], scalar=-TAU3, in1=ang[:, 3], op0=ALU.mult, op1=ALU.add))
            link(v.tensor_scalar(ang[:, 3], ang[:, 3], half * TAU / 4, PI_IN, ALU.add, ALU.min))
            v.tensor_scalar(ang[:, 5 - half], ang[:, 3], -PI_IN, None, ALU.max).then_inc(ang_done, 1)

        def ada_read_out(part):
            dve.wait_ge(ada_sum, part + 1)
            link(v.tensor_tensor(mod[:, 8 * part:8 * part + 8], ps[:, 6 + part % 2, 0:8],
                                 small("ada_b")[:, 8 * part:8 * part + 8], ALU.add))

        def ada_coef(layer):
            def m(p):
                return mod[:, 48 * layer + 8 * p:48 * layer + 8 * p + 8]

            def g(i):
                return small("norm_g")[:, 32 * layer + 8 * i:32 * layer + 8 * i + 8]
            for which, gain, part in ((0, 0, 1), (2, 1, 2), (3, 2, 4), (5, 3, 5)):
                v.scalar_tensor_tensor(out=coef[:, layer, which], in0=m(part), scalar=1.0, in1=g(gain), op0=ALU.add, op1=ALU.mult)
            v.tensor_copy(coef[:, layer, 1], m(0))
            link(v.tensor_copy(coef[:, layer, 4], m(3)))

        dve.wait_ge(cond_done, 1)
        for part in range(6):
            for k in range(8):
                n = 8 * part + k
                dve.wait_ge(ada_in[n % RING], 16 * (n // RING + 1))
                if k == 0:
                    op = v.tensor_scalar(acc[:], ada0[:, n % RING], cond[:, 0:1], None, ALU.mult)
                else:
                    op = v.scalar_tensor_tensor(out=acc[:], in0=ada0[:, n % RING], scalar=cond[:, k:k + 1], in1=acc[:],
                                                op0=ALU.mult, op1=ALU.add)
                op.then_inc(ada_used, 1)
                dve.wait_ge(ada_used, n + 1)
            ada_read_out(part)
        ada_coef(0)
        norm(x, ah, al)

        rot_uses = [0, 0]
        rots = [0]

        def rotary(dmas, whole=False):
            n = banks[0]
            a, b = ps[:, n % RING], ps[:, (n + 1) % RING]
            bank()
            bank()
            cos, sin = trig[:, 0], trig[:, 1]
            v.tensor_tensor(pair[:, 0], a, cos, ALU.mult)
            v.tensor_tensor(pair[:, 3], a, sin, ALU.mult).then_inc(evac, 1)
            v.tensor_tensor(pair[:, 1], b, sin, ALU.mult)
            v.tensor_tensor(pair[:, 2], b, cos, ALU.mult).then_inc(evac, 1)
            dve.wait_ge(evac, banks[0])
            if whole:
                v.tensor_tensor(rot_f[:, 0], pair[:, 0], pair[:, 1], ALU.subtract)
                v.tensor_tensor(rot_f[:, 1], pair[:, 2], pair[:, 3], ALU.add).then_inc(kc_made, 1)
                return
            v.tensor_tensor(pair[:, 4], pair[:, 0], pair[:, 1], ALU.subtract)
            link(v.tensor_tensor(pair[:, 5], pair[:, 2], pair[:, 3], ALU.add))
            r = rots[0] % 2
            if rot_uses[r]:
                dve.wait_ge(rot_kept[r], 16 * rot_uses[r])
            rot_uses[r] += dmas
            rots[0] += 1
            link(v.tensor_copy(rot_h[:, r], pair[:, 4:6]))
            v.tensor_tensor(rot_l[:, r], pair[:, 4:6], rot_h[:, r].bitcast(F32), ALU.subtract).then_inc(rot_made, 1)

        v_uses = [0, 0]

        def keep_value(n, dmas):
            if v_uses[n % 2]:
                dve.wait_ge(v_kept[n % 2], 16 * v_uses[n % 2])
            v_uses[n % 2] += dmas
            v.tensor_copy(vtmp[:, n % 2], bank()).then_inc(evac, 1)

        def token_blocks(kind):
            dve.wait_ge(x2_in[kind], 32)
            if kind:
                dve.wait_ge(unit_used, FIRST["phi"] + 4)
            for j in range(16):
                op = v.tensor_scalar(xb[:, j].rearrange("p (g n) -> p g n", g=4),
                                     x2[:, kind, :, 2 * j:2 * j + 16 * NCMP - 15:16],
                                     small("pe")[:, 16 * kind + j:16 * kind + j + 1], None, ALU.add)
            link(op)
            link(v.tensor_copy(xb_h[:], xb[:]))
            v.tensor_tensor(xb_l[:], xb[:], xb_h[:].bitcast(F32), ALU.subtract).then_inc(xb_made, 1)

        def attention(att):
            works, base, n = att["works"], att["base"], len(att["works"])
            ncmp = n % 16
            with dve.Fori(0, GROUPS) as g:
                chain.enter(g, V_STEPS["nsa" if ncmp else "swa"])
                w0 = g * n + base
                if ncmp:
                    link(v.tensor_copy(gg[:], gates[:, :, bass.ds(g * 12, 12)]))
                else:
                    v.tensor_copy(gs[:, 0], small("sinks")[:, bass.ds(g * 4, 4)])
                    link(v.tensor_copy(gs[:, 1], neg_sinks[:, bass.ds(g * 4, 4)]))

                def maximum(w):
                    kind, j, i = works[w]
                    s = w % 4
                    dve.wait_ge(sc_made, w0 + (w + 1))
                    if kind == "cmp":
                        if w >= 2:
                            dve.wait_ge(p_turned, w0 + (w - 1))
                        a, b = COL["cmp_add"]
                        o = pr[:, w % 2, 0:P]
                        link(v.tensor_tensor(o, ps[:, s, 0:P], sm[:, a + i * P:a + (i + 1) * P], ALU.add))
                        link(v.tensor_reduce(st4[:, 0], o.rearrange("p (j n) -> p j n", j=4), X, ALU.max))
                        link(v.tensor_scalar(st4[:, 0], st4[:, 0], NEG / 10, None, ALU.max))
                        for h in range(4):
                            op = v.tensor_scalar(pr[:, w % 2, 32 * h:32 * h + 32], pr[:, w % 2, 32 * h:32 * h + 32],
                                                 st4[:, 0, h:h + 1], None, ALU.subtract)
                        op.then_inc(nm_made, 1)
                        return
                    a, b = keys_of(att, i)
                    link(v.tensor_reduce(st[:, 0, s:s + 1], ps[:, s, 0:(b - a) * P], X, ALU.max))
                    if att["sink"]:
                        op = v.tensor_scalar(st[:, 2, s:s + 1], st[:, 0, s:s + 1], -SCALE, gs[:, 1, j:j + 1], ALU.mult, ALU.min)
                    else:
                        op = v.tensor_scalar(st[:, 2, s:s + 1], st[:, 0, s:s + 1], -SCALE, None, ALU.mult)
                    op.then_inc(nm_made, 1)

                def compressed(w):
                    i = works[w][2]
                    dve.wait_ge(p_made, w0 + (w + 1))
                    o = pr[:, w % 2, 0:P]
                    link(v.tensor_reduce(st4[:, 1], o.rearrange("p (j n) -> p j n", j=4), X, ALU.add))
                    link(v.tensor_scalar(st4[:, 1], st4[:, 1], 1e-30, None, ALU.max))
                    link(v.reciprocal(st4[:, 2], st4[:, 1]))
                    link(v.tensor_tensor(st4[:, 3], st4[:, 2], gg[:, i, 0:12:3], ALU.mult))
                    for h in range(4):
                        op = v.tensor_scalar(pr[:, w % 2, 32 * h:32 * h + 32], pr[:, w % 2, 32 * h:32 * h + 32],
                                             st4[:, 3, h:h + 1], None, ALU.mult)
                    op.then_inc(pc_made, 1)

                def add(w):
                    kind, j, i = works[w]
                    s, o = w % 4, ps[:, 6 + w % 2]
                    if kind == "cmp":
                        dve.wait_ge(pv_made, w0 + (w + 1))
                        v.tensor_copy(og[:, i], o[:, 0:4 * HD]).then_inc(o_added, 1)
                        return
                    dve.wait_ge(p_made, w0 + (w + 1))
                    og_j = og[:, i, j * HD:(j + 1) * HD]
                    if att["sink"]:
                        link(v.tensor_tensor(st[:, 1, s:s + 1], st[:, 1, s:s + 1], st[:, 4, s:s + 1], ALU.add))
                        link(v.reciprocal(st[:, 3, s:s + 1], st[:, 1, s:s + 1]))
                        dve.wait_ge(pv_made, w0 + (w + 1))
                        v.tensor_scalar(og_j, o[:, 0:HD], st[:, 3, s:s + 1], None, ALU.mult).then_inc(o_added, 1)
                        return
                    link(v.reciprocal(st[:, 5, s:s + 1], st[:, 1, s:s + 1]))
                    link(v.tensor_tensor(st[:, 3, s:s + 1], st[:, 5, s:s + 1],
                                         gg[:, i, 3 * j + 1 + kind:3 * j + 2 + kind], ALU.mult))
                    dve.wait_ge(pv_made, w0 + (w + 1))
                    dve.wait_ge(o_added, w0 + (w - 3))
                    v.scalar_tensor_tensor(out=og_j, in0=o[:, 0:HD], scalar=st[:, 3, s:s + 1], in1=og_j,
                                           op0=ALU.mult, op1=ALU.add).then_inc(o_added, 1)

                maximum(0)
                maximum(1)
                for w in range(n):
                    if works[w][0] == "cmp":
                        compressed(w)
                    if w + 2 < n:
                        maximum(w + 2)
                    if w:
                        add(w - 1)
                add(n - 1)
                for f in range(2):
                    dve.wait_ge(o_turned, 2 * g + (2 * att["turns"] + f + 1))
                    link(v.tensor_copy(ah[:, bass.ds(2 * g + f, 1)], ps[:, f:f + 1]))
                    v.tensor_tensor(al[:, bass.ds(2 * g + f, 1)], ps[:, f:f + 1], ah[:, bass.ds(2 * g + f, 1)].bitcast(F32),
                                    ALU.subtract).then_inc(o_split, 1)
                chain.leave(GROUPS)

        def copy_out(count=8):
            for c in range(count):
                v.tensor_copy(y[:, c], bank()).then_inc(evac, 1)

        def mlp(layer):
            for b, (what, grp) in enumerate(MLP_BLOCKS):
                ada_now = layer == 0 and b < 6
                if ada_now:
                    part = 6 + b
                    link(v.memset(acc[:], 0.0))

                def ada_step(i, j):
                    if ada_now:
                        n = i + 8 * part
                        turn = (i - j) * 8 + (64 * (part - 6) + 16 * (j // 2) + 16 + 12 * 16)
                        dve.wait_ge(ada_in[j % 2], turn)
                        v.scalar_tensor_tensor(out=acc[:], in0=ada_ring[:, j % 2], scalar=cond[:, bass.ds(i, 1)], in1=acc[:],
                                               op0=ALU.mult, op1=ALU.add).then_inc(ada_used, 1)
                        dve.wait_ge(ada_used, n + 1)

                def up(i, j, bk):
                    r, r2 = rs[:, 0], rs[:, 1]
                    v.tensor_scalar(r, bk, 0.0, None, ALU.max).then_inc(evac, 1)
                    dve.wait_ge(evac, i + (banks[0] + 1))
                    link(v.tensor_tensor(r2, r, r, ALU.mult))
                    link(v.tensor_copy(hh[:, grp % 2, bass.ds(i, 1)], rs[:, 1:2]))
                    v.tensor_tensor(hl[:, grp % 2, bass.ds(i, 1)], rs[:, 1:2], hh[:, grp % 2, bass.ds(i, 1)].bitcast(F32),
                                    ALU.subtract).then_inc(hid_made, 1)
                    ada_step(i, j)

                def down(i, j, bk):
                    b4 = (banks[0] + j) % RING
                    yc = y[:, bass.ds(i, 1)]
                    if grp == 0:
                        v.tensor_copy(yc, ps[:, b4:b4 + 1]).then_inc(evac, 1)
                    else:
                        v.tensor_tensor(yc, ps[:, b4:b4 + 1], yc, ALU.add).then_inc(evac, 1)
                    ada_step(i, j)
                banks_loop(8, up if what == "up" else down, steps=8 if what == "up" else 0)
                if ada_now:
                    ada_read_out(part)
            if layer == 0:
                ada_coef(1)

        dve.wait_ge(trig_in, 16)
        rotary(0, whole=True)
        for n in range(2):
            v.tensor_copy(vtmp[:, n], bank()).then_inc(evac, 1)
        dve.wait_ge(kc_made, 1)
        for _ in range(2):
            rotary(4)
        token_blocks(0)
        for _ in range(2):
            rotary(4)
        for _ in range(2):
            rotary(8)
        dve.wait_ge(c_kept, 64)
        for n in range(4):
            keep_value(n, 2)
        v.tensor_copy(gates[:].rearrange("p i f -> p (i f)"), bank()).then_inc(evac, 1)
        for m in range(4):
            n = banks[0]
            banks[0] += 1
            units[0] += 2
            dve.wait_ge(unit_used, units[0])
            v.tensor_scalar(h1[:, m // 2, m % 2], ps[:, n % RING, 0:4 * NCMP], small("b1")[:, m:m + 1], None,
                            ALU.add).then_inc(evac, 1)
            if m == 1:
                token_blocks(1)
        v.memset(kc_f[:], 0.0)
        link(v.memset(vc_f[:], 0.0))
        dve.wait_ge(comp_made, 1)
        v.tensor_scalar(kc_f[0:HD, :, 0:NCMP], ps[0:HD, 4, 0:4 * NCMP].rearrange("p (g n) -> p g n", g=4),
                        small("b2k")[0:HD], None, ALU.add)
        for g in range(GROUPS):
            op = v.tensor_tensor(vc_f[0:NCMP, g], ps[0:NCMP, 5, g * HD:(g + 1) * HD], small("b2v")[0:NCMP], ALU.add)
        link(op)
        link(v.tensor_copy(kc_h[:], kc_f[:]))
        v.tensor_tensor(kc_l[:], kc_f[:], kc_h[:].bitcast(F32), ALU.subtract).then_inc(comp_ready, 1)
        dve.wait_ge(gate_made, 1)
        for r in range(2):
            dve.wait_ge(rot_kept[r], 16 * ROT_DMAS[r])
            dve.wait_ge(v_kept[r], 16 * V_DMAS[r])
        dve.wait_ge(comp_kept, 16 * 5)
        v.memset(vb[:], 0.0).then_inc(vb_clear, 1)
        attention(NSA)
        copy_out()
        add_y(0, 2)
        norm(x, ah, al)
        mlp(0)
        add_y(0, 5)
        norm(x, ah, al)
        dve.wait_ge(trig_in, 32)
        for _ in range(4):
            rotary(4)
        rotary(8)
        keep_value(0, 4)
        for r in range(2):
            dve.wait_ge(rot_kept[r], 16 * (ROT_DMAS[r] + ROT_DMAS_SWA[r]))
        dve.wait_ge(v_kept[0], 16 * (V_DMAS[0] + GROUPS))
        attention(SWA)
        copy_out()
        add_y(1, 2)
        norm(x, ah, al)
        mlp(1)
        add_y(1, 5)
        norm(x, ah, al)

        def out_bank(o, rows=P, cols=S, scale=None):
            b = bank()[0:rows, 0:cols]
            (v.tensor_copy(o, b) if scale is None else v.tensor_scalar(o, b, scale, None, ALU.mult)).then_inc(evac, 1)

        out_bank(lo_g[:], rows=16)
        for c in range(2):
            out_bank(mq[:, c], scale=HD ** -0.5)
        for c in range(2):
            out_bank(mk[:, c])
        for c in range(4):
            out_bank(mr[:, c])
        for c in range(4):
            out_bank(po[:, c])
        for c in range(4):
            b = bank()
            v.tensor_copy(mv[:, :, c * P:(c + 1) * P], b.rearrange("p (i f) -> p i f", i=SC)).then_inc(evac, 1)
        dve.wait_ge(gate_sum, 1)
        for c in range(2):
            link(v.tensor_scalar(qd[:, c], ps[:, 6 + c], small("gk_b")[:, c:c + 1], None, ALU.add))
            v.scalar_tensor_tensor(out=gl2[:, c], in0=qd[:, c], scalar=-1.0, in1=qd[:, c], op0=ALU.mult,
                                   op1=ALU.min).then_inc(gate_exp, 1)
            v.tensor_scalar(gl[:, c], qd[:, c], 0.0, None, ALU.min)
        for g in range(4):
            have, here = po[:, g], 0
            for k in range(g + 1):
                d = 1 << k
                link(v.tensor_copy(tt[:, here, 0:d], have[:, 0:d]))
                link(v.tensor_tensor(tt[:, here, d:S], have[:, d:S], have[:, 0:S - d], ALU.add))
                have, here = tt[:, here], 1 - here
            if g:
                dve.wait_ge(pool_mixed, g)
            link(v.tensor_tensor(tt[:, here, 0:16], have[:, 0:16], small("invcnt")[:, 16 * g:16 * g + 16], ALU.mult))
            v.tensor_tensor(pd[:, 0:16], tt[:, here, 0:16], po[:, g, 0:16], ALU.subtract)
            v.scalar_tensor_tensor(out=pd[:, 16:S], in0=have[:, 16:S], scalar=1.0 / (2 << g), in1=po[:, g, 16:S],
                                   op0=ALU.mult, op1=ALU.subtract).then_inc(pooled, 1)
            n = banks[0]
            banks[0] += 1
            dve.wait_ge(pool_mixed, g + 1)
            v.tensor_scalar(tt[:, 2], ps[:, n % RING], small("pool_scale")[:, g:g + 1], None, ALU.mult).then_inc(evac, 1)
            dve.wait_ge(evac, banks[0])
            link(v.tensor_copy(ah[:, g], tt[:, 2]))
            v.tensor_tensor(al[:, g], tt[:, 2], ah[:, g].bitcast(F32), ALU.subtract).then_inc(mix_ready, 1)
        dve.wait_ge(gate_made, 3)
        link(v.tensor_tensor(gl[:], gl[:], gl2[:], ALU.subtract))
        link(v.tensor_scalar(gl[:], gl[:], 1 / 16.0, None, ALU.mult))
        have, there = gl, gl2
        for k in range(6):
            d = 1 << k
            a, b = (z[:].rearrange("p c (n t) -> p (c n) t", t=64) for z in (have, there))
            v.tensor_copy(b[:, :, 0:d], a[:, :, 0:d])
            op = v.tensor_tensor(b[:, :, d:64], a[:, :, d:64], a[:, :, 0:64 - d], ALU.add)
            if k < 5:
                link(op)
            else:
                op.then_inc(gate_exp, 1)
            have, there = there, have
        dve.wait_ge(cum_exp, 1)
        v.tensor_tensor(qd[:], qd[:], mq[:], ALU.mult)
        v.tensor_tensor(kd[:], kd[:], mk[:], ALU.mult)
        v.tensor_tensor(ke[:], ke[:], mk[:], ALU.mult).then_inc(decays, 1)
        dve.wait_ge(ke_turned, 1)
        for c in range(2):
            op = v.tensor_copy(ken[:, :, c * P:(c + 1) * P], ps[:, 4 + c].rearrange("p (i d) -> p i d", i=SC))
        op.then_inc(ken_made, 1)
        dve.wait_ge(gla_scores, 1)
        link(v.tensor_scalar(sct[:].rearrange("p a n b t -> p a (n b t)"), ps[:, 0:2], 3e38, -3e38, ALU.min, ALU.max))
        for h in range(2):
            for b in range(2):
                v.tensor_tensor(sct[:, h, :, b], sct[:, h, :, b],
                                small("tri")[:, None, :].to_broadcast([P, 4, HD]), ALU.mult)
        link(v.memset(stt[:, 0], 0.0))
        dve.wait_ge(chunk_kv, 1)
        for n in range(7):
            for c in range(2):
                b, col = kv_place(n, c)
                op = v.scalar_tensor_tensor(out=stt[:, n + 1, c], in0=stt[:, n, c], scalar=dec[:, c, n:n + 1],
                                            in1=ps[:, b, col:col + P], op0=ALU.mult, op1=ALU.add)
            if n < 6:
                link(op)
            else:
                op.then_inc(states, 1)
        for h in range(4):
            dve.wait_ge(gla_out, h // 2 * 2 + 2)
            link(v.tensor_copy(go[:, h], ps[:, 4 + 2 * (h % 2) + h // 2]))
            for odd in range(2):
                o = go[:, h].rearrange("p (n a t) -> p a n t", a=2, t=64)[:, odd]
                inner = ps[:, 2 * odd + h // 2, h % 2 * 256:h % 2 * 256 + 256].rearrange("p (n t) -> p n t", t=64)
                op = v.tensor_tensor(o, inner, o, ALU.add)
            op.then_inc(gla_o, 1)
        for h in range(4):
            dve.wait_ge(gla_std, h + 1)
            link(v.reciprocal(rs[:, h % 2], rs[:, h % 2]))
            op = v.tensor_tensor(tt[:, 0], go[:, h], rs[:, h % 2], ALU.mult)
            op.then_inc(gla_used, 1)
            dve.wait_ge(gla_used, h + 1)
            if h == 0:
                dve.wait_ge(silu_made, 4)
            link(v.scalar_tensor_tensor(out=tt[:, 1], in0=tt[:, 0], scalar=small("gla_norm"), in1=mr[:, h],
                                        op0=ALU.mult, op1=ALU.mult))
            link(v.tensor_copy(ah[:, 4 + h], tt[:, 1]))
            v.tensor_tensor(al[:, 4 + h], tt[:, 1], ah[:, 4 + h].bitcast(F32), ALU.subtract).then_inc(mix_ready, 1)

        def add_out():
            for c in range(DC):
                v.tensor_tensor(x[:, c], bank(), x[:, c], ALU.add).then_inc(evac, 1)
        add_out()
        norm(x, ah, al)
        for c in range(DC):
            out_bank(xq[:, c])
        norm(me, mh, ml, MEM)
        for c in range(DC):
            out_bank(xk[:, c], cols=MEM)
        for c in range(DC):
            b = bank()
            v.tensor_copy(xv[:, :, c * P:(c + 1) * P], b[:, 0:MEM].rearrange("p (i f) -> p i f", i=MC)).then_inc(evac, 1)

        def xmax(w):
            dve.wait_ge(xs_made, w + 1)
            link(v.tensor_reduce(xs[:, w, 0:1], ps[:, w % 4, 0:MEM], X, ALU.max))
            v.tensor_scalar(xs[:, w, 1:2], xs[:, w, 0:1], -(256 ** -0.5), None, ALU.mult).then_inc(xn_made, 1)

        def xsplit(h):
            for e in range(2):
                dve.wait_ge(xo_made, 2 * h + e + 1)
                link(v.tensor_copy(ah[:, 2 * h + e], ps[:, 6 + e]))
                v.tensor_tensor(al[:, 2 * h + e], ps[:, 6 + e], ah[:, 2 * h + e].bitcast(F32),
                                ALU.subtract).then_inc(xo_split, 1)
        xmax(0)
        xmax(1)
        for w in range(16):
            if w + 2 < 16:
                xmax(w + 2)
            dve.wait_ge(xp_made, w + 1)
            link(v.reciprocal(xs[:, w, 3:4], xs[:, w, 2:3]))
            v.tensor_scalar(xp[:, w % 2], xp[:, w % 2], xs[:, w, 3:4], None, ALU.mult).then_inc(xp_normed, 1)
            if w % SC == 0 and w:
                xsplit(w // SC - 1)
        xsplit(3)
        add_out()
        norm(x, ah, al)

        def taps(o, bk, c):
            cw = small("conv_w").rearrange("p (k c) -> p k c", k=3)
            link(v.tensor_scalar(o, bk, cw[:, 2, c], small("conv_b")[:, c], ALU.mult, ALU.add))
            link(v.scalar_tensor_tensor(out=o[:, 1:S], in0=bk[:, 0:S - 1], scalar=cw[:, 1, c], in1=o[:, 1:S],
                                        op0=ALU.mult, op1=ALU.add))
            v.scalar_tensor_tensor(out=o[:, 2:S], in0=bk[:, 0:S - 2], scalar=cw[:, 0, c], in1=o[:, 2:S],
                                   op0=ALU.mult, op1=ALU.add).then_inc(evac, 1)

        c0 = 0
        for what, grp in FFN_BLOCKS:
            if what == "up":
                n = FF_GROUPS[grp]
                turns = n // 2
                with dve.Fori(0, turns) as it:
                    chain.enter(it, 12)
                    for j in range(RING):
                        dve.wait_ge(unit_used, it * RING + (units[0] + j + 1))
                        c = it * 2 + (c0 + j // 2)
                        o = uc[:, j // 2, j % 2]
                        taps(o, ps[:, (banks[0] + j) % RING], bass.ds(c + FF_CHUNKS * (j % 2), 1))
                        if j % 2:
                            dve.wait_ge(conv_silu, it * 2 + (c0 + j // 2 + 1))
                            dve.wait_ge(evac, it * RING + (banks[0] + j + 1))
                            k = it * 2 + j // 2
                            link(v.tensor_tensor(uc[:, j // 2, 1], uc[:, j // 2, 0], uc[:, j // 2, 1], ALU.mult))
                            hid_h = hh[:, grp % 2, bass.ds(k, 1)]
                            link(v.tensor_copy(hid_h, uc[:, j // 2, 1:2]))
                            v.tensor_tensor(hl[:, grp % 2, bass.ds(k, 1)], uc[:, j // 2, 1:2], hid_h.bitcast(F32),
                                            ALU.subtract).then_inc(hid_made, 1)
                    chain.leave(turns)
                banks[0] += 2 * n
                units[0] += 2 * n
                c0 += n
            else:
                def down(i, j, bk):
                    b4 = (banks[0] + j) % RING
                    xc = x[:, bass.ds(i, 1)]
                    v.tensor_tensor(xc, ps[:, b4:b4 + 1], xc, ALU.add).then_inc(evac, 1)
                banks_loop(8, down)
        rms(1)
        t0 = mark(v.tensor_tensor(tt[:, 0], x[:, 0], rs[:, 1], ALU.mult))
        for c in range(DC):
            if c + 1 < DC:
                if c >= 2:
                    dve.wait_ge(out_ready, c - 1)
                t1 = mark(v.tensor_tensor(tt[:, (c + 1) % 3], x[:, c + 1], rs[:, 1], ALU.mult))
            dve.wait_ge(v_step, t0)
            v.tensor_scalar(ah_f[:, c], tt[:, c % 3], small("norm_final")[:, c:c + 1], None, ALU.mult).then_inc(out_ready, 1)
            t0 = t1

    @block.scalar
    def _(act):
        a = nc.scalar
        chain = Count(a_step)
        squared = [0]
        stds = [0]
        normed = [0]
        one = small("ones")[:, 0:1]

        def link(ins):
            ins.then_inc(a_step, 1)
            act.wait_ge(a_step, chain.add())

        def highs(first, last):
            def high(u, slot):
                act.wait_ge(raw_in[slot], (u // RING + 1) * 16 if isinstance(u, int) else (u - slot) * 4 + 16)
                if not isinstance(u, int) or u >= RING:
                    act.wait_ge(unit_used, u - (RING - 1))
                a.copy(wh[:, slot], raw[:, slot]).then_inc(hi_done, 1)
            over_units(act, first, min(last, UNITS), high)

        def squares(chunk, wait, tokens=S, count=DC):
            for c in range(count):
                act.wait_ge(wait[0], wait[1](c) if callable(wait[1]) else wait[1] + c + 1)
                if squared[0] >= 2:
                    act.wait_ge(sq_used, squared[0] - 1)
                a.activation(sq[:, squared[0] % 2, 0:tokens], chunk[:, c], ACT.Square).then_inc(sq_made, 1)
                squared[0] += 1

        def highs_and_squares(u, out_t, bank0):
            for c in range(DC):
                highs(u + RING + c, u + RING + c + 1)
                squares(out_t[:, c:c + 1], (evac, lambda _: bank0 + c + 1), count=1)

        def root(slot, tokens=S):
            act.wait_ge(sq_used, squared[0])
            a.activation(rs[:, slot, 0:tokens], ps[:, 4 + stds[0] % 2, 0:tokens], ACT.Sqrt, bias=eps[:],
                         scale=1.0 / D).then_inc(std_made, 1)
            stds[0] += 1

        def gains(high, gain, shift=None, tokens=S):
            for c in range(DC):
                act.wait_ge(t_made, DC * normed[0] + c + 1)
                t = tt[:, c % 3, 0:tokens]
                link(a.activation(t, t, ACT.Identity, bias=0.0 if shift is None else shift(c), scale=gain(c)))
                a.copy(high[:, c], t).then_inc(high_made, 1)
            normed[0] += 1

        def coef_at(layer, which):
            return lambda c: coef[:, layer, which, c:c + 1]

        def small_at(name):
            return lambda c: small(name)[:, c:c + 1]

        act.wait_ge(setup_done, 1)
        act.wait_ge(small_in, 32)
        a.activation(cond[:], small("cT"), ACT.Silu).then_inc(cond_done, 1)
        act.wait_ge(ang_done, 2)
        for h in range(2):
            a.activation(ang[:, 4 + h], ang[:, 4 + h], ACT.Sin).then_inc(trig_made, 1)
        squares(x, (x_in, lambda c: 16))
        root(1)
        highs(0, RING)
        gains(ah, coef_at(0, 0), coef_at(0, 1))

        def store_rot(index, att, grp):
            r = index % 2
            act.wait_ge(rot_made, index + 1)
            for low_part, rot in enumerate((rot_h, rot_l)):
                for half in range(2):
                    src_ap = rot[:, r, half].bitcast(F32)
                    if grp is not None:
                        row = 64 * low_part + 32 * half
                        act.dma_start(qscr[4 * grp:4 * grp + 4, row:row + 32], src_ap).then_inc(rot_kept[r], 16)
                        continue
                    for twice in range(2):
                        row = 64 * twice + 32 * half
                        act.dma_start(kscr[att, :, low_part, row:row + 32], src_ap).then_inc(rot_kept[r], 16)

        def store_value(n, bank, places):
            act.wait_ge(evac, bank + 1)
            for e, (branch, group) in enumerate(places):
                half = e % 2 if len(places) == 2 else e // 2
                act.dma_start(vscr[branch, group], vtmp[:, n % 2].rearrange("p (i f) -> p i f", i=SC)[
                    :, :, HD * half:HD * half + HD]).then_inc(v_kept[n % 2], 16)

        u = FIRST["nsa_in"]
        highs(4, 6)
        act.wait_ge(kc_made, 1)
        for half in range(2):
            act.dma_start(cscr[0, :, 32 * half:32 * half + 32], rot_f[:, half]).then_inc(c_kept, 16)
        highs(6, 8)
        for n in range(2):
            act.wait_ge(evac, 2 + n + 1)
            act.dma_start(cscr[1, 2 * n:2 * n + 2], vtmp[:, n]).then_inc(c_kept, 16)
        for p in range(6):
            highs(8 + 2 * p, 10 + 2 * p)
            store_rot(p, p - 4, p if p < 4 else None)
        for n in range(4):
            highs(20 + n, 21 + n)
            store_value(n, 16 + n, [(n // 2, 2 * (n % 2)), (n // 2, 2 * (n % 2) + 1)])
        highs(24, 25)
        act.wait_ge(evac, 21)
        a.activation(gates[:], gates[:], ACT.Sigmoid).then_inc(gate_made, 1)
        for m in range(4):
            highs(25 + 2 * m, 27 + 2 * m)
            act.wait_ge(evac, 22 + m)
            a.activation(h1[:, m // 2, m % 2], h1[:, m // 2, m % 2], ACT.Gelu_apprx_tanh).then_inc(h1_made, 1)
        act.wait_ge(comp_ready, 1)
        for part, tile in enumerate((kc_h, kc_l)):
            for twice in range(2):
                act.dma_start(kcscr[:, part, 64 * twice:64 * twice + 64].rearrange("g d n -> d g n"),
                              tile[0:HD].bitcast(F32)).then_inc(comp_kept, 16)
        act.dma_start(vcscr.rearrange("g n d -> n g d"), vc_f[0:32]).then_inc(comp_kept, 16)

        def attention(att):
            works, base, n = att["works"], att["base"], len(att["works"])
            with act.Fori(0, GROUPS) as g:
                chain.enter(g, 0)
                w0 = g * n + base

                def exponential(w):
                    kind, j, i = works[w]
                    s = w % 4
                    act.wait_ge(nm_made, w0 + (w + 1))
                    if kind == "cmp":
                        o = pr[:, w % 2, 0:P]
                        a.activation(o, o, ACT.Exp, scale=SCALE).then_inc(p_made, 1)
                        return
                    if w >= 2:
                        act.wait_ge(p_turned, w0 + (w - 1))
                    c0, c1 = keys_of(att, i)
                    if att["sink"]:
                        a.activation(st[:, 4, s:s + 1], gs[:, 0, j:j + 1], ACT.Exp, bias=st[:, 2, s:s + 1])
                    a.activation(pr[:, w % 2, 0:(c1 - c0) * P], ps[:, s, 0:(c1 - c0) * P], ACT.Exp, bias=st[:, 2, s:s + 1],
                                 scale=SCALE, accum_out=st[:, 1, s:s + 1]).then_inc(p_made, 1)

                def copy(w):
                    kind, j, i = works[w]
                    act.wait_ge(p_turned, w0 + (w + 1))
                    if w >= 2:
                        act.wait_ge(pv_made, w0 + (w - 1))
                    c0, c1 = keys_of(att, i)
                    cols = P if kind == "cmp" else (c1 - c0) * P
                    a.copy(pt[:, w % 2, 0:cols], ps[:, 4 + w % 2, 0:cols]).then_inc(pt_made, 1)

                exponential(0)
                for w in range(n):
                    if w + 1 < n:
                        exponential(w + 1)
                    copy(w)
                chain.leave(GROUPS)

        def mlp(name, layer, b0):
            u = FIRST[name]
            if layer:
                highs(u + RING, u + UNITS_MLP - DC + RING)
                highs_and_squares(u + UNITS_MLP - DC, y, b0 + UNITS_MLP - DC)
                return
            def load(n, slot):
                act.wait_ge(ada_used, n - 1)
                act.dma_start(ada_ring[:, slot], src["ada"][bass.ds(n, 1)].rearrange("a p n -> p (a n)")).then_inc(ada_in[slot], 16)
            act.wait_ge(unit_used, u + 1)
            load(48, 0)
            for part in range(6):
                for it in range(2):
                    for j in range(RING):
                        i = part * 8 + it * RING + j
                        highs(u + RING + i, u + RING + i + 1)
                        if i + 1 < 48:
                            load(48 + i + 1, (i + 1) % 2)
            highs(u + RING + 48, u + UNITS_MLP - DC + RING)
            highs_and_squares(u + UNITS_MLP - DC, y, b0 + UNITS_MLP - DC)

        attention(NSA)
        u = FIRST["nsa_out"]
        n = 25
        highs_and_squares(u, y, n)
        n += 8
        root(0)
        squares(x, (x_new, 0))
        root(1)
        gains(ah, coef_at(0, 3), coef_at(0, 4))
        mlp("mlp0", 0, n)
        n += 64
        root(0)
        squares(x, (x_new, DC))
        root(1)
        gains(ah, coef_at(1, 0), coef_at(1, 1))
        u = FIRST["swa_in"]
        for p in range(5):
            highs(u + RING + 2 * p, u + RING + 2 * p + 2)
            store_rot(6 + p, 0, p if p < 4 else None)
        highs(u + RING + 10, u + RING + 11)
        store_value(0, n + 10, [(0, g) for g in range(GROUPS)])
        n += UNITS_SWA_IN
        attention(SWA)
        u = FIRST["swa_out"]
        highs_and_squares(u, y, n)
        n += 8
        root(0)
        squares(x, (x_new, 2 * DC))
        root(1)
        gains(ah, coef_at(1, 3), coef_at(1, 4))
        mlp("mlp1", 1, n)
        n += 64
        root(0)
        squares(x, (x_new, 3 * DC))
        root(1)
        gains(ah, small_at("norm_mix"))
        highs(FIRST["mix_in"] + RING, FIRST["mix_in"] + 13 + RING)
        act.wait_ge(evac, n + 9)
        a.activation(mr[:], mr[:], ACT.Silu).then_inc(silu_made, 4)
        highs(FIRST["mix_in"] + 13 + RING, FIRST["mix_out"] + RING)
        n += UNITS_MIX_IN + 4
        act.wait_ge(gate_exp, 2)
        link(a.activation(gl2[:], gl2[:], ACT.Exp))
        a.activation(gl2[:], gl2[:], ACT.Ln, bias=one).then_inc(gate_made, 2)
        act.wait_ge(gate_exp, 3)
        a.activation(qd[:], gl[:], ACT.Exp)
        a.activation(kd[:], gl[:], ACT.Exp, scale=-1.0)
        g5 = gl[:].rearrange("p c (n t) -> p c n t", t=64)
        a.activation(dec[:], g5[:, :, :, 63], ACT.Exp)
        for c in range(2):
            for m in range(8):
                op = a.activation(ke[:, c, 64 * m:64 * m + 64], gl[:, c, 64 * m:64 * m + 64], ACT.Exp,
                                  bias=gl[:, c, 64 * m + 63:64 * m + 64], scale=-1.0)
        op.then_inc(cum_exp, 1)

        def head_square(h):
            act.wait_ge(gla_o, h + 1)
            if h >= 2:
                act.wait_ge(gla_ss, h - 1)
            a.activation(sq[:, h % 2], go[:, h], ACT.Square).then_inc(gla_sq, 1)

        def head_root(h):
            act.wait_ge(gla_ss, h + 1)
            if h >= 2:
                act.wait_ge(gla_used, h - 1)
            a.activation(rs[:, h % 2], ps[:, 4 + h % 2], ACT.Sqrt, bias=eps[:], scale=1.0 / P).then_inc(gla_std, 1)
        head_square(0)
        for h in range(4):
            if h < 3:
                head_square(h + 1)
            head_root(h)
        highs_and_squares(FIRST["mix_out"], x, n)
        n += 8
        root(1)
        gains(ah, small_at("norm_xattn"))
        highs(FIRST["xq"] + RING, FIRST["kv"] + RING)
        squares(me, (x_in, lambda c: 32), tokens=MEM)
        root(1, MEM)
        gains(mh, small_at("norm_mem"), tokens=MEM)
        highs(FIRST["kv"] + RING, FIRST["xo"] + RING)
        n += UNITS_Q + UNITS_KV

        def xexp(w):
            act.wait_ge(xn_made, w + 1)
            if w >= 2:
                act.wait_ge(xp_turned, w - 1)
            a.activation(xp[:, w % 2], ps[:, w % 4, 0:MEM], ACT.Exp, bias=xs[:, w, 1:2], scale=256 ** -0.5,
                         accum_out=xs[:, w, 2:3]).then_inc(xp_made, 1)
        xexp(0)
        for w in range(16):
            if w + 1 < 16:
                xexp(w + 1)
            h, i = w // SC, w % SC
            act.wait_ge(xp_turned, w + 1)
            if i == 0 and h >= 2:
                act.wait_ge(xo_made, 2 * (h - 1))
            a.copy(xt[:, h % 2, :, i * P:(i + 1) * P],
                   ps[:, 4 + w % 2, 0:MEM].rearrange("p (m q) -> p m q", m=MC)).then_inc(xt_made, 1)
        highs_and_squares(FIRST["xo"], x, n)
        n += UNITS_OUT
        root(1)
        gains(ah, small_at("norm_ffn"))
        u = FIRST["ffn"]
        c0 = 0
        for what, grp in FFN_BLOCKS:
            if what == "down":
                if grp == 2:
                    highs_and_squares(u, x, n)
                else:
                    highs(u + RING, u + 8 + RING)
                u += 8
                n += 8
                continue
            size = FF_GROUPS[grp]
            for c in range(size):
                highs(u + RING + 2 * c, u + RING + 2 * c + 2)
                act.wait_ge(evac, n + 2 * c + 1)
                o = uc[:, c % 2, 0]
                a.activation(o, o, ACT.Silu).then_inc(conv_silu, 1)
            u += 2 * size
            n += 2 * size
        root(1)

    ctx.close()


def unit_tiles(w, order=None):
    rows, cols = w.shape
    w = np.pad(w, ((0, -rows % D), (0, -cols % P)))
    t = w.reshape(w.shape[0] // D, DC, P, w.shape[1] // P, P).transpose(3, 0, 2, 1, 4)
    return t.reshape(t.shape[0], t.shape[1], P, D)


def halves(w, heads):
    t = w.reshape(w.shape[0], heads // 4, 4, 2, 32).transpose(0, 1, 3, 2, 4)
    return t.reshape(w.shape[0], heads * HD)


def flat(t):
    return t.reshape(-1, P, D)


def mlp_units(up, down):
    a, b = unit_tiles(up), unit_tiles(down)
    parts = []
    for what, g in (("u", 0), ("u", 1), ("d", 0), ("u", 2), ("d", 1), ("u", 3), ("d", 2), ("d", 3)):
        parts.append(flat(a[8 * g:8 * g + 8] if what == "u" else b[:, g:g + 1]))
    return parts


def by_chunk(v):
    return np.ascontiguousarray(np.asarray(v).reshape(-1, P).T)


def lay_out(i):
    w = i["nsa_w_in"][0]
    q, kc, vc, ks, vs, kw, vw, g = np.split(w, [1024 + 256 * n for n in range(7)], axis=1)
    units = [flat(unit_tiles(np.concatenate([halves(kc, 4), vc, halves(q, HEADS), halves(ks, 4), halves(kw, 4),
                                             vs, vw, g], axis=1)))]
    for kind in range(2):
        units.append(flat(unit_tiles(i["nsa_phi_w1"][0, kind])))
    units.append(flat(unit_tiles(i["nsa_w_out"][0])))
    units += mlp_units(i["mlp_w_up"][0], i["mlp_w_down"][0])
    q, k, v = np.split(i["swa_w_in"][0], [1024, 1152], axis=1)
    k4 = np.repeat(k.reshape(D, 2, HD), 2, axis=1).reshape(D, 4 * HD)
    units.append(flat(unit_tiles(np.concatenate([halves(q, HEADS), halves(k4, 4), v], axis=1))))
    units.append(flat(unit_tiles(i["swa_w_out"][0])))
    units += mlp_units(i["mlp_w_up"][1], i["mlp_w_down"][1])
    p, q, k, v, g, r = np.split(i["w_in_2"][0], [512, 768, 1024, 1536, 1552], axis=1)
    g = np.pad(g, ((0, 0), (0, P - g.shape[1])))
    units.append(flat(unit_tiles(np.concatenate([g, q, k, r, p, v], axis=1))))
    units.append(flat(unit_tiles(i["w_out_2"][0])))
    units.append(flat(unit_tiles(i["xattn_wq_2"][0])))
    units.append(flat(unit_tiles(i["xattn_wkv_2"][0])))
    units.append(flat(unit_tiles(i["xattn_wo_2"][0])))
    up = unit_tiles(i["ffn_w_up_2"][0]).reshape(2, FF_CHUNKS, P, D).transpose(1, 0, 2, 3)
    down = i["ffn_w_down_2"][0]
    for what, n in (("u", 0), ("u", 1), ("d", 0), ("u", 2), ("d", 1), ("d", 2)):
        a, b = sum(FF_GROUPS[:n]), sum(FF_GROUPS[:n + 1])
        units.append(flat(up[a:b]) if what == "u" else flat(unit_tiles(down[a * P:b * P])))
    units = np.concatenate(units)
    assert units.shape[0] == UNITS, units.shape

    f = np.float32
    q_, k_ = np.arange(P)[:, None], np.arange(P)[None, :]
    t, n = np.arange(S)[:, None], np.arange(32)[None, :]
    cmp_add = np.where((n * 16 + 31 <= t) & (n < NCMP), 0.0, NEG)
    cmp_add = np.tile(cmp_add.reshape(SC, P, 1, 32), (1, 1, 4, 1)).transpose(1, 0, 2, 3).reshape(P, SC * P)
    inv = (f(1.0) / np.power(f(10000.0), np.arange(0, HD, 2, dtype=f) / f(HD))).astype(f)
    counts = np.concatenate([1.0 / np.minimum(np.arange(16) + 1, m) for m in (2, 4, 8, 16)])
    cw = i["ffn_conv_w_2"][0]
    parts = dict(
        ones=np.ones((P, P)), ident=np.eye(P), diag=np.where(k_ <= q_, 0.0, NEG), prev=np.where(k_ > q_, 0.0, NEG),
        cmp_add=cmp_add, inv=np.tile(inv, 4)[:, None], cT=by_chunk(i["c"][0]),
        ada_b=by_chunk(i["ada_b"]), norm_g=by_chunk(i["norm_g"]),
        pe=i["nsa_cmp_pe"][0].reshape(2, 16, 2, HD).transpose(2, 3, 0, 1).reshape(P, 32),
        b1=by_chunk(i["nsa_phi_b1"][0]), b2k=np.pad(i["nsa_phi_b2"][0, 0][:, None], ((0, HD), (0, 0))),
        b2v=np.broadcast_to(i["nsa_phi_b2"][0, 1], (P, HD)),
        w2=i["nsa_phi_w2"][0].reshape(2, 2, P, HD).transpose(2, 0, 1, 3).reshape(P, 4 * HD),
        sinks=np.broadcast_to(i["swa_sinks"][0], (P, HEADS)),
        norm_mix=by_chunk(i["norm_mix_w_2"]), norm_xattn=by_chunk(i["norm_xattn_w_2"]),
        norm_mem=by_chunk(i["norm_mem_w_2"]), norm_ffn=by_chunk(i["norm_ffn_w_2"]),
        norm_final=by_chunk(i["norm_final_w_2"]), pool_scale=by_chunk(i["pool_scale_2"]), gk_b=by_chunk(i["gk_b_2"]),
        gla_norm=by_chunk(i["gla_norm_w_2"]), conv_w=by_chunk(cw), conv_b=by_chunk(i["ffn_conv_b_2"]),
        pool_w=i["pool_w_2"][0].transpose(1, 0, 2).reshape(P, 4 * P),
        gk_w2=np.pad(i["gk_w2_2"][0], ((0, P - 16), (0, 0))),
        invcnt=np.broadcast_to(counts, (P, 64)), tri=np.where(np.arange(P)[:, None] % 64 <= np.arange(HD)[None, :], 1.0, 0.0))
    table = np.concatenate([np.asarray(parts[name], dtype=f) for name, _ in SMALL], axis=1)
    assert table.shape == (P, SMALL_COLS)
    ada = i["ada_w"].reshape(2, DC, P, 6, D).transpose(0, 3, 1, 2, 4).reshape(96, P, D)
    xt = i["x"][0].T.reshape(DC, P, S).transpose(1, 0, 2)
    mem = i["mem_2"][0].T.reshape(DC, P, MEM).transpose(1, 0, 2)
    return dict(units=units, small=table, ada=ada, xT=xt, memT=mem,
                pos=np.broadcast_to(i["positions"], (P, S)))


def kernel(**inputs):
    import concourse.bacc as bacc
    from concourse.bass_utils import run_bass_kernel_spmd

    laid = lay_out({k: np.asarray(v) for k, v in inputs.items()})
    nc = bacc.Bacc("TRN2", target_bir_lowering=False, num_devices=1)
    arrays, src = {}, {}
    for name, a in laid.items():
        a = np.ascontiguousarray(a)
        arrays[f"in_{name}"] = a
        src[name] = nc.dram_tensor(f"in_{name}", a.shape, mybir.dt.from_np(a.dtype), kind="ExternalInput").ap()
    out = nc.dram_tensor("out_0", (P, DC, S), F32, kind="ExternalOutput").ap()
    build(nc, src, out)
    r = run_bass_kernel_spmd(nc, [arrays], core_ids=[0])
    got = r.results[0]["out_0"]
    return got.transpose(1, 0, 2).reshape(D, S).T.reshape(1, S, D)
```

```python
from contextlib import ExitStack

import concourse.bass as bass
import numpy as np
from concourse import mybir

F32 = mybir.dt.float32
F32R = mybir.dt.float32r
I32 = mybir.dt.int32
ALU = mybir.AluOpType
ACT = mybir.ActivationFunctionType
X = mybir.AxisListType.X

P = 128
D = 1024
S = 512
DC = D // P
SC = S // P
HD = 64
HEADS = D // HD
GROUPS = 4
NCMP = (S - 32) // 16 + 1
MEM = 256
MC = MEM // P
KB = 1024
NEG = -1.0e30
RING = 4

UNITS_NSA_IN = 21
UNITS_PHI = 8
UNITS_OUT = 8
UNITS_MLP = 64
UNITS_SWA_IN = 11
UNITS_MIX_IN = 17
UNITS_KV = 16
UNITS_Q = 8
FF_CHUNKS = 22
FF_GROUPS = (8, 8, 6)
UNITS_FFN = 2 * FF_CHUNKS + 8 * len(FF_GROUPS)
STAGES = (("nsa_in", UNITS_NSA_IN), ("phi", UNITS_PHI), ("nsa_out", UNITS_OUT), ("mlp0", UNITS_MLP),
          ("swa_in", UNITS_SWA_IN), ("swa_out", UNITS_OUT), ("mlp1", UNITS_MLP),
          ("mix_in", UNITS_MIX_IN), ("mix_out", UNITS_OUT), ("xq", UNITS_Q), ("kv", UNITS_KV),
          ("xo", UNITS_OUT), ("ffn", UNITS_FFN))
FIRST = {}
_n = 0
for _name, _count in STAGES:
    FIRST[_name] = _n
    _n += _count
UNITS = _n

SMALL = (("ones", P), ("ident", P), ("diag", P), ("prev", P), ("cmp_add", SC * P),
         ("inv", 1), ("cT", DC), ("ada_b", 96), ("norm_g", 64), ("pe", 32), ("b1", 4), ("b2k", 1), ("b2v", HD),
         ("w2", 4 * HD), ("sinks", HEADS), ("norm_mix", DC), ("norm_xattn", DC), ("norm_mem", DC),
         ("norm_ffn", DC), ("norm_final", DC), ("pool_scale", 4), ("gk_b", 2), ("gla_norm", 1),
         ("conv_w", 3 * 44), ("conv_b", 44), ("pool_w", 4 * P), ("gk_w2", 256), ("invcnt", 4 * 16),
         ("tri", HD), ("quarter", 4))
COL = {}
_n = 0
for _name, _count in SMALL:
    COL[_name] = (_n, _n + _count)
    _n += _count
SMALL_COLS = _n


class Count:

    def __init__(self, sem, start=0):
        self.sem, self.base, self.turn, self.per, self.inner = sem, start, None, 0, 0

    def add(self, n=1):
        self.inner += n
        return self.now()

    def now(self, ahead=0):
        if self.turn is None:
            return self.base + self.inner + ahead
        return self.turn * self.per + (self.base + self.inner + ahead)

    def enter(self, turn, per):
        self.base += self.inner
        self.turn, self.per, self.inner = turn, per, 0

    def leave(self, turns):
        assert self.inner == self.per, f"{self.sem}: {self.inner} in a turn, not {self.per}"
        self.base += self.per * turns
        self.turn, self.inner = None, 0


def over_units(eng, a, b, one):
    while a < b and (a % RING or b - a < 2 * RING):
        one(a, a % RING)
        a += 1
    turns = max(0, (b - a) // RING)
    if turns > 0:
        with eng.Fori(0, turns) as it:
            for slot in range(RING):
                one(it * RING + (a + slot), slot)
    for u in range(a + turns * RING, b):
        one(u, u % RING)


def build(nc, src, out):
    ctx = ExitStack()
    sb0 = (nc.sbuf_base + 63) // 64 * 64

    def at(name, kib, shape, dt=F32):
        return nc.alloc_sbuf_tensor_at(name, shape, dt, offset=sb0 + int(kib * KB))

    def sem(name):
        return ctx.enter_context(nc.semaphore(name))

    def scratch(name, shape):
        return nc.dram_tensor(name, shape, F32, kind="Internal").ap()

    ps = ctx.enter_context(nc.psum_tensor("ps", [P, 8, S], F32))

    x = at("x", 0, [P, DC, S])
    ah = at("ah", 16, [P, DC, S], F32R)
    al = at("al", 32, [P, DC, S], F32R)
    y = at("y", 48, [P, DC, S])
    raw = at("raw", 64, [P, RING, DC, P])
    wh = at("wh", 80, [P, RING, DC, P], F32R)
    wl = at("wl", 96, [P, RING, DC, P], F32R)
    rs = at("rs", 112, [P, 2, S])
    tt = at("tt", 116, [P, 3, S])
    sq = at("sq", 122, [P, 2, S])
    sm = at("sm", 126, [P, SMALL_COLS])
    k1 = 126 + (SMALL_COLS * 4 + KB - 1) // KB
    mod = at("mod", k1, [P, 96])
    cond = at("cond", k1 + 0.375, [P, DC])
    coef = at("coef", k1 + 0.4375, [P, 2, 6, DC])
    eps = at("eps", k1 + 0.875, [P, 1])
    neg_sinks = at("neg_sinks", k1 + 0.9375, [P, HEADS])
    ident_r = at("ident_r", k1 + 1, [P, P], F32R)
    diag_r = at("diag_r", k1 + 1.5, [P, P], F32R)
    prev_r = at("prev_r", k1 + 2, [P, P], F32R)
    w0 = k1 + 2.5
    assert w0 + 68 <= 207.75, w0

    def small(name):
        a, b = COL[name]
        return sm[:, a:b]

    hh = at("hh", w0, [P, 2, DC, S], F32R)
    hl = at("hl", w0 + 32, [P, 2, DC, S], F32R)
    sqs = tt[:, 2]
    ada0 = at("ada0", w0, [P, RING, 1024])
    acc0 = at("acc0", w0 + 64, [P, 1024])

    pair = at("pair", w0, [P, 6, S])
    rot_h = at("rot_h", w0 + 12, [P, 2, 2, S], F32R)
    rot_l = at("rot_l", w0 + 20, [P, 2, 2, S], F32R)
    rot_f = at("rot_f", w0 + 28, [P, 2, S])
    vtmp = at("vtmp", w0 + 32, [P, 2, S])
    xb = at("xb", w0 + 36, [P, 16, 4 * NCMP])
    xb_h = at("xb_h", w0 + 44, [P, 16, 4 * NCMP], F32R)
    xb_l = at("xb_l", w0 + 52, [P, 16, 4 * NCMP], F32R)
    h1 = at("h1", w0 + 60, [P, 2, 2, 4 * NCMP])
    kc_f = at("kc_f", w0 + 62, [P, 4, 32])
    kc_h = at("kc_h", w0 + 62.5, [P, 4, 32], F32R)
    kc_l = at("kc_l", w0 + 63, [P, 4, 32], F32R)
    vc_f = at("vc_f", w0 + 63.5, [P, 4, HD])
    gates = at("gates", w0 + 64.5, [P, SC, P])
    x2 = at("x2", 48, [P, 2, 4, S])
    ang = at("ang", 48, [P, 6, S])
    pos_i = at("pos_i", 60, [P, S], I32)
    trig = at("trig", 112, [P, 2, S])
    qs = at("qs", w0, [P, 4, S], F32R)
    ks = at("ks", w0 + 8, [P, 2, 2, S], F32R)
    vs = at("vs", w0 + 16, [P, 2, SC, HD])
    pr = at("pr", w0 + 18, [P, 2, S])
    pt = at("pt", w0 + 22, [P, 2, S])
    og = at("og", w0 + 26, [P, SC, 4 * HD])
    kcs = at("kcs", w0 + 30, [P, 2, 32], F32R)
    vb = at("vb", w0 + 31, [P, 4 * HD])
    st = at("st", w0 + 32, [P, 8, 4])
    st4 = at("st4", w0 + 33, [P, 4, 16])
    gg = at("gg", w0 + 34, [P, SC, 12])
    gs = at("gs", w0 + 34.25, [P, 2, 4])
    acc = at("acc", w0 + 36, [P, 2, 1024])
    acc_t = at("acc_t", 116, [P, 1024])
    ada_ring = at("ada_ring", 48, [P, RING, 1024])

    qscr = scratch("qscr", [HEADS, P, S])
    kscr = scratch("kscr", [2, GROUPS, 2, P, S])
    vscr = scratch("vscr", [2, GROUPS, P, SC, HD])
    cscr = scratch("cscr", [2, GROUPS, HD, S])
    kcscr = scratch("kcscr", [GROUPS, 2, P, 32])
    vcscr = scratch("vcscr", [GROUPS, 32, HD])
    trscr = scratch("trscr", [P, 2, S])

    po = at("po", 48, [P, 4, S])
    go = at("go", 56, [P, 4, S])
    mq = at("mq", w0, [P, 2, S])
    mk = at("mk", w0 + 4, [P, 2, S])
    mv = at("mv", w0 + 8, [P, SC, S])
    mr = at("mr", w0 + 16, [P, 4, S])
    lo_g = at("lo_g", w0 + 24, [16, S])
    gl = at("gl", w0 + 26, [P, 2, S])
    gl2 = at("gl2", w0 + 30, [P, 2, S])
    qd = at("qd", w0 + 34, [P, 2, S])
    kd = at("kd", w0 + 38, [P, 2, S])
    ke = at("ke", w0 + 42, [P, 2, S])
    ken = at("ken", w0 + 46, [P, SC, 2 * P])
    stt = at("stt", w0 + 50, [P, 8, 2, P])
    sct = at("sct", w0 + 58, [P, 2, 4, 2, HD])
    dec = at("dec", w0 + 62, [P, 2, 8])
    pd = at("pd", w0 + 62.5, [P, S])

    me = at("me", w0, [P, DC, MEM])
    mh = at("mh", w0 + 8, [P, DC, MEM], F32R)
    ml = at("ml", w0 + 16, [P, DC, MEM], F32R)
    xk = at("xk", w0 + 24, [P, DC, MEM])
    xv = at("xv", w0 + 32, [P, MC, D])
    xq = at("xq", w0 + 40, [P, DC, S])
    xp = at("xp", w0 + 56, [P, 2, MEM])
    xt = at("xt", w0 + 58, [P, 2, MC, S])
    xs = at("xs", w0 + 66, [P, 16, 4])

    uc = at("uc", 48, [P, 2, 2, S])
    ah_f = at("ah_f", 16, [P, DC, S])

    raw_in = [sem(f"raw_in{i}") for i in range(RING)]
    hi_done = sem("hi_done")
    lo_done = sem("lo_done")
    unit_used = sem("unit_used")
    evac = sem("evac")
    v_step = sem("v_step")
    a_step = sem("a_step")
    small_in = sem("small_in")
    x_in = sem("x_in")
    ada_in = [sem(f"ada_in{i}") for i in range(RING)]
    cond_done = sem("cond_done")
    ada_first = sem("ada_first")
    ada_used = sem("ada_used")
    ada_scaled = sem("ada_scaled")
    ada_sum = sem("ada_sum")
    setup_done = sem("setup_done")
    ang_done = sem("ang_done")
    trig_made = sem("trig_made")
    trig_kept = sem("trig_kept")
    trig_in = sem("trig_in")
    x_new = sem("x_new")
    sq_made = sem("sq_made")
    sq_added = sem("sq_added")
    sq_used = sem("sq_used")
    std_made = sem("std_made")
    inv_made = sem("inv_made")
    spread = sem("spread")
    gla_inv = sem("gla_inv")
    gla_spread = sem("gla_spread")
    t_made = sem("t_made")
    high_made = sem("high_made")
    a_ready = sem("a_ready")
    rot_made = sem("rot_made")
    rot_kept = [sem(f"rot_kept{i}") for i in range(2)]
    kc_made = sem("kc_made")
    v_kept = [sem(f"v_kept{i}") for i in range(2)]
    c_kept = sem("c_kept")
    x2_in = [sem(f"x2_in{i}") for i in range(2)]
    xb_made = sem("xb_made")
    h1_made = sem("h1_made")
    comp_made = sem("comp_made")
    comp_ready = sem("comp_ready")
    comp_kept = sem("comp_kept")
    gate_made = sem("gate_made")
    q_in = [sem(f"q_in{i}") for i in range(4)]
    k_in = [sem(f"k_in{i}") for i in range(2)]
    vv_in = [sem(f"vv_in{i}") for i in range(2)]
    kcs_in = sem("kcs_in")
    vb_in = sem("vb_in")
    vb_clear = sem("vb_clear")
    sc_made = sem("sc_made")
    nm_made = sem("nm_made")
    p_made = sem("p_made")
    pc_made = sem("pc_made")
    p_turned = sem("p_turned")
    pt_made = sem("pt_made")
    pv_made = sem("pv_made")
    o_added = sem("o_added")
    o_turned = sem("o_turned")
    o_split = sem("o_split")
    hid_made = sem("hid_made")

    gate_sum = sem("gate_sum")
    gate_exp = sem("gate_exp")
    cum_exp = sem("cum_exp")
    silu_made = sem("silu_made")
    pooled = sem("pooled")
    pool_mixed = sem("pool_mixed")
    pool_read = sem("pool_read")
    pool_high = sem("pool_high")
    decays = sem("decays")
    ke_turned = sem("ke_turned")
    ken_made = sem("ken_made")
    gla_scores = sem("gla_scores")
    chunk_kv = sem("chunk_kv")
    states = sem("states")
    gla_out = sem("gla_out")
    gla_o = sem("gla_o")
    gla_sq = sem("gla_sq")
    gla_ss = sem("gla_ss")
    gla_std = sem("gla_std")
    gla_used = sem("gla_used")
    mix_ready = sem("mix_ready")
    xs_made = sem("xs_made")
    xn_made = sem("xn_made")
    xp_made = sem("xp_made")
    xp_normed = sem("xp_normed")
    xp_turned = sem("xp_turned")
    xt_made = sem("xt_made")
    xo_made = sem("xo_made")
    xo_split = sem("xo_split")
    conv_silu = sem("conv_silu")
    out_ready = sem("out_ready")
    out_kept = sem("out_kept")

    TAU = 2 * float(np.pi)
    TAU1 = 6.28125
    TAU2 = float(np.float32(np.round((TAU - TAU1) * 2 ** 21) / 2 ** 21))
    TAU3 = TAU - TAU1 - TAU2
    ROUND = 1.5 * 2 ** 23
    PI_IN = float(np.nextafter(np.float32(np.pi), np.float32(0)))
    V_STEPS = {"nsa": 92, "swa": 51}
    ROT_DMAS, ROT_DMAS_SWA, V_DMAS = (16, 16), (16, 8), (4, 4)

    def kv_place(n, pair):
        return (2, 3, 6, 7)[2 * (n % 2) + n // 4], n // 2 % 2 * 256 + pair * P

    A_READY = {k: DC * i for i, k in enumerate(("nsa_in", "mlp0", "swa_in", "mlp1", "mix_in", "xq", "mem", "ffn"))}
    BANKS_MIX_OUT = FIRST["xq"] - 4
    FFN_BLOCKS = (("up", 0), ("up", 1), ("down", 0), ("up", 2), ("down", 1), ("down", 2))

    SCALE = HD ** -0.5

    def works(branch):
        return [(branch, j, i) for j in range(4) for i in range(SC)]

    NSA = dict(works=works(0) + [("cmp", 0, 0)] + works(1), window=False, base=0, turns=0, sink=False)
    SWA = dict(works=works(0), window=True, base=GROUPS * len(NSA["works"]), turns=GROUPS, sink=True)

    CMP = 16
    ADA_WORKS = (20, 32)

    def keys_of(att, i):
        return (max(i - 1, 0) if att["window"] else 0), i + 1

    MLP_BLOCKS = (("up", 0), ("up", 1), ("down", 0), ("up", 2), ("down", 1), ("up", 3), ("down", 2), ("down", 3))

    block = ctx.enter_context(nc.Block())

    def coef_at(layer, which):
        return lambda c: coef[:, layer, which, c:c + 1]

    def small_at(name):
        return lambda c: small(name)[:, c:c + 1]

    def ada_acc(turn, part):
        return (acc0, acc_t)[part][:] if isinstance(turn, int) else acc[:, part]

    @block.sync
    def _(sp):
        sp.dma_start(sm[:], src["small"]).then_inc(small_in, 16)
        sp.dma_start(pos_i[:], src["pos"]).then_inc(small_in, 16)

        def units(a, b):
            def one(u, slot):
                if not isinstance(u, int) or u >= RING:
                    sp.wait_ge(lo_done, u - (RING - 1))
                sp.dma_start(raw[:, slot].rearrange("p k m -> p (k m)"),
                             src["units"][bass.ds(u, 1)].rearrange("a p n -> p (a n)")).then_inc(raw_in[slot], 16)
            over_units(sp, a, b, one)

        def group_loads(att, g, first):
            n = len(att["works"])

            def after(work):
                if not first:
                    sp.wait_ge(pv_made, g * n + (att["base"] + work - n))
                elif att["base"]:
                    sp.wait_ge(pv_made, att["base"])

            def compressed():
                after(CMP + 1)
                sp.dma_start(kcs[:].bitcast(F32),
                             kcscr[bass.ds(g, 1)].rearrange("a h p n -> p (a h) n")).then_inc(kcs_in, 16)
                for j in range(4):
                    sp.dma_start(vb[32 * j:32 * j + 32, HD * j:HD * j + HD],
                                 vcscr[bass.ds(g, 1)].rearrange("a n d -> n (a d)")).then_inc(vb_in, 16)
            for b in range(n // 16):
                after(n if b else CMP)
                sp.dma_start(ks[:, b].bitcast(F32),
                             kscr[b, bass.ds(g, 1)].rearrange("a h p t -> p (a h) t")).then_inc(k_in[b], 16)
                sp.dma_start(vs[:, b], vscr[b, bass.ds(g, 1)].rearrange("a p i d -> p (a i) d")).then_inc(vv_in[b], 16)
                if att is NSA and not first and not b:
                    compressed()
            for j in range(4):
                after(n)
                sp.dma_start(qs[:, j].bitcast(F32),
                             qscr[bass.ds(g * 4 + j, 1)].rearrange("a p t -> p (a t)")).then_inc(q_in[j], 16)
            if att is NSA and first:
                sp.wait_ge(comp_kept, 16 * 5)
                sp.wait_ge(vb_clear, 1)
                compressed()

        def ada_loads(turn, units_of, first=False):
            for n in units_of:
                if not (first and n < RING):
                    sp.wait_ge(ada_used, turn * 16 + (n - RING + 1))
                sp.dma_start(ada_ring[:, n % RING],
                             src["ada"][bass.ds(turn * 16 + (16 + n), 1)].rearrange("a p n -> p (a n)")).then_inc(
                                 ada_in[n % RING], 16)

        for n in range(16):
            if n >= RING:
                sp.wait_ge(ada_first, n - RING + 1)
            sp.dma_start(ada0[:, n % RING], src["ada"][n]).then_inc(ada_in[n % RING], 16)
            if n == RING - 1:
                sp.dma_start(x[:], src["xT"]).then_inc(x_in, 16)
        sp.wait_ge(trig_made, 2)
        sp.dma_start(trscr, ang[:, 4:6]).then_inc(trig_kept, 16)
        units(0, RING)
        sp.wait_ge(trig_kept, 16)
        sp.wait_ge(t_made, DC)
        sp.dma_start(trig[:], trscr).then_inc(trig_in, 16)
        units(RING, 8)
        sp.wait_ge(c_kept, 64)
        for kind in range(2):
            for half in range(2):
                sp.dma_start(x2[64 * half:64 * half + 64, kind, :, 0:S - half],
                             cscr[kind].rearrange("g d t -> d g t")[:, :, half:S]).then_inc(x2_in[kind], 16)
        units(8, FIRST["nsa_out"] + RING)
        for r in range(2):
            sp.wait_ge(rot_kept[r], 16 * ROT_DMAS[r])
            sp.wait_ge(v_kept[r], 16 * V_DMAS[r])
        group_loads(NSA, 0, True)
        ada_loads(0, range(16), first=True)
        with sp.Fori(1, GROUPS) as g:
            group_loads(NSA, g, False)
            ada_loads(g, range(16))
        units(FIRST["nsa_out"] + RING, FIRST["mlp0"] + RING)
        sp.wait_ge(x_new, DC)
        ada_loads(GROUPS, range(RING))
        for n in range(16):
            u = FIRST["mlp0"] + RING + n
            units(u, u + 1)
            if 1 <= n <= 16 - RING:
                ada_loads(GROUPS, (RING + n - 1,))
        units(FIRST["mlp0"] + RING + 16, FIRST["swa_in"] + RING)
        sp.wait_ge(t_made, 3 * DC)
        sp.dma_start(trig[:], trscr).then_inc(trig_in, 16)
        units(FIRST["swa_in"] + RING, FIRST["swa_out"] + RING)
        for r in range(2):
            sp.wait_ge(rot_kept[r], 16 * (ROT_DMAS[r] + ROT_DMAS_SWA[r]))
        sp.wait_ge(v_kept[0], 16 * (V_DMAS[0] + GROUPS))
        group_loads(SWA, 0, True)
        with sp.Fori(1, GROUPS) as g:
            group_loads(SWA, g, False)
        units(FIRST["swa_out"] + RING, FIRST["xq"] + RING)
        sp.wait_ge(evac, BANKS_MIX_OUT)
        sp.dma_start(me[:], src["memT"]).then_inc(x_in, 16)
        units(FIRST["xq"] + RING, UNITS)
        for c in range(0, DC, 2):
            sp.wait_ge(out_ready, c + 2)
            sp.dma_start(out[:, c:c + 2], ah_f[:, c:c + 2]).then_inc(out_kept, 16)
        sp.wait_ge(out_kept, 16 * DC // 2)

    @block.gpsimd
    def _(pool):
        def low(u, slot):
            pool.wait_ge(hi_done, u + 1)
            nc.gpsimd.tensor_tensor(wl[:, slot], raw[:, slot], wh[:, slot].bitcast(F32), ALU.subtract).then_inc(lo_done, 1)
        def ada_add(turn, n):
            if n % 8:
                pool.wait_ge(ada_scaled, turn * 16 + (n + 1))
                if n % 8 > 1:
                    pool.wait_ge(ada_used, turn * 16 + n)
                a = ada_acc(turn, n // 8)
                nc.gpsimd.tensor_tensor(a, ada_ring[:, n % RING], a, ALU.add).then_inc(ada_used, 1 if n % 8 > 1 else 2)

        over_units(pool, 0, FIRST["nsa_out"] + RING, low)
        with pool.Fori(0, GROUPS) as turn:
            for n in range(16):
                ada_add(turn, n)
        over_units(pool, FIRST["nsa_out"] + RING, FIRST["mlp0"] + RING, low)
        for n in range(16):
            u = FIRST["mlp0"] + RING + n
            low(u, u % RING)
            ada_add(GROUPS, n)
        over_units(pool, FIRST["mlp0"] + RING + 16, UNITS, low)

    @block.tensor
    def _(pe):
        done = [0]

        def bank_free(n):
            if not isinstance(n, int) or n >= RING:
                pe.wait_ge(evac, n - (RING - 1))

        def products(out_ap, slot, high, low, k0=0, ks=DC, first=True, last=True, ready=None):
            for k in range(ks):
                if ready is not None:
                    pe.wait_ge(ready[0], ready[1] + k + 1)
                nc.tensor.matmul(out_ap, wh[:, slot, k], high[:, k0 + k], start=first and k == 0, stop=False)
                nc.tensor.matmul(out_ap, wl[:, slot, k], high[:, k0 + k], start=False, stop=False)
                mm = nc.tensor.matmul(out_ap, wh[:, slot, k], low[:, k0 + k], start=False, stop=last and k == ks - 1)
            return mm

        def products_t(bank, slot, high, low, tokens, ready=None):
            if ready is not None:
                pe.wait_ge(ready[0], ready[1] + DC)
            for i in range(tokens // P):
                o = ps[:, bank, i * P:(i + 1) * P]
                t = slice(i * P, (i + 1) * P)
                for k in range(DC):
                    nc.tensor.matmul(o, high[:, k, t], wh[:, slot, k], start=k == 0, stop=False)
                    nc.tensor.matmul(o, high[:, k, t], wl[:, slot, k], start=False, stop=False)
                    mm = nc.tensor.matmul(o, low[:, k, t], wh[:, slot, k], start=False, stop=k == DC - 1)
            return mm

        def gemm(first, count, high, low, turned=False, tokens=S, ks=DC, ready=None):
            n0 = done[0] - first

            def one(u, slot):
                n = u + n0
                bank = (slot + n0) % RING
                bank_free(n)
                pe.wait_ge(lo_done, u + 1)
                if turned:
                    mm = products_t(bank, slot, high, low, tokens, ready)
                else:
                    mm = products(ps[:, bank, 0:tokens], slot, high, low, ks=ks, ready=ready)
                mm.then_inc(unit_used, 1)
            over_units(pe, first, first + count, one)
            done[0] += count

        def gemm_pairs(first, pairs, high, low, tokens=S):
            for u in range(first, first + 2 * pairs, 2):
                n, slot = done[0], u % RING
                pe.wait_ge(lo_done, u + 2)
                for i in range(tokens // P):
                    if i % 2 == 0:
                        bank_free(n + i // 2)
                    o = ps[:, (n + i // 2) % RING, i % 2 * 256:i % 2 * 256 + 256].rearrange("p (a f) -> p a f", a=2)
                    t = slice(i * P, (i + 1) * P)
                    for k in range(DC):
                        nc.tensor.matmul(o, high[:, k, t], wh[:, slot:slot + 2, k], start=k == 0, stop=False)
                        nc.tensor.matmul(o, high[:, k, t], wl[:, slot:slot + 2, k], start=False, stop=False)
                        mm = nc.tensor.matmul(o, low[:, k, t], wh[:, slot:slot + 2, k], start=False, stop=k == DC - 1)
                mm.then_inc(unit_used, 2)
                done[0] += tokens // P // 2

        squares = [0]
        gemms_squared = [0]

        def quarters(bank, squares_of, start, stop, tokens=S):
            for j in range(tokens // P):
                mm = nc.tensor.matmul(ps[32 * j:32 * j + 32, bank, 0:P], small("ones")[:, 0:32],
                                      squares_of[:, j * P:(j + 1) * P], start=start, stop=stop)
            return mm

        def spread_out(bank, inverses, tokens=S):
            rows = tokens // 4
            for j in range(tokens // P):
                mm = nc.tensor.matmul(ps[:, bank, j * P:(j + 1) * P],
                                      small("quarter")[0:rows, j:j + 1].to_broadcast([rows, P]), inverses[0:rows, 0:P],
                                      start=True, stop=True)
            return mm

        def root_spread(slot, tokens=S):
            pe.wait_ge(inv_made, squares[0])
            spread_out(4 + (squares[0] - 1) % 2, rs[:, slot], tokens).then_inc(spread, 1)

        def square_sum(c, tokens=S):
            q = squares[0]
            pe.wait_ge(sq_made, DC * q + c + 1)
            quarters(4 + q % 2, sq[:, c % 2], c == 0, c == DC - 1, tokens).then_inc(sq_used, 1)
            if c == DC - 1:
                squares[0] += 1

        def square_sums(tokens=S):
            for c in range(DC):
                square_sum(c, tokens)
            if squares[0] > 1:
                root_spread(1, tokens)

        def gemm_squared(first, high, low, slot, ready=None, ks=DC):
            for c in range(DC):
                gemm(first + c, 1, high, low, ready=ready, ks=ks)
            q = squares[0]
            pe.wait_ge(sq_added, 6 * (gemms_squared[0] + 1))
            quarters(4 + q % 2, sqs, True, False)
            pe.wait_ge(sq_made, DC * (q + 1))
            quarters(4 + q % 2, sq[:, 1], False, True).then_inc(sq_used, DC)
            gemms_squared[0] += 1
            squares[0] += 1
            root_spread(slot)

        def ada(sums, rows):
            for m in range(8):
                mm = nc.tensor.matmul(sums[:, m:m + 1], rows[:, m * P:(m + 1) * P],
                                      small("ones")[:, 0:1], start=True, stop=True)
            mm.then_inc(ada_sum, 1)

        def attention(att):
            works, base, n = att["works"], att["base"], len(att["works"])
            pe.wait_ge(evac, done[0])

            def group(g):
                w0 = g * n + base

                def score(w):
                    kind, j, i = works[w]
                    t = slice(i * P, (i + 1) * P)
                    bank = w % 4
                    if w >= 4:
                        pe.wait_ge(p_made, w0 + (w - 3))
                    if kind == "cmp":
                        pe.wait_ge(kcs_in, (g + 1) * 16)
                        for c in range(4 * SC):
                            for part in range(2):
                                mm = nc.tensor.matmul(ps[:, bank, 32 * c:32 * c + 32],
                                                      qs[:, c % 4, c // 4 * P:(c // 4 + 1) * P], kcs[:, part],
                                                      start=part == 0, stop=part == 1)
                    else:
                        if i == 0 and j == 0:
                            pe.wait_ge(k_in[kind], (g + (att["turns"] + 1)) * 16)
                        if i == 0 and w < 16:
                            pe.wait_ge(q_in[j], (g + (att["turns"] + 1)) * 16)
                        a, b = keys_of(att, i)
                        width = (b - a) * P
                        for part in range(2):
                            nc.tensor.matmul(ps[:, bank, 0:width], qs[:, j, t], ks[:, kind, part, a * P:b * P],
                                             start=part == 0, stop=False)
                        if att["window"] and i > 0:
                            nc.tensor.matmul(ps[:, bank, 0:P], ident_r[:], prev_r[:], start=False, stop=False)
                        mm = nc.tensor.matmul(ps[:, bank, width - P:width], ident_r[:], diag_r[:], start=False, stop=True)
                    mm.then_inc(sc_made, 1)

                def turn(w):
                    kind, j, i = works[w]
                    if w >= 2:
                        pe.wait_ge(pt_made, w0 + (w - 1))
                    if kind == "cmp":
                        pe.wait_ge(pc_made, g + 1)
                        blocks = SC
                    else:
                        pe.wait_ge(p_made, w0 + (w + 1))
                        a, b = keys_of(att, i)
                        blocks = b - a
                    for m in range(blocks):
                        mm = nc.tensor.transpose(ps[:, 4 + w % 2, m * P:(m + 1) * P], pr[:, w % 2, m * P:(m + 1) * P],
                                                 small("ident"))
                    mm.then_inc(p_turned, 1)

                def value(w):
                    kind, j, i = works[w]
                    pe.wait_ge(pt_made, w0 + (w + 1))
                    if w >= 2:
                        pe.wait_ge(o_added, w0 + (w if att is NSA and w in (CMP, CMP + 1) else w - 1))
                    if kind == "cmp":
                        pe.wait_ge(vb_in, (g + 1) * 64)
                        for c in range(SC):
                            mm = nc.tensor.matmul(ps[:, 6 + c // 2, c % 2 * 4 * HD:(c % 2 + 1) * 4 * HD],
                                                  pt[:, w % 2, c * P:(c + 1) * P], vb[:], start=True, stop=True)
                    else:
                        if i == 0 and j == 0:
                            pe.wait_ge(vv_in[kind], (g + (att["turns"] + 1)) * 16)
                        a, b = keys_of(att, i)
                        if att is NSA and w in ADA_WORKS:
                            part = ADA_WORKS.index(w)
                            pe.wait_ge(ada_used, g * 16 + 8 * (part + 1))
                            ada(ps[:, 6 + w % 2, 256:264], acc[:, part])
                        for m in range(b - a):
                            mm = nc.tensor.matmul(ps[:, 6 + w % 2, 0:HD], pt[:, w % 2, m * P:(m + 1) * P],
                                                  vs[:, kind, a + m], start=m == 0, stop=m == b - a - 1)
                    mm.then_inc(pv_made, 1)

                score(0)
                score(1)
                score(2)
                for w in range(n):
                    if w + 3 < n:
                        score(w + 3)
                    turn(w)
                    if w:
                        value(w - 1)
                value(n - 1)
                pe.wait_ge(o_added, w0 + n)
                for f in range(2):
                    for i in range(SC):
                        mm = nc.tensor.transpose(ps[:, f, i * P:(i + 1) * P], og[:, i, f * P:(f + 1) * P], small("ident"))
                    mm.then_inc(o_turned, 1)
                pe.wait_ge(o_split, 2 * g + 2 * (att["turns"] + 1))
            with pe.Fori(0, GROUPS) as g:
                group(g)

        def mlp(name, hid0):
            u = FIRST[name]
            for b, (what, grp) in enumerate(MLP_BLOCKS):
                if what == "up":
                    gemm(u, 8, ah, al, ready=(a_ready, A_READY[name]))
                else:
                    pe.wait_ge(hid_made, hid0 + 8 * (grp + 1))
                    if b == 7:
                        gemm_squared(u, hh[:, grp % 2], hl[:, grp % 2], 0)
                    else:
                        gemm(u, 8, hh[:, grp % 2], hl[:, grp % 2])
                if name == "mlp0" and b == 2:
                    pe.wait_ge(ada_used, 16 * (GROUPS + 1))
                    for part in range(2):
                        ada(ps[:, 6 + part, 0:8], ada_acc(GROUPS, part))
                u += 8

        pe.wait_ge(setup_done, 1)
        square_sums()
        for part in range(2):
            pe.wait_ge(ada_first, 8 * (part + 1))
            ada(ps[:, 6 + part, 0:8], acc0)
            if part == 0:
                root_spread(1)
        u = FIRST["nsa_in"]
        gemm(u, RING, ah, al, ready=(a_ready, 0))
        gemm(u + RING, 16 - RING, ah, al, ready=(a_ready, 0))
        gemm_pairs(u + 16, 2, ah, al)
        gemm(u + 20, 1, ah, al, turned=True)
        for m in range(4):
            n = done[0]
            bank_free(n)
            for half in range(2):
                v = FIRST["phi"] + 2 * m + half
                pe.wait_ge(lo_done, v + 1)
                if half == 0:
                    pe.wait_ge(xb_made, m // 2 + 1)
                products(ps[:, n % RING, 0:4 * NCMP], v % RING, xb_h, xb_l, k0=8 * half,
                         first=half == 0, last=half == 1).then_inc(unit_used, 1)
            done[0] += 1
        w2 = small("w2").rearrange("p (k c d) -> p k c d", k=2, c=2)
        pe.wait_ge(h1_made, 4)
        for c in range(2):
            mm = nc.tensor.matmul(ps[0:HD, 4, 0:4 * NCMP], w2[:, 0, c], h1[:, 0, c], start=c == 0, stop=c == 1)
        for g in range(GROUPS):
            for c in range(2):
                mm = nc.tensor.matmul(ps[0:NCMP, 5, g * HD:(g + 1) * HD], h1[:, 1, c, g * NCMP:(g + 1) * NCMP],
                                      w2[:, 1, c], start=c == 0, stop=c == 1)
        mm.then_inc(comp_made, 1)
        pe.wait_ge(comp_ready, 1)
        attention(NSA)
        gemm_squared(FIRST["nsa_out"], ah, al, 0)
        square_sums()
        mlp("mlp0", 0)
        square_sums()
        gemm(FIRST["swa_in"], 10, ah, al, ready=(a_ready, A_READY["swa_in"]))
        gemm(FIRST["swa_in"] + 10, 1, ah, al, turned=True)
        attention(SWA)
        gemm_squared(FIRST["swa_out"], ah, al, 0)
        square_sums()
        mlp("mlp1", 32)
        square_sums()
        u = FIRST["mix_in"]
        gemm(u, 7, ah, al, ready=(a_ready, A_READY["mix_in"]))
        pe.wait_ge(evac, done[0] - 6)
        for c in range(2):
            mm = nc.tensor.matmul(ps[:, 6 + c], small("gk_w2")[0:16, c * P:(c + 1) * P], lo_g[:], start=True, stop=True)
        mm.then_inc(gate_sum, 1)
        gemm(u + 7, 2, ah, al)

        def pool_mix(g):
            pe.wait_ge(pooled, g + 1)
            if g >= 2:
                pe.wait_ge(pool_read, g - 1)
            nc.tensor.matmul(ps[:, 4 + g % 2], small("pool_w")[:, g * P:(g + 1) * P], pd[:],
                             start=True, stop=True).then_inc(pool_mixed, 1)
        for g in range(3):
            gemm(u + 9 + g, 1, ah, al)
            pool_mix(g)
        gemm_pairs(u + 12, 1, ah, al)
        pool_mix(3)
        gemm_pairs(u + 14, 1, ah, al)
        gemm(u + 16, 1, ah, al)
        pe.wait_ge(evac, done[0])
        pe.wait_ge(decays, 1)
        for c in range(2):
            for i in range(SC):
                mm = nc.tensor.transpose(ps[:, 4 + c, i * P:(i + 1) * P], ke[:, c, i * P:(i + 1) * P], small("ident"))
        mm.then_inc(ke_turned, 1)
        for n in range(8):
            for h in range(4):
                r, a = slice(64 * (h % 2), 64 * (h % 2) + 64), 64 * (n % 2)
                col = (n // 2) * P + h // 2 * HD
                mm = nc.tensor.matmul(ps[a:a + 64, h % 2, col:col + 64], kd[r, h // 2, 64 * n:64 * n + 64],
                                      qd[r, h // 2, 64 * n:64 * n + 64], start=True, stop=True)
        mm.then_inc(gla_scores, 1)
        pe.wait_ge(ken_made, 1)
        for n in range(7):
            for h in range(4):
                t = slice(64 * (n % 2), 64 * (n % 2) + 64)
                d = 64 * (h % 2)
                b, col = kv_place(n, h // 2)
                mm = nc.tensor.matmul(ps[d:d + 64, b, col:col + P], ken[t, n // 2, h * HD:(h + 1) * HD],
                                      mv[t, n // 2, h * P:(h + 1) * P], start=True, stop=True)
        mm.then_inc(chunk_kv, 1)
        pe.wait_ge(states, 1)
        for h in range(4):
            r = slice(64 * (h % 2), 64 * (h % 2) + 64)
            for n in range(8):
                t, col = slice(64 * (n % 2), 64 * (n % 2) + 64), h % 2 * 256 + n // 2 * 64
                nc.tensor.matmul(ps[:, 2 * (n % 2) + h // 2, col:col + 64], mv[t, n // 2, h * P:(h + 1) * P],
                                 sct[t, h % 2, n // 2, h // 2], start=True, stop=True)
                mm = nc.tensor.matmul(ps[:, 4 + 2 * (h % 2) + h // 2, 64 * n:64 * n + 64], stt[r, n, h // 2],
                                      qd[r, h // 2, 64 * n:64 * n + 64], start=True, stop=True)
            mm.then_inc(gla_out, 1)
        pe.wait_ge(gla_o, 4)

        def head_spread(h):
            pe.wait_ge(gla_inv, h + 1)
            spread_out(6 + h % 2, rs[:, h % 2]).then_inc(gla_spread, 1)
        for h in range(4):
            pe.wait_ge(gla_sq, h + 1)
            if h >= 2:
                pe.wait_ge(gla_used, h - 1)
            quarters(4 + h % 2, sq[:, h % 2], True, True).then_inc(gla_ss, 1)
            if h:
                head_spread(h - 1)
        head_spread(3)
        gemm_squared(FIRST["mix_out"], ah, al, 1, ready=(mix_ready, 0))
        gemm(FIRST["xq"], 8, ah, al, ready=(a_ready, A_READY["xq"]))
        square_sums(MEM)
        gemm(FIRST["kv"], 7, mh, ml, tokens=MEM, ready=(a_ready, A_READY["mem"]))
        gemm_pairs(FIRST["kv"] + 7, 4, mh, ml, tokens=MEM)
        gemm(FIRST["kv"] + 15, 1, mh, ml, tokens=MEM)
        pe.wait_ge(evac, done[0])

        def xscore(w):
            h, i = w // SC, w % SC
            if w >= 4:
                pe.wait_ge(xp_made, w - 3)
            for c in range(2):
                mm = nc.tensor.matmul(ps[:, w % 4, 0:MEM], xq[:, 2 * h + c, i * P:(i + 1) * P], xk[:, 2 * h + c],
                                      start=c == 0, stop=c == 1)
            mm.then_inc(xs_made, 1)

        xscore(0)
        xscore(1)
        for w in range(16):
            h, i = w // SC, w % SC
            if w + 2 < 16:
                xscore(w + 2)
            pe.wait_ge(xp_normed, w + 1)
            if w >= 2:
                pe.wait_ge(xt_made, w - 1)
            for m in range(MC):
                mm = nc.tensor.transpose(ps[:, 4 + w % 2, m * P:(m + 1) * P], xp[:, w % 2, m * P:(m + 1) * P],
                                         small("ident"))
            mm.then_inc(xp_turned, 1)
            if i == SC - 1:
                pe.wait_ge(xt_made, w + 1)
                if h:
                    pe.wait_ge(xo_split, 2 * h)
                for e in range(2):
                    for m in range(MC):
                        mm = nc.tensor.matmul(ps[:, 6 + e], xv[:, m, (2 * h + e) * P:(2 * h + e + 1) * P],
                                              xt[:, h % 2, m], start=m == 0, stop=m == MC - 1)
                    mm.then_inc(xo_made, 1)
        gemm_squared(FIRST["xo"], ah, al, 1, ready=(xo_split, 0))
        u = FIRST["ffn"]
        made = 0
        for what, grp in FFN_BLOCKS:
            n = FF_GROUPS[grp]
            if what == "up":
                gemm(u, 2 * n, ah, al, ready=(a_ready, A_READY["ffn"]))
                u += 2 * n
            else:
                pe.wait_ge(hid_made, 64 + sum(FF_GROUPS[:grp + 1]))
                if grp == 2:
                    gemm_squared(u, hh[:, grp % 2], hl[:, grp % 2], 1, ks=n)
                else:
                    gemm(u, 8, hh[:, grp % 2], hl[:, grp % 2], ks=n)
                u += 8

    @block.vector
    def _(dve):
        v = nc.vector
        chain = Count(v_step)
        banks = [0]
        units = [0]
        normed = [0]
        stds = [0]
        added = [0]

        def mark(ins):
            ins.then_inc(v_step, 1)
            return chain.add()

        def link(ins):
            dve.wait_ge(v_step, mark(ins))

        def rms(slot, tokens=S):
            stds[0] += 1
            dve.wait_ge(std_made, stds[0])
            inv = rs[0:tokens // 4, slot, 0:P]
            v.reciprocal(inv, inv).then_inc(inv_made, 1)

        def spread_rs(tokens=S):
            dve.wait_ge(spread, stds[0])
            return ps[:, 4 + (stds[0] - 1) % 2, 0:tokens]

        def add_y(layer, which):
            rms(0)
            inv = spread_rs()
            t0 = mark(v.tensor_tensor(tt[:, 0], y[:, 0], inv, ALU.mult))
            x0 = DC * added[0]
            added[0] += 1
            for c in range(DC):
                if c + 1 < DC:
                    if c >= 2:
                        dve.wait_ge(x_new, x0 + c - 1)
                    t1 = mark(v.tensor_tensor(tt[:, (c + 1) % 3], y[:, c + 1], inv, ALU.mult))
                dve.wait_ge(v_step, t0)
                v.scalar_tensor_tensor(out=x[:, c], in0=tt[:, c % 3], scalar=coef[:, layer, which, c:c + 1], in1=x[:, c],
                                       op0=ALU.mult, op1=ALU.add).then_inc(x_new, 1)
                t0 = t1

        def norm(src_t, gain, shift, high, low, tokens=S, root=True):
            if root:
                rms(1, tokens)
            inv = spread_rs(tokens)
            n0 = DC * normed[0]

            def scaled(c):
                v.scalar_tensor_tensor(out=tt[:, c % 3, 0:tokens], in0=src_t[:, c], scalar=gain(c), in1=inv,
                                       op0=ALU.mult, op1=ALU.mult).then_inc(t_made, 1)
            scaled(0)
            scaled(1)
            for c in range(DC):
                if c + 2 < DC:
                    if c:
                        dve.wait_ge(a_ready, n0 + c)
                    scaled(c + 2)
                dve.wait_ge(high_made, n0 + c + 1)
                t, h = tt[:, c % 3, 0:tokens], high[:, c].bitcast(F32)
                if shift is None:
                    op = v.tensor_tensor(low[:, c], t, h, ALU.subtract)
                else:
                    op = v.scalar_tensor_tensor(out=low[:, c], in0=t, scalar=shift(c), in1=h, op0=ALU.add, op1=ALU.subtract)
                op.then_inc(a_ready, 1)
            normed[0] += 1

        def bank():
            b = banks[0] % RING
            banks[0] += 1
            units[0] += 1
            dve.wait_ge(unit_used, units[0])
            return ps[:, b]

        def pair_banks(tokens=S):
            units[0] += 2
            dve.wait_ge(unit_used, units[0])
            for _ in range(tokens // P // 2):
                banks[0] += 1
                yield ps[:, (banks[0] - 1) % RING]

        def banks_loop(count, one, steps=0):
            with dve.Fori(0, count // RING) as it:
                chain.enter(it, steps)
                for j in range(RING):
                    dve.wait_ge(unit_used, it * RING + (units[0] + j + 1))
                    one(it * RING + j, j, ps[:, (banks[0] + j) % RING])
                chain.leave(count // RING)
            banks[0] += count
            units[0] += count

        v.memset(eps[:], 1e-6)
        dve.wait_ge(small_in, 32)
        v.tensor_copy(ident_r[:], small("ident"))
        v.tensor_copy(diag_r[:], small("diag"))
        v.tensor_copy(prev_r[:], small("prev"))
        v.tensor_scalar(neg_sinks[:], small("sinks"), -1.0, None, ALU.mult).then_inc(setup_done, 1)
        link(v.tensor_copy(ang[:, 0], pos_i[:]))
        link(v.tensor_scalar(ang[:, 1], ang[:, 0], small("inv"), None, ALU.mult))
        for half in range(2):
            link(v.tensor_scalar(ang[:, 2], ang[:, 1], 1 / TAU, 0.25 * half, ALU.mult, ALU.add))
            link(v.tensor_scalar(ang[:, 2], ang[:, 2], ROUND, None, ALU.add))
            link(v.tensor_scalar(ang[:, 2], ang[:, 2], -ROUND, None, ALU.add))
            link(v.scalar_tensor_tensor(out=ang[:, 3], in0=ang[:, 2], scalar=-TAU1, in1=ang[:, 1], op0=ALU.mult, op1=ALU.add))
            link(v.scalar_tensor_tensor(out=ang[:, 3], in0=ang[:, 2], scalar=-TAU2, in1=ang[:, 3], op0=ALU.mult, op1=ALU.add))
            link(v.scalar_tensor_tensor(out=ang[:, 3], in0=ang[:, 2], scalar=-TAU3, in1=ang[:, 3], op0=ALU.mult, op1=ALU.add))
            link(v.tensor_scalar(ang[:, 3], ang[:, 3], half * TAU / 4, PI_IN, ALU.add, ALU.min))
            v.tensor_scalar(ang[:, 5 - half], ang[:, 3], -PI_IN, None, ALU.max).then_inc(ang_done, 1)

        def ada_read_out(part, sums):
            link(v.tensor_tensor(mod[:, part * 8:part * 8 + 8] if isinstance(part, int) else mod[:, bass.ds(part * 8, 8)],
                                 sums,
                                 small("ada_b")[:, bass.ds(part * 8, 8)], ALU.add))

        def ada_coef(layer, which):
            def m(p):
                return mod[:, 48 * layer + 8 * p:48 * layer + 8 * p + 8]

            def g(i):
                return small("norm_g")[:, 32 * layer + 8 * i:32 * layer + 8 * i + 8]
            gain, part = {0: (0, 1), 1: (None, 0), 2: (1, 2), 3: (2, 4), 4: (None, 3), 5: (3, 5)}[which]
            if gain is None:
                link(v.tensor_copy(coef[:, layer, which], m(part)))
            else:
                link(v.scalar_tensor_tensor(out=coef[:, layer, which], in0=m(part), scalar=1.0, in1=g(gain), op0=ALU.add,
                                            op1=ALU.mult))

        dve.wait_ge(cond_done, 1)
        for part in range(2):
            if part:
                rms(1)
            for k in range(8):
                n = 8 * part + k
                dve.wait_ge(ada_in[n % RING], 16 * (n // RING + 1))
                if k == 0:
                    op = v.tensor_scalar(acc0[:], ada0[:, n % RING], cond[:, 0:1], None, ALU.mult)
                else:
                    op = v.scalar_tensor_tensor(out=acc0[:], in0=ada0[:, n % RING], scalar=cond[:, k:k + 1], in1=acc0[:],
                                                op0=ALU.mult, op1=ALU.add)
                op.then_inc(ada_first, 1)
                dve.wait_ge(ada_first, n + 1)
            dve.wait_ge(ada_sum, part + 1)
            ada_read_out(part, ps[:, 6 + part, 0:8])
        for which in range(2):
            ada_coef(0, which)
        norm(x, coef_at(0, 0), coef_at(0, 1), ah, al, root=False)

        rot_uses = [0, 0]
        rots = [0]

        def rotary(dmas, whole=False):
            n = banks[0]
            a, b = ps[:, n % RING], ps[:, (n + 1) % RING]
            bank()
            bank()
            cos, sin = trig[:, 0], trig[:, 1]
            v.tensor_tensor(pair[:, 0], a, cos, ALU.mult)
            v.tensor_tensor(pair[:, 3], a, sin, ALU.mult).then_inc(evac, 1)
            v.tensor_tensor(pair[:, 1], b, sin, ALU.mult)
            v.tensor_tensor(pair[:, 2], b, cos, ALU.mult).then_inc(evac, 1)
            dve.wait_ge(evac, banks[0])
            if whole:
                v.tensor_tensor(rot_f[:, 0], pair[:, 0], pair[:, 1], ALU.subtract)
                v.tensor_tensor(rot_f[:, 1], pair[:, 2], pair[:, 3], ALU.add).then_inc(kc_made, 1)
                return
            v.tensor_tensor(pair[:, 4], pair[:, 0], pair[:, 1], ALU.subtract)
            link(v.tensor_tensor(pair[:, 5], pair[:, 2], pair[:, 3], ALU.add))
            r = rots[0] % 2
            if rot_uses[r]:
                dve.wait_ge(rot_kept[r], 16 * rot_uses[r])
            rot_uses[r] += dmas
            rots[0] += 1
            link(v.tensor_copy(rot_h[:, r], pair[:, 4:6]))
            v.tensor_tensor(rot_l[:, r], pair[:, 4:6], rot_h[:, r].bitcast(F32), ALU.subtract).then_inc(rot_made, 1)

        v_uses = [0, 0]

        def keep_value(n, dmas, b=None):
            if v_uses[n % 2]:
                dve.wait_ge(v_kept[n % 2], 16 * v_uses[n % 2])
            v_uses[n % 2] += dmas
            v.tensor_copy(vtmp[:, n % 2], bank() if b is None else b).then_inc(evac, 1)

        def token_blocks(kind):
            dve.wait_ge(x2_in[kind], 32)
            if kind:
                dve.wait_ge(unit_used, FIRST["phi"] + 4)
            for j in range(16):
                op = v.tensor_scalar(xb[:, j].rearrange("p (g n) -> p g n", g=4),
                                     x2[:, kind, :, 2 * j:2 * j + 16 * NCMP - 15:16],
                                     small("pe")[:, 16 * kind + j:16 * kind + j + 1], None, ALU.add)
            link(op)
            link(v.tensor_copy(xb_h[:], xb[:]))
            v.tensor_tensor(xb_l[:], xb[:], xb_h[:].bitcast(F32), ALU.subtract).then_inc(xb_made, 1)

        def attention(att):
            works, base, n = att["works"], att["base"], len(att["works"])
            with dve.Fori(0, GROUPS) as g:
                chain.enter(g, V_STEPS["nsa" if att is NSA else "swa"])
                w0 = g * n + base
                if att is NSA:
                    link(v.tensor_copy(gg[:], gates[:, :, bass.ds(g * 12, 12)]))
                else:
                    v.tensor_copy(gs[:, 0], small("sinks")[:, bass.ds(g * 4, 4)])
                    link(v.tensor_copy(gs[:, 1], neg_sinks[:, bass.ds(g * 4, 4)]))

                def maximum(w, meanwhile=None):
                    kind, j, i = works[w]
                    s = w % 4
                    dve.wait_ge(sc_made, w0 + (w + 1))
                    if kind == "cmp":
                        if meanwhile:
                            meanwhile()
                        dve.wait_ge(p_turned, w0 + (w - 1))
                        o = pr[:, w % 2].rearrange("p (c n) -> p c n", n=32)
                        link(v.tensor_tensor(pr[:, w % 2], ps[:, s], small("cmp_add"), ALU.add))
                        link(v.tensor_reduce(st4[:, 0], o, X, ALU.max))
                        link(v.tensor_scalar(st4[:, 0], st4[:, 0], NEG / 10, None, ALU.max))
                        v.tensor_tensor(o, o, st4[:, 0][:, :, None].to_broadcast([P, 16, 32]),
                                        ALU.subtract).then_inc(nm_made, 1)
                        return
                    a, b = keys_of(att, i)
                    reduced = mark(v.tensor_reduce(st[:, 0, s:s + 1], ps[:, s, 0:(b - a) * P], X, ALU.max))
                    if meanwhile:
                        meanwhile()
                    dve.wait_ge(v_step, reduced)
                    if att["sink"]:
                        op = v.tensor_scalar(st[:, 2, s:s + 1], st[:, 0, s:s + 1], -SCALE, gs[:, 1, j:j + 1], ALU.mult, ALU.min)
                    else:
                        op = v.tensor_scalar(st[:, 2, s:s + 1], st[:, 0, s:s + 1], -SCALE, None, ALU.mult)
                    op.then_inc(nm_made, 1)

                def compressed(w):
                    dve.wait_ge(p_made, w0 + (w + 1))
                    o = pr[:, w % 2].rearrange("p (c n) -> p c n", n=32)
                    link(v.tensor_reduce(st4[:, 1], o, X, ALU.add))
                    link(v.tensor_scalar(st4[:, 1], st4[:, 1], 1e-30, None, ALU.max))
                    link(v.reciprocal(st4[:, 2], st4[:, 1]))
                    link(v.tensor_tensor(st4[:, 3].rearrange("p (i h) -> p i h", i=SC),
                                         st4[:, 2].rearrange("p (i h) -> p i h", i=SC), gg[:, :, 0:12:3], ALU.mult))
                    v.tensor_tensor(o, o, st4[:, 3][:, :, None].to_broadcast([P, 16, 32]), ALU.mult).then_inc(pc_made, 1)

                factor = {}

                def inverse(w):
                    if works[w][0] == "cmp":
                        return
                    s = w % 4
                    dve.wait_ge(p_made, w0 + (w + 1))
                    if att["sink"]:
                        link(v.tensor_tensor(st[:, 1, s:s + 1], st[:, 1, s:s + 1], st[:, 4, s:s + 1], ALU.add))
                    factor[w] = mark(v.reciprocal(st[:, 3, s:s + 1], st[:, 1, s:s + 1]))

                def add(w):
                    kind, j, i = works[w]
                    s, o = w % 4, ps[:, 6 + w % 2]
                    if kind == "cmp":
                        dve.wait_ge(pv_made, w0 + (w + 1))
                        dve.wait_ge(o_added, w0 + w)
                        whole = og[:].rearrange("p (a b) f -> p a (b f)", a=2)
                        v.tensor_tensor(whole, ps[:, 6:8], whole, ALU.add).then_inc(o_added, 1)
                        return
                    og_j = og[:, i, j * HD:(j + 1) * HD]
                    gate = gg[:, i, 3 * j + 1 + kind:3 * j + 2 + kind]
                    dve.wait_ge(v_step, factor[w])
                    if att["sink"]:
                        dve.wait_ge(pv_made, w0 + (w + 1))
                        v.tensor_scalar(og_j, o[:, 0:HD], st[:, 3, s:s + 1], None, ALU.mult).then_inc(o_added, 1)
                        return
                    if w > CMP:
                        link(v.tensor_tensor(st[:, 5, s:s + 1], st[:, 3, s:s + 1], gate, ALU.mult))
                    dve.wait_ge(pv_made, w0 + (w + 1))
                    if att is NSA and w in ADA_WORKS:
                        part = ADA_WORKS.index(w)
                        ada_read_out(g * 2 + (part + 2), ps[:, 6 + w % 2, 256:264])
                    if w < CMP:
                        v.tensor_scalar(og_j, o[:, 0:HD], st[:, 3, s:s + 1], gate, ALU.mult, ALU.mult).then_inc(o_added, 1)
                        return
                    dve.wait_ge(o_added, w0 + max(w - 3, CMP + 1))
                    v.scalar_tensor_tensor(out=og_j, in0=o[:, 0:HD], scalar=st[:, 5, s:s + 1], in1=og_j,
                                           op0=ALU.mult, op1=ALU.add).then_inc(o_added, 1)

                maximum(0)
                maximum(1)
                maximum(2)
                for w in range(n):
                    if works[w][0] == "cmp":
                        compressed(w)
                    last = None if w == 0 else lambda: inverse(w - 1)
                    if w + 3 < n:
                        maximum(w + 3, last)
                    elif last:
                        last()
                    if w:
                        add(w - 1)
                inverse(n - 1)
                add(n - 1)
                for f in range(2):
                    dve.wait_ge(o_turned, 2 * g + (2 * att["turns"] + f + 1))
                    link(v.tensor_copy(ah[:, bass.ds(2 * g + f, 1)], ps[:, f:f + 1]))
                    v.tensor_tensor(al[:, bass.ds(2 * g + f, 1)], ps[:, f:f + 1], ah[:, bass.ds(2 * g + f, 1)].bitcast(F32),
                                    ALU.subtract).then_inc(o_split, 1)
                chain.leave(GROUPS)

        summed = [0]

        def squared_out(one):
            for c in range(DC):
                one(c).then_inc(evac, 1)
                if c < 2:
                    continue
                dve.wait_ge(sq_made, DC * stds[0] + c)
                if c == 2:
                    dve.wait_ge(sq_used, DC * stds[0])
                    op = v.tensor_tensor(sqs, sq[:, 0], sq[:, 1], ALU.add)
                else:
                    dve.wait_ge(sq_added, 6 * summed[0] + c - 2)
                    op = v.tensor_tensor(sqs, sq[:, (c - 1) % 2], sqs, ALU.add)
                op.then_inc(sq_added, 1)
            summed[0] += 1

        def copy_out():
            squared_out(lambda c: v.tensor_copy(y[:, c], bank()))

        def mlp(layer):
            for b, (what, grp) in enumerate(MLP_BLOCKS):
                def up(i, j, bk):
                    r, r2 = rs[:, 0], rs[:, 1]
                    v.tensor_scalar(r, bk, 0.0, None, ALU.max).then_inc(evac, 1)
                    dve.wait_ge(evac, i + (banks[0] + 1))
                    link(v.tensor_tensor(r2, r, r, ALU.mult))
                    link(v.tensor_copy(hh[:, grp % 2, bass.ds(i, 1)], rs[:, 1:2]))
                    v.tensor_tensor(hl[:, grp % 2, bass.ds(i, 1)], rs[:, 1:2], hh[:, grp % 2, bass.ds(i, 1)].bitcast(F32),
                                    ALU.subtract).then_inc(hid_made, 1)

                def down(i, j, bk):
                    b4 = (banks[0] + j) % RING
                    yc = y[:, bass.ds(i, 1)]
                    if grp == 0:
                        v.tensor_copy(yc, ps[:, b4:b4 + 1]).then_inc(evac, 1)
                    else:
                        v.tensor_tensor(yc, ps[:, b4:b4 + 1], yc, ALU.add).then_inc(evac, 1)
                if b == 7:
                    squared_out(lambda c: v.tensor_tensor(y[:, c], bank(), y[:, c], ALU.add))
                    continue
                if layer == 0 and b == 2:
                    dve.wait_ge(ada_used, 16 * (GROUPS + 1))
                banks_loop(8, up if what == "up" else down, steps=8 if what == "up" else 0)
                if layer == 0 and b == 3:
                    for part in range(2):
                        dve.wait_ge(ada_sum, 11 + part)
                        ada_read_out(10 + part, ps[:, 6 + part, 0:8])
                    for which in (3, 5):
                        ada_coef(1, which)

        dve.wait_ge(trig_in, 16)
        rotary(0, whole=True)
        for n in range(2):
            v.tensor_copy(vtmp[:, n], bank()).then_inc(evac, 1)
        dve.wait_ge(kc_made, 1)
        for _ in range(2):
            rotary(4)
        token_blocks(0)
        for _ in range(2):
            rotary(4)
        for _ in range(2):
            rotary(8)
        dve.wait_ge(c_kept, 64)
        for branch in range(2):
            for half, b in enumerate(pair_banks()):
                keep_value(2 * branch + half, 2, b)
        v.tensor_copy(gates[:].rearrange("p i f -> p (i f)"), bank()).then_inc(evac, 1)
        for m in range(4):
            n = banks[0]
            banks[0] += 1
            units[0] += 2
            dve.wait_ge(unit_used, units[0])
            v.tensor_scalar(h1[:, m // 2, m % 2], ps[:, n % RING, 0:4 * NCMP], small("b1")[:, m:m + 1], None,
                            ALU.add).then_inc(evac, 1)
            if m == 1:
                token_blocks(1)
        v.memset(kc_f[:], 0.0)
        link(v.memset(vc_f[:], 0.0))
        dve.wait_ge(comp_made, 1)
        v.tensor_scalar(kc_f[0:HD, :, 0:NCMP], ps[0:HD, 4, 0:4 * NCMP].rearrange("p (g n) -> p g n", g=4),
                        small("b2k")[0:HD], None, ALU.add)
        for g in range(GROUPS):
            op = v.tensor_tensor(vc_f[0:NCMP, g], ps[0:NCMP, 5, g * HD:(g + 1) * HD], small("b2v")[0:NCMP], ALU.add)
        link(op)
        link(v.tensor_copy(kc_h[:], kc_f[:]))
        v.tensor_tensor(kc_l[:], kc_f[:], kc_h[:].bitcast(F32), ALU.subtract).then_inc(comp_ready, 1)
        dve.wait_ge(gate_made, 1)
        for r in range(2):
            dve.wait_ge(rot_kept[r], 16 * ROT_DMAS[r])
            dve.wait_ge(v_kept[r], 16 * V_DMAS[r])
        v.memset(vb[:], 0.0).then_inc(vb_clear, 1)
        attention(NSA)
        for which in range(2, 6):
            ada_coef(0, which)
        for which in (0, 1, 2, 4):
            ada_coef(1, which)
        dve.wait_ge(ada_used, 16 * GROUPS)
        copy_out()
        add_y(0, 2)
        norm(x, coef_at(0, 3), coef_at(0, 4), ah, al)
        mlp(0)
        add_y(0, 5)
        norm(x, coef_at(1, 0), coef_at(1, 1), ah, al)
        dve.wait_ge(trig_in, 32)
        for _ in range(4):
            rotary(4)
        rotary(8)
        keep_value(0, 4)
        for r in range(2):
            dve.wait_ge(rot_kept[r], 16 * (ROT_DMAS[r] + ROT_DMAS_SWA[r]))
        dve.wait_ge(v_kept[0], 16 * (V_DMAS[0] + GROUPS))
        attention(SWA)
        copy_out()
        add_y(1, 2)
        norm(x, coef_at(1, 3), coef_at(1, 4), ah, al)
        mlp(1)
        add_y(1, 5)
        norm(x, small_at("norm_mix"), None, ah, al)

        def out_bank(o, rows=P, cols=S, scale=None):
            b = bank()[0:rows, 0:cols]
            (v.tensor_copy(o, b) if scale is None else v.tensor_scalar(o, b, scale, None, ALU.mult)).then_inc(evac, 1)

        out_bank(lo_g[:], rows=16)
        for c in range(4):
            out_bank(po[:, c])
        for c in range(2):
            out_bank(mq[:, c], scale=HD ** -0.5)
        dve.wait_ge(gate_sum, 1)
        for c in range(2):
            link(v.tensor_scalar(qd[:, c], ps[:, 6 + c], small("gk_b")[:, c:c + 1], None, ALU.add))
            v.scalar_tensor_tensor(out=gl2[:, c], in0=qd[:, c], scalar=-1.0, in1=qd[:, c], op0=ALU.mult,
                                   op1=ALU.min).then_inc(gate_exp, 1)
            v.tensor_scalar(gl[:, c], qd[:, c], 0.0, None, ALU.min)
        for c in range(2):
            out_bank(mk[:, c])

        def pool(g):
            have, here = po[:, g], 0
            for k in range(g + 1):
                d = 1 << k
                link(v.tensor_copy(tt[:, here, 0:d], have[:, 0:d]))
                link(v.tensor_tensor(tt[:, here, d:S], have[:, d:S], have[:, 0:S - d], ALU.add))
                have, here = tt[:, here], 1 - here
            link(v.tensor_tensor(tt[:, here, 0:16], have[:, 0:16], small("invcnt")[:, 16 * g:16 * g + 16], ALU.mult))
            v.tensor_tensor(pd[:, 0:16], tt[:, here, 0:16], po[:, g, 0:16], ALU.subtract)
            v.scalar_tensor_tensor(out=pd[:, 16:S], in0=have[:, 16:S], scalar=1.0 / (2 << g), in1=po[:, g, 16:S],
                                   op0=ALU.mult, op1=ALU.subtract).then_inc(pooled, 1)

        def pool_out(g):
            dve.wait_ge(pool_mixed, g + 1)
            v.tensor_scalar(po[:, g], ps[:, 4 + g % 2], small("pool_scale")[:, g:g + 1], None, ALU.mult).then_inc(pool_read, 1)

        pool(0)
        for g in range(3):
            out_bank(mr[:, g])
            pool_out(g)
            pool(g + 1)
        dve.wait_ge(gate_made, 3)
        link(v.tensor_tensor(gl[:], gl[:], gl2[:], ALU.subtract))
        link(v.tensor_scalar(gl[:], gl[:], 1 / 16.0, None, ALU.mult))

        def values(c):
            for half, b in enumerate(pair_banks()):
                v.tensor_copy(mv[:, 2 * half:2 * half + 2, c * 256:(c + 1) * 256],
                              b.rearrange("p (i f) -> p i f", i=2)).then_inc(evac, 1)
        have, there = gl, gl2
        for k in range(6):
            if k == 2:
                values(0)
            d = 1 << k
            a, b = (z[:].rearrange("p c (n t) -> p (c n) t", t=64) for z in (have, there))
            v.tensor_copy(b[:, :, 0:d], a[:, :, 0:d])
            op = v.tensor_tensor(b[:, :, d:64], a[:, :, d:64], a[:, :, 0:64 - d], ALU.add)
            if k < 5:
                link(op)
            else:
                op.then_inc(gate_exp, 1)
            have, there = there, have
        pool_out(3)
        values(1)
        out_bank(mr[:, 3])
        dve.wait_ge(cum_exp, 1)
        v.tensor_tensor(qd[:], qd[:], mq[:], ALU.mult)
        v.tensor_tensor(kd[:], kd[:], mk[:], ALU.mult)
        v.tensor_tensor(ke[:], ke[:], mk[:], ALU.mult).then_inc(decays, 1)
        dve.wait_ge(ke_turned, 1)
        for c in range(2):
            op = v.tensor_copy(ken[:, :, c * P:(c + 1) * P], ps[:, 4 + c].rearrange("p (i d) -> p i d", i=SC))
        op.then_inc(ken_made, 1)
        dve.wait_ge(pool_high, 1)
        v.tensor_tensor(al[:, 0:4], po[:], ah[:, 0:4].bitcast(F32), ALU.subtract).then_inc(mix_ready, 4)
        dve.wait_ge(gla_scores, 1)
        link(v.tensor_scalar(sct[:].rearrange("p a n b t -> p a (n b t)"), ps[:, 0:2], 3e38, -3e38, ALU.min, ALU.max))
        for h in range(2):
            for b in range(2):
                v.tensor_tensor(sct[:, h, :, b], sct[:, h, :, b],
                                small("tri")[:, None, :].to_broadcast([P, 4, HD]), ALU.mult)
        link(v.memset(stt[:, 0], 0.0))
        dve.wait_ge(chunk_kv, 1)
        for n in range(7):
            for c in range(2):
                b, col = kv_place(n, c)
                op = v.scalar_tensor_tensor(out=stt[:, n + 1, c], in0=stt[:, n, c], scalar=dec[:, c, n:n + 1],
                                            in1=ps[:, b, col:col + P], op0=ALU.mult, op1=ALU.add)
            if n < 6:
                link(op)
            else:
                op.then_inc(states, 1)
        for h in range(4):
            dve.wait_ge(gla_out, h // 2 * 2 + 2)
            link(v.tensor_copy(go[:, h], ps[:, 4 + 2 * (h % 2) + h // 2]))
            for odd in range(2):
                o = go[:, h].rearrange("p (n a t) -> p a n t", a=2, t=64)[:, odd]
                inner = ps[:, 2 * odd + h // 2, h % 2 * 256:h % 2 * 256 + 256].rearrange("p (n t) -> p n t", t=64)
                op = v.tensor_tensor(o, inner, o, ALU.add)
            op.then_inc(gla_o, 1)
        for h in range(4):
            dve.wait_ge(gla_std, h + 1)
            v.reciprocal(rs[:, h % 2, 0:P], rs[:, h % 2, 0:P]).then_inc(gla_inv, 1)
            dve.wait_ge(gla_spread, h + 1)
            op = v.tensor_tensor(tt[:, 0], go[:, h], ps[:, 6 + h % 2], ALU.mult)
            op.then_inc(gla_used, 1)
            dve.wait_ge(gla_used, h + 1)
            if h == 0:
                dve.wait_ge(silu_made, 4)
            link(v.scalar_tensor_tensor(out=tt[:, 1], in0=tt[:, 0], scalar=small("gla_norm"), in1=mr[:, h],
                                        op0=ALU.mult, op1=ALU.mult))
            link(v.tensor_copy(ah[:, 4 + h], tt[:, 1]))
            v.tensor_tensor(al[:, 4 + h], tt[:, 1], ah[:, 4 + h].bitcast(F32), ALU.subtract).then_inc(mix_ready, 1)

        def add_out():
            squared_out(lambda c: v.tensor_tensor(x[:, c], bank(), x[:, c], ALU.add))
        add_out()
        norm(x, small_at("norm_xattn"), None, ah, al)
        for c in range(DC):
            out_bank(xq[:, c])
        norm(me, small_at("norm_mem"), None, mh, ml, MEM)
        for c in range(DC - 1):
            out_bank(xk[:, c], cols=MEM)
        for c in range(4):
            for b in pair_banks(MEM):
                v.tensor_copy(xv[:, :, c * 256:(c + 1) * 256], b.rearrange("p (i f) -> p i f", i=MC)).then_inc(evac, 1)
        out_bank(xk[:, DC - 1], cols=MEM)

        def xmax(w):
            dve.wait_ge(xs_made, w + 1)
            link(v.tensor_reduce(xs[:, w, 0:1], ps[:, w % 4, 0:MEM], X, ALU.max))
            v.tensor_scalar(xs[:, w, 1:2], xs[:, w, 0:1], -(256 ** -0.5), None, ALU.mult).then_inc(xn_made, 1)

        def xsplit(h):
            for e in range(2):
                dve.wait_ge(xo_made, 2 * h + e + 1)
                link(v.tensor_copy(ah[:, 2 * h + e], ps[:, 6 + e]))
                v.tensor_tensor(al[:, 2 * h + e], ps[:, 6 + e], ah[:, 2 * h + e].bitcast(F32),
                                ALU.subtract).then_inc(xo_split, 1)
        xmax(0)
        xmax(1)
        for w in range(16):
            if w + 2 < 16:
                xmax(w + 2)
            dve.wait_ge(xp_made, w + 1)
            link(v.reciprocal(xs[:, w, 3:4], xs[:, w, 2:3]))
            v.tensor_scalar(xp[:, w % 2], xp[:, w % 2], xs[:, w, 3:4], None, ALU.mult).then_inc(xp_normed, 1)
            if w % SC == 0 and w:
                xsplit(w // SC - 1)
        xsplit(3)
        add_out()
        norm(x, small_at("norm_ffn"), None, ah, al)

        def taps(o, bk, c):
            cw = small("conv_w").rearrange("p (k c) -> p k c", k=3)
            link(v.tensor_scalar(o, bk, cw[:, 2, c], small("conv_b")[:, c], ALU.mult, ALU.add))
            link(v.scalar_tensor_tensor(out=o[:, 1:S], in0=bk[:, 0:S - 1], scalar=cw[:, 1, c], in1=o[:, 1:S],
                                        op0=ALU.mult, op1=ALU.add))
            v.scalar_tensor_tensor(out=o[:, 2:S], in0=bk[:, 0:S - 2], scalar=cw[:, 0, c], in1=o[:, 2:S],
                                   op0=ALU.mult, op1=ALU.add).then_inc(evac, 1)

        c0 = 0
        for what, grp in FFN_BLOCKS:
            if what == "up":
                n = FF_GROUPS[grp]
                turns = n // 2
                with dve.Fori(0, turns) as it:
                    chain.enter(it, 12)
                    for j in range(RING):
                        dve.wait_ge(unit_used, it * RING + (units[0] + j + 1))
                        c = it * 2 + (c0 + j // 2)
                        o = uc[:, j // 2, j % 2]
                        taps(o, ps[:, (banks[0] + j) % RING], bass.ds(c + FF_CHUNKS * (j % 2), 1))
                        if j % 2:
                            dve.wait_ge(conv_silu, it * 2 + (c0 + j // 2 + 1))
                            dve.wait_ge(evac, it * RING + (banks[0] + j + 1))
                            k = it * 2 + j // 2
                            link(v.tensor_tensor(uc[:, j // 2, 1], uc[:, j // 2, 0], uc[:, j // 2, 1], ALU.mult))
                            hid_h = hh[:, grp % 2, bass.ds(k, 1)]
                            link(v.tensor_copy(hid_h, uc[:, j // 2, 1:2]))
                            v.tensor_tensor(hl[:, grp % 2, bass.ds(k, 1)], uc[:, j // 2, 1:2], hid_h.bitcast(F32),
                                            ALU.subtract).then_inc(hid_made, 1)
                    chain.leave(turns)
                banks[0] += 2 * n
                units[0] += 2 * n
                c0 += n
            else:
                def down(i, j, bk):
                    b4 = (banks[0] + j) % RING
                    xc = x[:, bass.ds(i, 1)]
                    v.tensor_tensor(xc, ps[:, b4:b4 + 1], xc, ALU.add).then_inc(evac, 1)
                if grp == 2:
                    add_out()
                else:
                    banks_loop(8, down)
        rms(1)
        inv = spread_rs()
        for c in range(DC):
            v.scalar_tensor_tensor(out=ah_f[:, c], in0=x[:, c], scalar=small("norm_final")[:, c:c + 1], in1=inv,
                                   op0=ALU.mult, op1=ALU.mult).then_inc(out_ready, 1)

    @block.scalar
    def _(act):
        a = nc.scalar
        chain = Count(a_step)
        squared = [0]
        summed = [0]
        stds = [0]
        normed = [0]
        one = small("ones")[:, 0:1]

        def link(ins):
            ins.then_inc(a_step, 1)
            act.wait_ge(a_step, chain.add())

        def highs(first, last):
            def high(u, slot):
                act.wait_ge(raw_in[slot], (u // RING + 1) * 16 if isinstance(u, int) else (u - slot) * 4 + 16)
                if not isinstance(u, int) or u >= RING:
                    act.wait_ge(unit_used, u - (RING - 1))
                a.copy(wh[:, slot], raw[:, slot]).then_inc(hi_done, 1)
            over_units(act, first, min(last, UNITS), high)

        def squares(chunk, wait, tokens=S, count=DC, added=None):
            for c in range(count):
                act.wait_ge(wait[0], wait[1](c) if callable(wait[1]) else wait[1] + c + 1)
                if added:
                    act.wait_ge(sq_added, added)
                elif squared[0] >= 2:
                    act.wait_ge(sq_used, squared[0] - 1)
                a.activation(sq[:, squared[0] % 2, 0:tokens], chunk[:, c], ACT.Square).then_inc(sq_made, 1)
                squared[0] += 1

        def highs_and_squares(u, out_t, bank0):
            for c in range(DC):
                highs(u + RING + c, u + RING + c + 1)
                squares(out_t[:, c:c + 1], (evac, lambda _: bank0 + c + 1), count=1,
                        added=6 * summed[0] + max(c - 2, 1) if c >= 2 else None)
            summed[0] += 1

        def root(slot, tokens=S):
            act.wait_ge(sq_used, squared[0])
            rows = tokens // 4
            a.activation(rs[0:rows, slot, 0:P], ps[0:rows, 4 + stds[0] % 2, 0:P], ACT.Sqrt, bias=eps[0:rows],
                         scale=1.0 / D).then_inc(std_made, 1)
            stds[0] += 1

        def highs_of_norm(high, shift=None, tokens=S):
            for c in range(DC):
                act.wait_ge(t_made, DC * normed[0] + c + 1)
                t = tt[:, c % 3, 0:tokens]
                if shift is None:
                    op = a.copy(high[:, c], t)
                else:
                    op = a.activation(high[:, c], t, ACT.Identity, bias=shift(c))
                op.then_inc(high_made, 1)
            normed[0] += 1

        act.wait_ge(setup_done, 1)
        act.wait_ge(small_in, 32)
        a.activation(cond[:], small("cT"), ACT.Silu).then_inc(cond_done, 1)
        act.wait_ge(ang_done, 2)
        for h in range(2):
            a.activation(ang[:, 4 + h], ang[:, 4 + h], ACT.Sin).then_inc(trig_made, 1)
        squares(x, (x_in, lambda c: 16))
        root(1)
        highs(0, RING)
        highs_of_norm(ah, coef_at(0, 1))

        def store_rot(index, att, grp):
            r = index % 2
            act.wait_ge(rot_made, index + 1)
            for low_part, rot in enumerate((rot_h, rot_l)):
                for half in range(2):
                    src_ap = rot[:, r, half].bitcast(F32)
                    if grp is not None:
                        row = 64 * low_part + 32 * half
                        act.dma_start(qscr[4 * grp:4 * grp + 4, row:row + 32], src_ap).then_inc(rot_kept[r], 16)
                        continue
                    for twice in range(2):
                        row = 64 * twice + 32 * half
                        act.dma_start(kscr[att, :, low_part, row:row + 32], src_ap).then_inc(rot_kept[r], 16)

        def store_value(branch, half):
            act.wait_ge(evac, 16 + 2 * branch + half + 1)
            for e in range(2):
                act.dma_start(vscr[branch, :, :, 2 * half + e].rearrange("g p d -> p g d"),
                              vtmp[:, half, 256 * e:256 * e + 256].rearrange("p (g d) -> p g d", g=GROUPS)).then_inc(
                                  v_kept[half], 16)

        u = FIRST["nsa_in"]
        highs(4, 6)
        act.wait_ge(kc_made, 1)
        for half in range(2):
            act.dma_start(cscr[0, :, 32 * half:32 * half + 32], rot_f[:, half]).then_inc(c_kept, 16)
        highs(6, 8)
        for n in range(2):
            act.wait_ge(evac, 2 + n + 1)
            act.dma_start(cscr[1, 2 * n:2 * n + 2], vtmp[:, n]).then_inc(c_kept, 16)
        for p in range(6):
            highs(8 + 2 * p, 10 + 2 * p)
            store_rot(p, p - 4, p if p < 4 else None)
        for n in range(4):
            highs(20 + n, 21 + n)
            store_value(n // 2, n % 2)
        highs(24, 25)
        act.wait_ge(evac, 21)
        a.activation(gates[:], gates[:], ACT.Sigmoid).then_inc(gate_made, 1)
        for m in range(4):
            highs(25 + 2 * m, 27 + 2 * m)
            act.wait_ge(evac, 22 + m)
            a.activation(h1[:, m // 2, m % 2], h1[:, m // 2, m % 2], ACT.Gelu_apprx_tanh).then_inc(h1_made, 1)
        act.wait_ge(comp_ready, 1)
        for part, tile in enumerate((kc_h, kc_l)):
            for twice in range(2):
                act.dma_start(kcscr[:, part, 64 * twice:64 * twice + 64].rearrange("g d n -> d g n"),
                              tile[0:HD].bitcast(F32)).then_inc(comp_kept, 16)
        act.dma_start(vcscr.rearrange("g n d -> n g d"), vc_f[0:32]).then_inc(comp_kept, 16)

        def ada_scale(turn, n):
            act.wait_ge(ada_in[n % RING], turn * 64 + (64 + 16 * (n // RING + 1)))
            w = ada_ring[:, n % RING]
            if n % 8 == 0:
                act.wait_ge(ada_sum, turn * 2 + (n // 8 + 1))
            a.activation(w if n % 8 else ada_acc(turn, n // 8), w, ACT.Copy, scale=cond[:, n % 8:n % 8 + 1]).then_inc(ada_scaled, 1)

        def attention(att):
            works, base, n = att["works"], att["base"], len(att["works"])
            ada_after = [3 * k // 2 + 1 for k in range(16)]
            with act.Fori(0, GROUPS) as g:
                w0 = g * n + base

                def exponential(w):
                    kind, j, i = works[w]
                    s = w % 4
                    act.wait_ge(nm_made, w0 + (w + 1))
                    if kind == "cmp":
                        o = pr[:, w % 2]
                        a.activation(o, o, ACT.Exp, scale=SCALE).then_inc(p_made, 1)
                        return
                    if w >= 2:
                        act.wait_ge(p_turned, w0 + (w - 1))
                    c0, c1 = keys_of(att, i)
                    if att["sink"]:
                        a.activation(st[:, 4, s:s + 1], gs[:, 0, j:j + 1], ACT.Exp, bias=st[:, 2, s:s + 1])
                    a.activation(pr[:, w % 2, 0:(c1 - c0) * P], ps[:, s, 0:(c1 - c0) * P], ACT.Exp, bias=st[:, 2, s:s + 1],
                                 scale=SCALE, accum_out=st[:, 1, s:s + 1]).then_inc(p_made, 1)

                def copy(w):
                    kind, j, i = works[w]
                    act.wait_ge(p_turned, w0 + (w + 1))
                    if w >= 2:
                        act.wait_ge(pv_made, w0 + (w - 1))
                    c0, c1 = keys_of(att, i)
                    cols = S if kind == "cmp" else (c1 - c0) * P
                    a.copy(pt[:, w % 2, 0:cols], ps[:, 4 + w % 2, 0:cols]).then_inc(pt_made, 1)

                exponential(0)
                for w in range(n):
                    if w + 1 < n:
                        exponential(w + 1)
                    copy(w)
                    if att is NSA and w in ada_after:
                        ada_scale(g, ada_after.index(w))

        def mlp(name, b0):
            u = FIRST[name]
            if name == "mlp0":
                for k in range(16):
                    highs(u + RING + k, u + RING + k + 1)
                    ada_scale(GROUPS, k)
                highs(u + RING + 16, u + UNITS_MLP - DC + RING)
            else:
                highs(u + RING, u + UNITS_MLP - DC + RING)
            highs_and_squares(u + UNITS_MLP - DC, y, b0 + UNITS_MLP - DC)

        attention(NSA)
        u = FIRST["nsa_out"]
        n = 25
        highs_and_squares(u, y, n)
        n += 8
        root(0)
        squares(x, (x_new, 0))
        root(1)
        highs_of_norm(ah, coef_at(0, 4))
        mlp("mlp0", n)
        n += 64
        root(0)
        squares(x, (x_new, DC))
        root(1)
        highs_of_norm(ah, coef_at(1, 1))
        u = FIRST["swa_in"]
        for p in range(5):
            highs(u + RING + 2 * p, u + RING + 2 * p + 2)
            store_rot(6 + p, 0, p if p < 4 else None)
        highs(u + RING + 10, u + RING + 11)
        act.wait_ge(evac, n + 11)
        for g in range(GROUPS):
            act.dma_start(vscr[0, g], vtmp[:, 0].rearrange("p (i f) -> p i f", i=SC)[
                :, :, g // 2 * HD:(g // 2 + 1) * HD]).then_inc(v_kept[0], 16)
        n += UNITS_SWA_IN
        attention(SWA)
        u = FIRST["swa_out"]
        highs_and_squares(u, y, n)
        n += 8
        root(0)
        squares(x, (x_new, 2 * DC))
        root(1)
        highs_of_norm(ah, coef_at(1, 4))
        mlp("mlp1", n)
        n += 64
        root(0)
        squares(x, (x_new, 3 * DC))
        root(1)
        highs_of_norm(ah)
        highs(FIRST["mix_in"] + RING, FIRST["mix_in"] + 9 + RING)
        act.wait_ge(gate_exp, 2)
        link(a.activation(gl2[:], gl2[:], ACT.Exp))
        a.activation(gl2[:], gl2[:], ACT.Ln, bias=one).then_inc(gate_made, 2)
        highs(FIRST["mix_in"] + 9 + RING, FIRST["mix_out"] + RING)
        n += UNITS_MIX_IN
        act.wait_ge(gate_exp, 3)
        a.activation(qd[:], gl[:], ACT.Exp)
        a.activation(kd[:], gl[:], ACT.Exp, scale=-1.0)
        g5 = gl[:].rearrange("p c (n t) -> p c n t", t=64)
        a.activation(dec[:], g5[:, :, :, 63], ACT.Exp)
        for c in range(2):
            for m in range(8):
                op = a.activation(ke[:, c, 64 * m:64 * m + 64], gl[:, c, 64 * m:64 * m + 64], ACT.Exp,
                                  bias=gl[:, c, 64 * m + 63:64 * m + 64], scale=-1.0)
        op.then_inc(cum_exp, 1)
        act.wait_ge(evac, n)
        act.wait_ge(pool_read, 4)
        a.copy(ah[:, 0:4], po[:]).then_inc(pool_high, 1)
        a.activation(mr[:], mr[:], ACT.Silu).then_inc(silu_made, 4)

        def head_square(h):
            act.wait_ge(gla_o, h + 1)
            if h >= 2:
                act.wait_ge(gla_ss, h - 1)
            a.activation(sq[:, h % 2], go[:, h], ACT.Square).then_inc(gla_sq, 1)

        def head_root(h):
            act.wait_ge(gla_ss, h + 1)
            if h >= 2:
                act.wait_ge(gla_used, h - 1)
            a.activation(rs[:, h % 2, 0:P], ps[:, 4 + h % 2, 0:P], ACT.Sqrt, bias=eps[:], scale=1.0 / P).then_inc(gla_std, 1)
        head_square(0)
        for h in range(4):
            if h < 3:
                head_square(h + 1)
            head_root(h)
        highs_and_squares(FIRST["mix_out"], x, n)
        n += 8
        root(1)
        highs_of_norm(ah)
        highs(FIRST["xq"] + RING, FIRST["kv"] + RING)
        squares(me, (x_in, lambda c: 32), tokens=MEM)
        root(1, MEM)
        highs_of_norm(mh, tokens=MEM)
        highs(FIRST["kv"] + RING, FIRST["xo"] + RING)
        n += UNITS_Q + UNITS_KV - 4

        def xexp(w):
            act.wait_ge(xn_made, w + 1)
            if w >= 2:
                act.wait_ge(xp_turned, w - 1)
            a.activation(xp[:, w % 2], ps[:, w % 4, 0:MEM], ACT.Exp, bias=xs[:, w, 1:2], scale=256 ** -0.5,
                         accum_out=xs[:, w, 2:3]).then_inc(xp_made, 1)
        xexp(0)
        for w in range(16):
            if w + 1 < 16:
                xexp(w + 1)
            h, i = w // SC, w % SC
            act.wait_ge(xp_turned, w + 1)
            if i == 0 and h >= 2:
                act.wait_ge(xo_made, 2 * (h - 1))
            a.copy(xt[:, h % 2, :, i * P:(i + 1) * P],
                   ps[:, 4 + w % 2, 0:MEM].rearrange("p (m q) -> p m q", m=MC)).then_inc(xt_made, 1)
        highs_and_squares(FIRST["xo"], x, n)
        n += UNITS_OUT
        root(1)
        highs_of_norm(ah)
        u = FIRST["ffn"]
        c0 = 0
        for what, grp in FFN_BLOCKS:
            if what == "down":
                if grp == 2:
                    highs_and_squares(u, x, n)
                else:
                    highs(u + RING, u + 8 + RING)
                u += 8
                n += 8
                continue
            size = FF_GROUPS[grp]
            for c in range(size):
                highs(u + RING + 2 * c, u + RING + 2 * c + 2)
                act.wait_ge(evac, n + 2 * c + 1)
                o = uc[:, c % 2, 0]
                a.activation(o, o, ACT.Silu).then_inc(conv_silu, 1)
            u += 2 * size
            n += 2 * size
        root(1)

    ctx.close()


def unit_tiles(w, order=None):
    rows, cols = w.shape
    w = np.pad(w, ((0, -rows % D), (0, -cols % P)))
    t = w.reshape(w.shape[0] // D, DC, P, w.shape[1] // P, P).transpose(3, 0, 2, 1, 4)
    return t.reshape(t.shape[0], t.shape[1], P, D)


def halves(w, heads):
    t = w.reshape(w.shape[0], heads // 4, 4, 2, 32).transpose(0, 1, 3, 2, 4)
    return t.reshape(w.shape[0], heads * HD)


def flat(t):
    return t.reshape(-1, P, D)


def mlp_units(up, down):
    a, b = unit_tiles(up), unit_tiles(down)
    parts = []
    for what, g in (("u", 0), ("u", 1), ("d", 0), ("u", 2), ("d", 1), ("u", 3), ("d", 2), ("d", 3)):
        parts.append(flat(a[8 * g:8 * g + 8] if what == "u" else b[:, g:g + 1]))
    return parts


def by_chunk(v):
    return np.ascontiguousarray(np.asarray(v).reshape(-1, P).T)


def lay_out(i):
    w = i["nsa_w_in"][0]
    q, kc, vc, ks, vs, kw, vw, g = np.split(w, [1024 + 256 * n for n in range(7)], axis=1)
    units = [flat(unit_tiles(np.concatenate([halves(kc, 4), vc, halves(q, HEADS), halves(ks, 4), halves(kw, 4),
                                             vs, vw, g], axis=1)))]
    for kind in range(2):
        units.append(flat(unit_tiles(i["nsa_phi_w1"][0, kind])))
    units.append(flat(unit_tiles(i["nsa_w_out"][0])))
    units += mlp_units(i["mlp_w_up"][0], i["mlp_w_down"][0])
    q, k, v = np.split(i["swa_w_in"][0], [1024, 1152], axis=1)
    k4 = np.repeat(k.reshape(D, 2, HD), 2, axis=1).reshape(D, 4 * HD)
    units.append(flat(unit_tiles(np.concatenate([halves(q, HEADS), halves(k4, 4), v], axis=1))))
    units.append(flat(unit_tiles(i["swa_w_out"][0])))
    units += mlp_units(i["mlp_w_up"][1], i["mlp_w_down"][1])
    p, q, k, v, g, r = np.split(i["w_in_2"][0], [512, 768, 1024, 1536, 1552], axis=1)
    g = np.pad(g, ((0, 0), (0, P - g.shape[1])))
    units.append(flat(unit_tiles(np.concatenate([g, p, q, k, r[:, :384], v, r[:, 384:]], axis=1))))
    units.append(flat(unit_tiles(i["w_out_2"][0])))
    units.append(flat(unit_tiles(i["xattn_wq_2"][0])))
    kv = flat(unit_tiles(i["xattn_wkv_2"][0]))
    units.append(np.concatenate([kv[:7], kv[8:], kv[7:8]]))
    units.append(flat(unit_tiles(i["xattn_wo_2"][0])))
    up = unit_tiles(i["ffn_w_up_2"][0]).reshape(2, FF_CHUNKS, P, D).transpose(1, 0, 2, 3)
    down = i["ffn_w_down_2"][0]
    for what, n in (("u", 0), ("u", 1), ("d", 0), ("u", 2), ("d", 1), ("d", 2)):
        a, b = sum(FF_GROUPS[:n]), sum(FF_GROUPS[:n + 1])
        units.append(flat(up[a:b]) if what == "u" else flat(unit_tiles(down[a * P:b * P])))
    units = np.concatenate(units)
    assert units.shape[0] == UNITS, units.shape

    f = np.float32
    q_, k_ = np.arange(P)[:, None], np.arange(P)[None, :]
    t, n = np.arange(S)[:, None], np.arange(32)[None, :]
    cmp_add = np.where((n * 16 + 31 <= t) & (n < NCMP), 0.0, NEG)
    cmp_add = np.tile(cmp_add.reshape(SC, P, 1, 32), (1, 1, 4, 1)).transpose(1, 0, 2, 3).reshape(P, SC * P)
    inv = (f(1.0) / np.power(f(10000.0), np.arange(0, HD, 2, dtype=f) / f(HD))).astype(f)
    counts = np.concatenate([1.0 / np.minimum(np.arange(16) + 1, m) for m in (2, 4, 8, 16)])
    cw = i["ffn_conv_w_2"][0]
    parts = dict(
        ones=np.ones((P, P)), ident=np.eye(P), diag=np.where(k_ <= q_, 0.0, NEG), prev=np.where(k_ > q_, 0.0, NEG),
        cmp_add=cmp_add, inv=np.tile(inv, 4)[:, None], cT=by_chunk(i["c"][0]),
        ada_b=by_chunk(i["ada_b"]), norm_g=by_chunk(i["norm_g"]),
        pe=i["nsa_cmp_pe"][0].reshape(2, 16, 2, HD).transpose(2, 3, 0, 1).reshape(P, 32),
        b1=by_chunk(i["nsa_phi_b1"][0]), b2k=np.pad(i["nsa_phi_b2"][0, 0][:, None], ((0, HD), (0, 0))),
        b2v=np.broadcast_to(i["nsa_phi_b2"][0, 1], (P, HD)),
        w2=i["nsa_phi_w2"][0].reshape(2, 2, P, HD).transpose(2, 0, 1, 3).reshape(P, 4 * HD),
        sinks=np.broadcast_to(i["swa_sinks"][0], (P, HEADS)),
        norm_mix=by_chunk(i["norm_mix_w_2"]), norm_xattn=by_chunk(i["norm_xattn_w_2"]),
        norm_mem=by_chunk(i["norm_mem_w_2"]), norm_ffn=by_chunk(i["norm_ffn_w_2"]),
        norm_final=by_chunk(i["norm_final_w_2"]), pool_scale=by_chunk(i["pool_scale_2"]), gk_b=by_chunk(i["gk_b_2"]),
        gla_norm=by_chunk(i["gla_norm_w_2"]), conv_w=by_chunk(cw), conv_b=by_chunk(i["ffn_conv_b_2"]),
        pool_w=i["pool_w_2"][0].transpose(1, 0, 2).reshape(P, 4 * P),
        gk_w2=np.pad(i["gk_w2_2"][0], ((0, P - 16), (0, 0))),
        quarter=np.arange(P)[:, None] == 32 * np.arange(4)[None, :], invcnt=np.broadcast_to(counts, (P, 64)), tri=np.where(np.arange(P)[:, None] % 64 <= np.arange(HD)[None, :], 1.0, 0.0))
    table = np.concatenate([np.asarray(parts[name], dtype=f) for name, _ in SMALL], axis=1)
    assert table.shape == (P, SMALL_COLS)
    ada = i["ada_w"].reshape(2, DC, P, 6, D).transpose(0, 3, 1, 2, 4).reshape(96, P, D)
    xt = i["x"][0].T.reshape(DC, P, S).transpose(1, 0, 2)
    mem = i["mem_2"][0].T.reshape(DC, P, MEM).transpose(1, 0, 2)
    return dict(units=units, small=table, ada=ada, xT=xt, memT=mem,
                pos=np.broadcast_to(i["positions"], (P, S)))


def kernel(**inputs):
    import concourse.bacc as bacc
    from concourse.bass_utils import run_bass_kernel_spmd

    laid = lay_out({k: np.asarray(v) for k, v in inputs.items()})
    nc = bacc.Bacc("TRN2", target_bir_lowering=False, num_devices=1)
    arrays, src = {}, {}
    for name, a in laid.items():
        a = np.ascontiguousarray(a)
        arrays[f"in_{name}"] = a
        src[name] = nc.dram_tensor(f"in_{name}", a.shape, mybir.dt.from_np(a.dtype), kind="ExternalInput").ap()
    out = nc.dram_tensor("out_0", (P, DC, S), F32, kind="ExternalOutput").ap()
    build(nc, src, out)
    r = run_bass_kernel_spmd(nc, [arrays], core_ids=[0])
    got = r.results[0]["out_0"]
    return got.transpose(1, 0, 2).reshape(D, S).T.reshape(1, S, D)
```
